# Optimizing a Trainium2 kernel written in Bass

```python
import numpy as np
import jax
import jax.numpy as jnp
from jax import lax
import math
import jax, jax.numpy as jnp

D_MODEL = 1024
BATCH = 1
SEQ = 256
DEPTH = 2

HEAD_DIM = 64
MIX_WIDTH = D_MODEL
N_HEADS_DIL = (MIX_WIDTH // 2) // HEAD_DIM
DIL_CONFIGS = ((128, 1), (512, 4), (2048, 16))
N_HEADS_MLA = (MIX_WIDTH // 2) // HEAD_DIM
MLA_NOPE = HEAD_DIM
MLA_ROPE = HEAD_DIM // 2
MLA_V = HEAD_DIM
Q_LORA = D_MODEL // 4
KV_LORA = D_MODEL // 8
D_FF = 4 * D_MODEL
ROPE_THETA = 10000.0
EPS = 1e-6
Q_BLOCK = 128
NEG_INF = -1e30
IN_SPLITS = (N_HEADS_DIL * HEAD_DIM, N_HEADS_DIL * HEAD_DIM, N_HEADS_DIL * HEAD_DIM, Q_LORA, KV_LORA, MLA_ROPE)
W_IN_COLS = sum(IN_SPLITS)


def rms_norm(x, g):
    xf = x.astype(jnp.float32)
    y = xf * lax.rsqrt(jnp.mean(xf * xf, axis=-1, keepdims=True) + EPS)
    return (y * g.astype(jnp.float32)).astype(x.dtype)

def alibi_slopes(n):
    return jnp.asarray([2.0 ** (-8.0 * (h + 1) / n) for h in range(n)], dtype=jnp.float32)

def rope(x, pos):
    half = x.shape[-1] // 2
    inv = ROPE_THETA ** (-jnp.arange(half, dtype=jnp.float32) / half)
    ang = pos.astype(jnp.float32)[..., None] * inv
    ang = ang.reshape(ang.shape[:2] + (1,) * (x.ndim - 3) + (half,))
    cos, sin = jnp.cos(ang), jnp.sin(ang)
    xf = x.astype(jnp.float32)
    x1, x2 = xf[..., :half], xf[..., half:]
    return jnp.concatenate([x1 * cos - x2 * sin, x2 * cos + x1 * sin], axis=-1).astype(x.dtype)

def dilated_branch(q, k, v, pos, slopes, window, dil):
    B, S, H, Dh = q.shape
    half = window // (2 * dil)
    blk = half
    span = dil * blk
    Sp = -(-S // span) * span
    L = Sp // dil
    nb = L // blk
    pad = Sp - S

    def to_strided(a):
        a = jnp.pad(a, ((0, 0), (0, pad), (0, 0), (0, 0)))
        return a.reshape(B, L, dil, H, Dh).transpose(0, 2, 3, 1, 4)

    def band(a, axis, fill):
        pw = [(0, 0)] * a.ndim
        pw[axis] = (blk, blk)
        a = jnp.pad(a, pw, constant_values=fill)
        a = a.reshape(a.shape[:axis] + (nb + 2, blk) + a.shape[axis + 1:])
        parts = [lax.slice_in_dim(a, s, s + nb, axis=axis) for s in range(3)]
        return jnp.concatenate(parts, axis=axis + 1)

    qs, ks, vs = to_strided(q), to_strided(k), to_strided(v)
    pos_s = jnp.pad(pos, ((0, 0), (0, pad))).reshape(B, L, dil).transpose(0, 2, 1)
    val_s = (jnp.arange(Sp) < S).reshape(L, dil).T

    qb = qs.reshape(B, dil, H, nb, blk, Dh)
    kw = band(ks, 3, 0)
    vw = band(vs, 3, 0)
    pk = band(pos_s, 2, 0)
    vk = band(val_s, 1, False)
    pq = pos_s.reshape(B, dil, nb, blk)

    s = jnp.einsum('brhnid,brhnjd->brhnij', qb, kw, preferred_element_type=jnp.float32) * (Dh ** -0.5)
    dist = jnp.abs(pq[..., :, None] - pk[..., None, :]).astype(jnp.float32)
    s = s - slopes[None, None, :, None, None, None] * dist[:, :, None]
    rel = jnp.arange(3 * blk)[None, :] - blk - jnp.arange(blk)[:, None]
    mask = (jnp.abs(rel) <= half)[None] & vk[:, :, None, :]
    s = jnp.where(mask[None, :, None], s, NEG_INF)
    m = jnp.max(s, axis=-1, keepdims=True)
    p = jnp.exp(s - m)
    l = jnp.sum(p, axis=-1, keepdims=True)
    o = jnp.einsum('brhnij,brhnjd->brhnid', p, vw.astype(jnp.float32)) / l
    lse = (m + jnp.log(l))[..., 0]
    o = o.reshape(B, dil, H, L, Dh).transpose(0, 3, 1, 2, 4).reshape(B, Sp, H, Dh)[:, :S]
    lse = lse.reshape(B, dil, H, L).transpose(0, 3, 1, 2).reshape(B, Sp, H)[:, :S]
    return o, lse

def dilated_attention(q, k, v, pos, slopes):
    outs, lses = [], []
    for window, dil in DIL_CONFIGS:
        o, lse = dilated_branch(q, k, v, pos, slopes, window, dil)
        outs.append(o)
        lses.append(lse)
    wts = jax.nn.softmax(jnp.stack(lses), axis=0)
    return jnp.sum(jnp.stack(outs) * wts[..., None], axis=0)

def latent_attention(cq, ckv, k_rope, pos, g_cq, w_q_up, g_ckv, w_kv_up, g_qn, g_qr, g_kn, g_kr):
    B, S, _ = cq.shape
    H = N_HEADS_MLA
    q = (rms_norm(cq, g_cq) @ w_q_up).reshape(B, S, H, MLA_NOPE + MLA_ROPE)
    q_nope = rms_norm(q[..., :MLA_NOPE], g_qn)
    q_rot = rope(rms_norm(q[..., MLA_NOPE:], g_qr), pos)
    kv = (rms_norm(ckv, g_ckv) @ w_kv_up).reshape(B, S, H, MLA_NOPE + MLA_V)
    k_nope = rms_norm(kv[..., :MLA_NOPE], g_kn)
    v = kv[..., MLA_NOPE:]
    k_rot = rope(rms_norm(k_rope, g_kr), pos)
    scale = (MLA_NOPE + MLA_ROPE) ** -0.5
    nq = S // Q_BLOCK
    qn_b = q_nope.reshape(B, nq, Q_BLOCK, H, MLA_NOPE).transpose(1, 0, 2, 3, 4)
    qr_b = q_rot.reshape(B, nq, Q_BLOCK, H, MLA_ROPE).transpose(1, 0, 2, 3, 4)

    def block(args):
        qn, qr = args
        s = (jnp.einsum('bqhd,bkhd->bhqk', qn, k_nope, preferred_element_type=jnp.float32)
             + jnp.einsum('bqhr,bkr->bhqk', qr, k_rot, preferred_element_type=jnp.float32)) * scale
        p = jax.nn.softmax(s, axis=-1)
        return jnp.einsum('bhqk,bkhd->bqhd', p.astype(v.dtype), v)

    o = lax.map(block, (qn_b, qr_b))
    return o.transpose(1, 0, 2, 3, 4).reshape(B, S, H * MLA_V)

def first_inputs(seed: int = 0) -> dict:
    key = jax.random.key(seed)
    k = jax.random.split(key, 21)
    Ld = DEPTH
    f32 = jnp.float32

    def nrm(i, shape, fan_in, mult=1.0):
        return jax.random.normal(k[i], shape, f32) * (mult * fan_in ** -0.5)

    def gain(i, shape):
        return 1.0 + 0.02 * jax.random.normal(k[i], shape, f32)

    x = jax.random.normal(k[0], (BATCH, SEQ, D_MODEL), f32)
    c = jax.random.normal(k[1], (BATCH, D_MODEL), f32)
    offs = jax.random.randint(k[2], (BATCH, 1), 0, 1024, dtype=jnp.int32)
    positions = jnp.arange(SEQ, dtype=jnp.int32)[None, :] + offs
    return {
        'x': x,
        'c': c,
        'positions': positions,
        'w_mod': nrm(3, (Ld, D_MODEL, 6 * D_MODEL), D_MODEL, 0.5),
        'b_mod': 0.01 * jax.random.normal(k[4], (Ld, 6 * D_MODEL), f32),
        'g_norm_mix': gain(5, (Ld, D_MODEL)),
        'w_in': nrm(6, (Ld, D_MODEL, W_IN_COLS), D_MODEL),
        'g_q_dil': gain(7, (Ld, HEAD_DIM)),
        'g_k_dil': gain(8, (Ld, HEAD_DIM)),
        'g_cq': gain(9, (Ld, Q_LORA)),
        'w_q_up': nrm(10, (Ld, Q_LORA, N_HEADS_MLA * (MLA_NOPE + MLA_ROPE)), Q_LORA),
        'g_ckv': gain(11, (Ld, KV_LORA)),
        'w_kv_up': nrm(12, (Ld, KV_LORA, N_HEADS_MLA * (MLA_NOPE + MLA_V)), KV_LORA),
        'g_q_nope': gain(13, (Ld, MLA_NOPE)),
        'g_q_rope': gain(14, (Ld, MLA_ROPE)),
        'g_k_nope': gain(15, (Ld, MLA_NOPE)),
        'g_k_rope': gain(16, (Ld, MLA_ROPE)),
        'w_out': nrm(17, (Ld, MIX_WIDTH, D_MODEL), MIX_WIDTH),
        'g_norm_mlp': gain(18, (Ld, D_MODEL)),
        'w_mlp_in': nrm(19, (Ld, D_MODEL, D_FF), D_MODEL),
        'w_mlp_out': nrm(20, (Ld, D_FF, D_MODEL), D_FF),
    }

def first_block(x, c, positions, w_mod, b_mod, g_norm_mix, w_in, g_q_dil, g_k_dil, g_cq, w_q_up,
              g_ckv, w_kv_up, g_q_nope, g_q_rope, g_k_nope, g_k_rope, w_out, g_norm_mlp,
              w_mlp_in, w_mlp_out):
    B, S, _ = x.shape
    slopes = alibi_slopes(N_HEADS_DIL)
    cuts = [int(v) for v in np.cumsum(IN_SPLITS)[:-1]]
    c_act = jax.nn.silu(c)
    for l in range(DEPTH):
        mod = c_act @ w_mod[l] + b_mod[l]
        sh1, sc1, gt1, sh2, sc2, gt2 = jnp.split(mod, 6, axis=-1)

        h = rms_norm(x, g_norm_mix[l]) * (1.0 + sc1[:, None]) + sh1[:, None]
        proj = h @ w_in[l]
        q_d, k_d, v_d, cq, ckv, k_rope = jnp.split(proj, cuts, axis=-1)
        q_d = rms_norm(q_d.reshape(B, S, N_HEADS_DIL, HEAD_DIM), g_q_dil[l])
        k_d = rms_norm(k_d.reshape(B, S, N_HEADS_DIL, HEAD_DIM), g_k_dil[l])
        v_d = v_d.reshape(B, S, N_HEADS_DIL, HEAD_DIM)
        o_dil = dilated_attention(q_d, k_d, v_d, positions, slopes).reshape(B, S, -1).astype(x.dtype)
        o_mla = latent_attention(cq, ckv, k_rope, positions, g_cq[l], w_q_up[l], g_ckv[l], w_kv_up[l],
                                 g_q_nope[l], g_q_rope[l], g_k_nope[l], g_k_rope[l]).astype(x.dtype)
        mix = jnp.concatenate([o_dil, o_mla], axis=-1) @ w_out[l]
        x = x + gt1[:, None] * mix

        h = rms_norm(x, g_norm_mlp[l]) * (1.0 + sc2[:, None]) + sh2[:, None]
        y = jnp.square(jax.nn.relu(h @ w_mlp_in[l])) @ w_mlp_out[l]
        x = x + gt2[:, None] * y
    return x


N_HEADS_SB = 8
N_HEADS_FOX = 8
W_SB = N_HEADS_SB * HEAD_DIM
W_FOX = N_HEADS_FOX * HEAD_DIM
D_FF_2 = 2816
N_EXPERTS = 8
TOP_K = 2
D_FF_EXPERT = 1408
N_DENSE = (DEPTH + 1) // 2
N_MOE = DEPTH // 2
RMS_EPS = 1e-6
PROJ_IN = 3 * W_SB + 3 * W_FOX + N_HEADS_FOX + 2 * D_MODEL


def rmsnorm(x, g):
    x32 = x.astype(jnp.float32)
    y = x32 * lax.rsqrt(jnp.mean(x32 * x32, axis=-1, keepdims=True) + RMS_EPS)
    return (y * g.astype(jnp.float32)).astype(x.dtype)

def split_heads(t, n_heads):
    b, s, _ = t.shape
    return t.reshape(b, s, n_heads, HEAD_DIM).transpose(0, 2, 1, 3)

def merge_heads(t):
    b, h, s, d = t.shape
    return t.transpose(0, 2, 1, 3).reshape(b, s, h * d)

def stick_breaking_attention(q, k, v):
    seq = q.shape[2]
    scale = 1.0 / math.sqrt(HEAD_DIM)
    outs = []
    for i in range(seq // Q_BLOCK):
        t0 = i * Q_BLOCK
        kv_len = t0 + Q_BLOCK
        qb = q[:, :, t0:kv_len]
        kb = k[:, :, :kv_len]
        vb = v[:, :, :kv_len]
        z = jnp.einsum('bhqd,bhkd->bhqk', qb, kb).astype(jnp.float32) * scale
        q_pos = t0 + jnp.arange(Q_BLOCK)[:, None]
        k_pos = jnp.arange(kv_len)[None, :]
        mask = k_pos < q_pos
        log_beta = jax.nn.log_sigmoid(z)
        log_keep = jnp.where(mask, jax.nn.log_sigmoid(-z), 0.0)
        tail = lax.cumsum(log_keep, axis=log_keep.ndim - 1, reverse=True) - log_keep
        w = jnp.where(mask, jnp.exp(log_beta + tail), 0.0)
        outs.append(jnp.einsum('bhqk,bhkd->bhqd', w.astype(vb.dtype), vb))
    return jnp.concatenate(outs, axis=2)

def forgetting_attention(q, k, v, log_f):
    seq = q.shape[2]
    scale = 1.0 / math.sqrt(HEAD_DIM)
    cum_f = lax.cumsum(log_f, axis=log_f.ndim - 1)
    outs = []
    for i in range(seq // Q_BLOCK):
        t0 = i * Q_BLOCK
        kv_len = t0 + Q_BLOCK
        qb = q[:, :, t0:kv_len]
        kb = k[:, :, :kv_len]
        vb = v[:, :, :kv_len]
        z = jnp.einsum('bhqd,bhkd->bhqk', qb, kb).astype(jnp.float32) * scale
        decay = cum_f[:, :, t0:kv_len, None] - cum_f[:, :, None, :kv_len]
        q_pos = t0 + jnp.arange(Q_BLOCK)[:, None]
        k_pos = jnp.arange(kv_len)[None, :]
        logits = jnp.where(k_pos <= q_pos, z + decay, -jnp.inf)
        p = jax.nn.softmax(logits, axis=-1)
        outs.append(jnp.einsum('bhqk,bhkd->bhqd', p.astype(vb.dtype), vb))
    return jnp.concatenate(outs, axis=2)

def swiglu(h, w_gu, w_dn):
    gu = h @ w_gu
    g, u = jnp.split(gu, 2, axis=-1)
    return (jax.nn.silu(g) * u) @ w_dn

def moe_swiglu(h, w_router, w_gu_e, w_dn_e):
    logits = (h @ w_router).astype(jnp.float32)
    top_val, top_idx = lax.top_k(logits, TOP_K)
    top_w = jax.nn.softmax(top_val, axis=-1)
    combine = jnp.sum(jax.nn.one_hot(top_idx, N_EXPERTS, dtype=jnp.float32) * top_w[..., None], axis=-2)
    combine = combine.astype(h.dtype)
    out = jnp.zeros_like(h)
    for e in range(N_EXPERTS):
        out = out + combine[..., e:e + 1] * swiglu(h, w_gu_e[e], w_dn_e[e])
    return out

def second_inputs(seed: int = 0) -> dict:
    key = jax.random.key(seed)
    ks = jax.random.split(key, 16)
    nrm = lambda k, shape, fan_in: jax.random.normal(k, shape, jnp.float32) * fan_in ** -0.5
    return {
        "x": jax.random.normal(ks[0], (BATCH, SEQ, D_MODEL), jnp.float32),
        "g_mix": 1.0 + 0.02 * jax.random.normal(ks[1], (DEPTH, D_MODEL), jnp.float32),
        "w_in": nrm(ks[2], (DEPTH, D_MODEL, PROJ_IN), D_MODEL),
        "b_f": 2.0 + 0.1 * jax.random.normal(ks[3], (DEPTH, N_HEADS_FOX), jnp.float32),
        "b_gate": 0.02 * jax.random.normal(ks[4], (DEPTH, 2 * D_MODEL), jnp.float32),
        "g_q": 1.0 + 0.02 * jax.random.normal(ks[5], (DEPTH, HEAD_DIM), jnp.float32),
        "g_k": 1.0 + 0.02 * jax.random.normal(ks[6], (DEPTH, HEAD_DIM), jnp.float32),
        "w_o_sb": nrm(ks[7], (DEPTH, W_SB, D_MODEL), W_SB),
        "w_o_fox": nrm(ks[8], (DEPTH, W_FOX, D_MODEL), W_FOX),
        "w_out": nrm(ks[9], (DEPTH, D_MODEL, D_MODEL), D_MODEL),
        "g_ffn": 1.0 + 0.02 * jax.random.normal(ks[10], (DEPTH, D_MODEL), jnp.float32),
        "w_gu_dense": nrm(ks[11], (N_DENSE, D_MODEL, 2 * D_FF_2), D_MODEL),
        "w_dn_dense": nrm(ks[12], (N_DENSE, D_FF_2, D_MODEL), D_FF_2),
        "w_router": nrm(ks[13], (N_MOE, D_MODEL, N_EXPERTS), D_MODEL),
        "w_gu_exp": nrm(ks[14], (N_MOE, N_EXPERTS, D_MODEL, 2 * D_FF_EXPERT), D_MODEL),
        "w_dn_exp": nrm(ks[15], (N_MOE, N_EXPERTS, D_FF_EXPERT, D_MODEL), D_FF_EXPERT),
    }

def second_block(x, g_mix, w_in, b_f, b_gate, g_q, g_k, w_o_sb, w_o_fox, w_out,
              g_ffn, w_gu_dense, w_dn_dense, w_router, w_gu_exp, w_dn_exp):
    splits = [int(c) for c in np.cumsum([W_SB, W_SB, W_SB, W_FOX, W_FOX, W_FOX, N_HEADS_FOX])]
    for l in range(DEPTH):
        h = rmsnorm(x, g_mix[l])
        p = h @ w_in[l]
        q_sb, k_sb, v_sb, q_fx, k_fx, v_fx, f_pre, gate_pre = jnp.split(p, splits, axis=-1)

        y_sb = stick_breaking_attention(split_heads(q_sb, N_HEADS_SB),
                                        split_heads(k_sb, N_HEADS_SB),
                                        split_heads(v_sb, N_HEADS_SB))
        y_sb = merge_heads(y_sb) @ w_o_sb[l]

        qf = rmsnorm(split_heads(q_fx, N_HEADS_FOX), g_q[l])
        kf = rmsnorm(split_heads(k_fx, N_HEADS_FOX), g_k[l])
        log_f = jax.nn.log_sigmoid(f_pre.astype(jnp.float32) + b_f[l].astype(jnp.float32))
        y_fx = forgetting_attention(qf, kf, split_heads(v_fx, N_HEADS_FOX), log_f.transpose(0, 2, 1))
        y_fx = merge_heads(y_fx) @ w_o_fox[l]

        g_sb, g_fx = jnp.split(jax.nn.sigmoid(gate_pre + b_gate[l]), 2, axis=-1)
        x = x + (g_sb * y_sb + g_fx * y_fx) @ w_out[l]

        h = rmsnorm(x, g_ffn[l])
        if l % 2 == 0:
            x = x + swiglu(h, w_gu_dense[l // 2], w_dn_dense[l // 2])
        else:
            x = x + moe_swiglu(h, w_router[l // 2], w_gu_exp[l // 2], w_dn_exp[l // 2])
    return x


def setup_inputs(seed=0):
    out = dict(first_inputs(seed))
    for name, value in second_inputs(seed + 1).items():
        if name != "x":
            out[name + "_2"] = value
    return out


def reference(
    x, c, positions, w_mod, b_mod, g_norm_mix, w_in, g_q_dil, g_k_dil, g_cq, w_q_up, g_ckv,
    w_kv_up, g_q_nope, g_q_rope, g_k_nope, g_k_rope, w_out, g_norm_mlp, w_mlp_in, w_mlp_out,
    g_mix_2, w_in_2, b_f_2, b_gate_2, g_q_2, g_k_2, w_o_sb_2, w_o_fox_2, w_out_2, g_ffn_2,
    w_gu_dense_2, w_dn_dense_2, w_router_2, w_gu_exp_2, w_dn_exp_2,
):
    x = first_block(
        x, c, positions, w_mod, b_mod, g_norm_mix, w_in, g_q_dil, g_k_dil, g_cq, w_q_up, g_ckv,
        w_kv_up, g_q_nope, g_q_rope, g_k_nope, g_k_rope, w_out, g_norm_mlp, w_mlp_in, w_mlp_out,
    )
    return second_block(
        x, g_mix_2, w_in_2, b_f_2, b_gate_2, g_q_2, g_k_2, w_o_sb_2, w_o_fox_2, w_out_2,
        g_ffn_2, w_gu_dense_2, w_dn_dense_2, w_router_2, w_gu_exp_2, w_dn_exp_2,
    )


_drawn_inputs = setup_inputs


def setup_inputs(seed=0):
    import zlib

    import numpy as np

    out = dict(_drawn_inputs(seed))
    spreads = {}
    factors = {'g_norm_mix': 3.539,
     'g_q_dil': 5.366,
     'g_k_dil': 8.0,
     'g_cq': 8.0,
     'g_ckv': 5.223,
     'g_q_nope': 8.0,
     'g_q_rope': 8.0,
     'g_k_nope': 8.0,
     'g_k_rope': 8.0,
     'g_mix_2': 3.709,
     'b_f_2': 2.886,
     'b_gate_2': 7.995,
     'g_q_2': 3.853,
     'g_k_2': 3.733,
     'g_ffn_2': 3.701}
    for name, (base, spread) in spreads.items():
        noise = np.random.default_rng([zlib.crc32(name.encode()), seed]).standard_normal(out[name].shape)
        drawn = base * np.exp(spread * noise) if base else spread * noise
        out[name] = jnp.asarray(drawn.astype(out[name].dtype))
    for name, factor in factors.items():
        out[name] = (out[name] * factor).astype(out[name].dtype)
    return out
```

```python
from contextlib import ExitStack

import concourse.bass as bass
import numpy as np
from concourse import mybir

F32 = mybir.dt.float32
F32R = mybir.dt.float32r
I32 = mybir.dt.int32
ACT = mybir.ActivationFunctionType
ALU = mybir.AluOpType
AX = mybir.AxisListType

P = 128
S = 256
D = 1024
TT = S // P
KD = D // P
H = 8
DH = 64
ROPE = 32
QL, KVL = 256, 128
QUP = H * (DH + ROPE)
KVUP = H * 2 * DH
W_IN = 1952
F1 = 4096
F2 = 2816
NE, FE = 8, 1408
EPS = 1e-6
PIECE = 2048
RAW, SPLIT = 6, 3
AHEAD = 2
BIG = 1.0e30
LOWEST = -3.0e38
MAGIC = 1.5 * 2.0**23

MODP = 24
N_IN1, N_QUP, N_KVUP, N_OUT, N_MLP = 8, 1, 1, 4, 2 * (F1 // 256)
L1 = N_IN1 + N_QUP + N_KVUP + N_OUT + N_MLP
N_NAT2, N_TURN2, N_WO, N_DENSE = 8, 12, 4, 3 * (F2 // 256)
EXPERT = 18
W_B2 = 2 * L1
L2_MIX = N_NAT2 + N_TURN2 + N_WO + N_OUT
W_DENSE = W_B2 + L2_MIX
W_L3 = W_DENSE + N_DENSE
W_MOE = W_L3 + L2_MIX
W_END = W_MOE + NE * EXPERT


def raw_of(w):
    return w + MODP if w < L1 + AHEAD else w + 2 * MODP


C_ID = 0
C_LNM = C_ID + P
C_INV = C_LNM + TT * S
N_FIRST = C_INV + 16
C_CAUS = 0
C_SBM = C_CAUS + S
C_SBN = C_SBM + 384
C_NTRI = C_SBN + 384
C_TRI = C_NTRI + P
C_TIE = C_TRI + S
N_SECOND = C_TIE + 64

V_C, V_G1, V_G2, V_G3, V_G4 = 0, 8, 24, 40, 56
V_CQ, V_CKV, V_BG = 72, 76, 78
V_QD, V_KD, V_QN, V_KN, V_QF, V_KF = 110, 112, 114, 116, 118, 120
N_VEC = 128
N_LOADS = 25
SETUP_VEC, SETUP_V = 1, 5


def constants():
    first = np.zeros((P, N_FIRST), np.float32)
    c = np.zeros((P, N_SECOND), np.float32)
    p = np.arange(P)
    first[:, C_ID:C_ID + P] = np.eye(P)
    q, k = np.arange(S)[:, None], np.arange(S)[None, :]
    count = np.zeros((S, S))
    for window, dil in ((128, 1), (512, 4), (2048, 16)):
        count += ((k - q) % dil == 0) & (np.abs(k - q) <= window // 2)
    ln = np.where(count > 0, np.log(np.maximum(count, 1)), -BIG)
    first[:, C_LNM:C_LNM + TT * S] = ln.reshape(TT, P, S).transpose(1, 0, 2).reshape(P, TT * S)
    c[:, C_CAUS + P:C_CAUS + S] = np.where(p[None, :] <= p[:, None], 0, -BIG)
    before = (p[:, None] < p[None, :]).astype(np.float32)
    blocks = np.concatenate([before, np.ones((P, P)), before], 1)
    c[:, C_SBM:C_SBM + 384] = blocks
    c[:, C_SBN:C_SBN + 384] = (1 - blocks) * -BIG
    c[:, C_NTRI:C_NTRI + P] = -(p[:, None] >= p[None, :]).astype(np.float32)
    c[:, C_TRI:C_TRI + P] = p[:, None] <= p[None, :]
    c[:, C_TRI + P:C_TRI + S] = 1
    half = ROPE // 2
    first[:, C_INV:C_INV + half] = np.float32(10000.0) ** (-np.arange(half, dtype=np.float32) / half)
    e = np.arange(NE)
    c[:, C_TIE:C_TIE + 64] = (e[None, :] < e[:, None]).reshape(1, 64)
    return first, c


def two_blocks_kernel(nc, a, consts, out):
    with ExitStack() as ctx:
        program(nc, ctx, a, consts, out)


def program(nc, ctx, a, consts, out):
    def sb(name, shape, dt=F32, into=ctx):
        return into.enter_context(nc.sbuf_tensor(name, shape, dt))

    def sem(name):
        return ctx.enter_context(nc.semaphore(name))

    raw = [sb(f"raw{i}", [P, PIECE]) for i in range(RAW)]
    whi = [sb(f"w_high{i}", [P, PIECE], F32R) for i in range(SPLIT)]
    wlo = [sb(f"w_low{i}", [P, PIECE], F32R) for i in range(SPLIT)]
    x = sb("x", [P, TT, D])
    hhi = sb("h_high", [P, KD, S], F32R)
    hlo = sb("h_low", [P, KD, S], F32R)
    acthi = sb("act_high", [P, 3, 512], F32R)
    actlo = sb("act_low", [P, 3, 512], F32R)
    nat = sb("natural", [P, TT, 2048])
    probs = sb("probs", [P, 2, 2 * S])
    pturn = sb("probs_turned", [P, 2, 2 * S])
    con = sb("constants", [P, N_FIRST])
    vec = sb("vector_columns", [P, N_VEC])
    ones = sb("ones", [P, P])
    minus = sb("minus_ones", [P, P])
    modc = sb("mod_columns", [P, 4, KD])
    stat = sb("statistics", [P, 4, 48])
    expsum = sb("exp_sums", [P, 2, TT * H])
    rowmax = sb("row_max", [P, 2, TT])
    negmax = sb("negative_max", [P, 2, TT])
    trig = sb("trig", [P, 2, TT, ROPE // 2])
    grope = sb("rope_gains", [P, 2, 2, ROPE])
    poscol = sb("position_columns", [P, TT])
    psum = [ctx.enter_context(nc.psum_tensor(f"bank{i}", [P, 512], F32)) for i in range(8)]

    first = ExitStack()
    ta = sb("turned1", [P, 4864 + 2048], into=first)
    bias = sb("dilated_bias", [P, 2, TT * S], into=first)
    rtmp = sb("rope_products", [P, 2, TT * H * ROPE // 2], into=first)
    gtb = sb("gate_rows", [P, 2, D], into=first)
    dist = sb("distance", [P, TT * S], into=first)
    first.close()
    tb = sb("turned2", [P, 8192])
    con2 = sb("constants2", [P, N_SECOND])
    forget = sb("forget", [P, 3, TT * H])
    wsmall = sb("small_weights", [P, 3, KD * H])
    small = sb("small_rows", [1, 2 * H])

    def heads_turned(t, c0):
        return t[:, c0:c0 + 1024].rearrange("p (a s) -> p a s", s=S)

    qdT, kdT, qnT, knT = (heads_turned(ta, 1024 * i) for i in range(4))
    qrT = ta[:, 4096:4608].rearrange("p (a s) -> p a s", s=S)
    krT = ta[:, 4608:4864]
    kvup = ta[:, 4864:6912].rearrange("p (t n) -> p t n", t=TT)
    hf1 = ta[:, 4864:6912]
    latent = ta[:, 2048:2816]
    relu = ta[:, 0:3072].rearrange("p (i b n) -> p i b n", i=2, b=3)
    modsum = nat[:, :, 1024:2048]
    sqT, skT, fqT, fkT = (heads_turned(tb, 1024 * i) for i in range(4))
    gates = tb[:, 4096:8192]
    hf2 = tb[:, 4864:6912]
    silu = tb[:, 0:2048].rearrange("p (i b n) -> p i b n", i=2, b=2)
    combine = tb[:, 2048:4096].rearrange("p (e s) -> p e s", s=S)
    route = tb[:, 4096:4608]
    ident = con[:, C_ID:C_ID + P]
    lathi = acthi[:, :, :].rearrange("p a n -> p (a n)")[:, 0:768]
    latlo = actlo[:, :, :].rearrange("p a n -> p (a n)")[:, 0:768]
    square = probs[:, :, :].rearrange("p b s -> p (b s)")
    qn_nat = probs
    stage = bias[:, 0, 0:P]
    pos_int = bias[0:1, 1, 0:S].bitcast(I32)
    pos_row = rtmp[0:1, 0, 0:S]
    gain_row = rtmp[0:1, 1, 0:4 * ROPE]

    arrived = [sem(f"piece_arrived{i}") for i in range(RAW)]
    high_done = sem("weights_high_done")
    raw_used = sem("raw_piece_used")
    used = sem("piece_multiplied")
    loaded, ones_set, small_in = sem("vectors_loaded"), sem("ones_set"), sem("small_weights_in")
    bias_zero, bias_row = sem("mod_sums_zeroed"), sem("mod_bias_in")
    setup_t, setup_v, setup_a = sem("setup_tensor"), sem("setup_vector"), sem("setup_scalar")
    mod_summed, mod_reduced, gt_ready = sem("mod_summed"), sem("mod_reduced"), sem("gate_rows_ready")
    squares, squares_used = sem("squares_ready"), sem("squares_used")
    ms_ready, rs_ready = sem("mean_squares_ready"), sem("rsqrt_guess_ready")
    xn_ready, h_turned, h_float = sem("xn_ready"), sem("h_turned"), sem("h_float")
    h_high, h_low = sem("h_high_ready"), sem("h_low_ready")
    proj_out = sem("projection_stored")
    qk_norm, qk_turned, qk_out = sem("qk_normed"), sem("qk_turned"), sem("qk_turned_stored")
    lat_norm, lat_turned, lat_float = sem("latent_normed"), sem("latent_turned"), sem("latent_float")
    lat_high, lat_low = sem("latent_high"), sem("latent_low")
    qup_out, kvup_out = sem("q_up_stored"), sem("kv_up_stored")
    mla_norm, mla_turned = sem("mla_normed"), sem("mla_turned")
    mla_out_a, mla_out_v = sem("mla_nope_stored"), sem("mla_rope_stored")
    bias_ready = sem("dilated_bias_ready")
    scores, shift, probs_ready = sem("scores_ready"), sem("row_shift_ready"), sem("probs_ready")
    turned, pt_ready, values = sem("probs_turned"), sem("probs_turned_stored"), sem("values_done")
    attn_out = sem("attention_stored")
    sb_tail, sb_soft, sb_sum, sb_log = sem("sb_tail"), sem("sb_softplus"), sem("sb_summed"), sem("sb_log_weights")
    o_turned, o_high, o_low = sem("o_turned"), sem("o_high"), sem("o_low")
    x_mixed, x_done = sem("x_mixed"), sem("x_done")
    f_logit, f_abs, f_tail, f_cost = sem("forget_logits"), sem("forget_abs"), sem("forget_tail"), sem("forget_cost")
    t2_out = sem("turned_projection_stored")
    gated, z_high, z_low = sem("gated"), sem("gated_high"), sem("gated_low")
    r_logit, r_max, r_exp, r_comb = sem("router_logits"), sem("router_max"), sem("router_exp"), sem("router_weights")
    r_spread, r_out = sem("router_spread"), sem("router_spread_stored")
    f_one = [sem(f"ff{i}_function") for i in range(4)]
    f_two = [sem(f"ff{i}_product") for i in range(4)]
    f_hi = [sem(f"ff{i}_high") for i in range(4)]
    f_lo = [sem(f"ff{i}_low") for i in range(4)]
    e_comb = sem("expert_silu_up")
    vstep, astep, pstep = sem("vector_step"), sem("scalar_step"), sem("pool_step")
    stored = sem("out_stored")

    block = ctx.enter_context(nc.Block())

    def loop(value, it, per):
        return value if it is None else value + it * per

    def group_of(layer, second):
        return 2 * layer + second

    def softmax_of(g):
        return g if g < 32 else 32 + (g - 32) // 16 * H + g % 16 - H

    @block.sync
    def _(sp):
        def load(r, src, it=None, per=RAW):
            if r >= RAW:
                sp.wait_ge(raw_used, loop(r - RAW + 1, it, per))
            k, n = src.shape[1], src.shape[2]
            dst = raw[r % RAW][:, 0:k * n].rearrange("p (k n) -> p k n", k=k)
            sp.dma_start(dst, src).then_inc(arrived[r % RAW], 16)

        def rows_of_k(w):
            return w.rearrange("(k p) n -> p k n", p=P)

        def load_mod(l, r):
            w = rows_of_k(a["w_mod"][l])
            for s in range(6):
                for q in range(4):
                    load(r + 4 * s + q, w[:, 2 * q:2 * q + 2, s * D:(s + 1) * D])

        def load_natural(w, r, chunks):
            for c0, n in chunks:
                for half in range(2):
                    load(r, rows_of_k(w)[:, 4 * half:4 * half + 4, c0:c0 + n])
                    r += 1
                    if r == raw_of(L1) + AHEAD:
                        load_mod(1, r)
                        r += MODP

        def take(w, b, k):
            return w.rearrange("(b k p) n -> p b k n", k=k, p=P)[:, bass.ds(b, 1)].rearrange("p b k n -> p (b k) n")

        load_mod(0, 0)
        for l in range(2):
            w = l * L1
            load_natural(a["w_in"][l], raw_of(w), [(0, 512), (512, 512), (1024, 512), (1536, W_IN - 1536)])
            w += N_IN1
            load(raw_of(w), rows_of_k(a["w_q_up"][l]))
            load(raw_of(w + 1), rows_of_k(a["w_kv_up"][l]))
            load_natural(a["w_out"][l], raw_of(w + 2), [(0, 512), (512, 512)])
            w += 2 + N_OUT
            wu, wd = rows_of_k(a["w_mlp_in"][l]), a["w_mlp_out"][l]

            def pair(j, it):
                b = j if it is None else it * 3 + j
                load(raw_of(w + 1 + 2 * j), wu[:, :, bass.ds((b + 1) * 256, 256)], it)
                load(raw_of(w + 2 + 2 * j), take(wd, b, 2), it)

            load(raw_of(w), wu[:, :, 0:256])
            for j in range(3):
                pair(j, None)
            with sp.Fori(1, 5) as it:
                for j in range(3):
                    pair(j, it)
            load(raw_of(w + N_MLP - 1), take(wd, F1 // 256 - 1, 2))
        for l in range(2):
            w = (W_B2, W_L3)[l]
            wi = a["w_in_2"][l]
            load_natural(wi, raw_of(w), [(1536, 512), (2048, 512), (2560, 512), (1024, 512)])
            w += N_NAT2
            for j in range(N_TURN2):
                c0 = 256 * j if j < 4 else 3080 + 256 * (j - 4)
                load(raw_of(w + j), rows_of_k(wi)[:, :, c0:c0 + 256])
            w += N_TURN2
            for i, name in enumerate(("w_o_sb_2", "w_o_fox_2")):
                for j in range(2):
                    load(raw_of(w + 2 * i + j), rows_of_k(a[name][l])[:, :, 512 * j:512 * j + 512])
            load_natural(a["w_out_2"][l], raw_of(w + N_WO), [(0, 512), (512, 512)])
            if l == 0:
                w = W_DENSE
                wu, wd = rows_of_k(a["w_gu_dense_2"][0]), a["w_dn_dense_2"][0]

                def triple(j, it):
                    b = j if it is None else it * 2 + j
                    load(raw_of(w + 2 + 3 * j), wu[:, :, bass.ds((b + 1) * 256, 256)], it)
                    load(raw_of(w + 3 + 3 * j), wu[:, :, bass.ds((b + 1) * 256 + F2, 256)], it)
                    load(raw_of(w + 4 + 3 * j), take(wd, b, 2), it)

                load(raw_of(w), wu[:, :, 0:256])
                load(raw_of(w + 1), wu[:, :, F2:F2 + 256])
                for j in range(2):
                    triple(j, None)
                with sp.Fori(1, 5) as it:
                    for j in range(2):
                        triple(j, it)
                load(raw_of(w + N_DENSE - 1), take(wd, F2 // 256 - 1, 2))
            else:
                wu = a["w_gu_exp_2"][0].rearrange("e (k p) n -> p e k n", p=P)
                wd = a["w_dn_exp_2"][0].rearrange("e (k p) n -> p e k n", p=P)
                with sp.Fori(0, NE) as it:
                    r = raw_of(W_MOE)

                    def gate_up(b, c0):
                        n = 256 if b < 5 else 128
                        v = wu[:, bass.ds(it, 1), :, c0 + 256 * b:c0 + 256 * b + n]
                        return v.rearrange("p e k n -> p (e k) n")

                    def down(b):
                        v = wd[:, bass.ds(it, 1), 2 * b:min(2 * b + 2, 11), :]
                        return v.rearrange("p e k n -> p (e k) n")

                    load(r, gate_up(0, 0), it, EXPERT)
                    load(r + 1, gate_up(0, FE), it, EXPERT)
                    for b in range(5):
                        load(r + 2 + 3 * b, gate_up(b + 1, 0), it, EXPERT)
                        load(r + 3 + 3 * b, gate_up(b + 1, FE), it, EXPERT)
                        load(r + 4 + 3 * b, down(b), it, EXPERT)
                    load(r + 17, down(5), it, EXPERT)
        sp.wait_ge(x_done, 3 + NE)
        sp.dma_start(out.rearrange("b (t p) d -> p (b t) d", p=P), x[:, :, :]).then_inc(stored, 16)
        sp.wait_ge(stored, 16)

    @block.gpsimd
    def _(pool):
        nc.gpsimd.memset(stage, 0.0).then_inc(pstep, 1)
        nc.gpsimd.memset(minus[:, :], -1.0).then_inc(ones_set, 1)
        nc.gpsimd.memset(ones[:, :], 1.0).then_inc(ones_set, 1)
        pool.wait_ge(pstep, 1)
        n = [0]

        def fetch(dst, src, slow=False):
            pool.dma_start(dst, src, allow_slow_non_contiguous=slow).then_inc(loaded, 16)
            n[0] += 1

        fetch(stage[V_C:V_C + KD, :], a["c"].rearrange("o (k p) -> (o k) p", p=P))
        for r, name in ((V_G1, "g_norm_mix"), (V_G2, "g_norm_mlp"), (V_G3, "g_mix_2"), (V_G4, "g_ffn_2"),
                        (V_CQ, "g_cq"), (V_CKV, "g_ckv"), (V_BG, "b_gate_2")):
            src = a[name].rearrange("l (k p) -> (l k) p", p=P)
            fetch(stage[r:r + src.shape[0], :], src)
        for r, name in ((V_QD, "g_q_dil"), (V_KD, "g_k_dil"), (V_QN, "g_q_nope"), (V_KN, "g_k_nope"),
                        (V_QF, "g_q_2"), (V_KF, "g_k_2")):
            for twice in range(2):
                fetch(stage[r:r + 2, DH * twice:DH * twice + DH], a[name])
        fetch(con[:, :], consts[0])
        fetch(pos_int, a["positions"])
        for i, name in enumerate(("g_q_rope", "g_k_rope")):
            fetch(gain_row[:, 64 * i:64 * i + 64], a[name].rearrange("(o l) r -> o (l r)", o=1))
        fetch(x[:, :, :], a["x"].rearrange("b (t p) d -> p (b t) d", p=P))
        assert n[0] == N_LOADS
        step = [1]
        for l in range(2):
            for s in range(6):
                g = 6 * l + s
                if l == 1 and s == 0:
                    pool.wait_ge(x_done, 1)
                if g >= 2:
                    pool.wait_ge(mod_reduced, g - 1)
                nc.gpsimd.memset(modsum[:, g % 2, :], 0.0).then_inc(bias_zero, 1)
                pool.wait_ge(bias_zero, g + 1)
                pool.dma_start(modsum[0:1, g % 2, :], a["b_mod"][l:l + 1, s * D:(s + 1) * D]).then_inc(bias_row, 16)
                pool.wait_ge(bias_row, 16 * (g + 1))
            pool.wait_ge(setup_v, SETUP_V)
            for h in range(H):
                g = 8 * l + h
                if g >= 2:
                    pool.wait_ge(shift, 16 * l + h - 1 if h >= 2 else 16 * (l - 1) + h + 7)
                b = bias[:, g % 2, :]
                nc.gpsimd.tensor_scalar(b, dist[:, :], -(2.0 ** -(h + 1)), None, ALU.mult).then_inc(pstep, 1)
                step[0] += 1
                pool.wait_ge(pstep, step[0])
                nc.gpsimd.tensor_tensor(b, b, con[:, C_LNM:C_LNM + TT * S], ALU.add).then_inc(bias_ready, 1)
        pool.wait_ge(x_done, 2)
        pool.dma_start(con2[:, :], consts[1]).then_inc(small_in, 16)
        pool.dma_start(small[0:1, :], a["b_f_2"].rearrange("(o l) h -> o (l h)", o=1)).then_inc(small_in, 16)
        for i, w in enumerate((a["w_in_2"][0][:, 3072:3080], a["w_in_2"][1][:, 3072:3080], a["w_router_2"][0])):
            pool.dma_start(wsmall[:, i, :].rearrange("p (k n) -> p k n", k=KD),
                           w.rearrange("(k p) n -> p k n", p=P), allow_slow_non_contiguous=True).then_inc(small_in, 16)

    @block.scalar
    def _(act):
        steps, ahead, jobs, sqs = [0], [0], [0], [0]

        def step(ins):
            steps[0] += 1
            ins.then_inc(astep, 1)
            act.wait_ge(astep, steps[0])

        def copy(dst, src, scale=1.0):
            return nc.scalar.activation(dst, src, ACT.Copy, scale=scale)

        def split(w, it=None, per=RAW):
            r = raw_of(w)
            act.wait_ge(arrived[r % RAW], loop(16 * (r // RAW + 1), it, 16 * per // RAW))
            if w >= SPLIT:
                act.wait_ge(used, loop(w - SPLIT + 1, it, per))
            copy(whi[w % SPLIT][:, :], raw[r % RAW][:, :]).then_inc(high_done, 1)

        def split_to(w):
            while ahead[0] <= min(w, W_END - 1):
                split(ahead[0])
                ahead[0] += 1

        def rsqrt_guess(n):
            jobs[0] += 1
            act.wait_ge(ms_ready, jobs[0])
            step(nc.scalar.activation(stat[:, 1, 0:n], stat[:, 0, 0:n], ACT.Ln))
            nc.scalar.activation(stat[:, 1, 0:n], stat[:, 1, 0:n], ACT.Exp, scale=-0.5).then_inc(rs_ready, 1)

        def square_job(parts):
            if sqs[0]:
                act.wait_ge(squares_used, sqs[0])
            for dst, src, total in parts[:-1]:
                step(nc.scalar.activation(dst, src, ACT.Square, accum_out=total))
            dst, src, total = parts[-1]
            ins = nc.scalar.activation(dst, src, ACT.Square, accum_out=total) if total is not None \
                else nc.scalar.activation(dst, src, ACT.Square)
            ins.then_inc(squares, 1)
            sqs[0] += 1

        def norm_squares():
            square_job([(square, x[:, t, :], stat[:, 2, t:t + 1]) for t in range(TT)])
            rsqrt_guess(TT)

        def norm_high(n):
            hf = hf1 if n < 4 else hf2
            for b in range(4):
                act.wait_ge(h_float, 4 * n + b + 1)
                copy(hhi[:, 2 * b:2 * b + 2, :], hf[:, 512 * b:512 * b + 512].rearrange("p (a s) -> p a s", s=S)) \
                    .then_inc(h_high, 1)

        def store_chunk(c, w, n):
            split_to(w + AHEAD)
            act.wait_ge(used, w + 1)
            for t in range(TT):
                ins = copy(nat[:, t, 512 * c:512 * c + n], psum[4 + 2 * (c % 2) + t][:, 0:n])
            ins.then_inc(proj_out, 1)

        def qk_heads(l, qT, kT, vq, vk):
            for t in range(TT):
                square_job([(square, nat[:, t, 0:D], None)])
            rsqrt_guess(32)
            for b in range(4):
                act.wait_ge(qk_turned, 4 * l + b + 1)
                dst, g = ((qT, vq), (kT, vk))[b // 2]
                copy(dst[:, 2 * (b % 2):2 * (b % 2) + 2, :], psum[b][:, :].rearrange("p (a s) -> p a s", s=S),
                     scale=vec[:, g:g + 1]).then_inc(qk_out, 1)

        def softmax_head(g, scale, from_psum, causal=False):
            si = softmax_of(g)
            act.wait_ge(shift, si + 1)
            if g >= 2:
                act.wait_ge(turned, max(si - 1, 1))
            for t in range(TT):
                n = P if causal and t == 0 else S
                src = psum[g % 2] if from_psum else probs[:, g % 2, :]
                i = 8 * t + g % H
                ins = nc.scalar.activation(probs[:, g % 2, S * t:S * t + n], src[:, S * t:S * t + n], ACT.Exp,
                                           bias=negmax[:, g % 2, t:t + 1], scale=scale,
                                           accum_out=expsum[:, (g // H) % 2, i:i + 1])
            ins.then_inc(probs_ready, 1)

        def turn_o(l):
            for b in range(4):
                act.wait_ge(o_turned, 4 * l + b + 1)
                copy(hhi[:, 2 * b:2 * b + 2, :], psum[b][:, :].rearrange("p (a s) -> p a s", s=S)).then_inc(o_high, 1)

        act.wait_ge(setup_v, SETUP_VEC)
        nc.scalar.activation(vec[:, V_C:V_C + KD], vec[:, V_C:V_C + KD], ACT.Silu).then_inc(setup_a, 1)
        act.wait_ge(setup_v, SETUP_V)
        nc.scalar.activation(trig[:, :, :, :], trig[:, :, :, :], ACT.Sin).then_inc(setup_a, 1)

        for l in range(2):
            w = l * L1
            if l == 0:
                act.wait_ge(loaded, 16 * N_LOADS)
            else:
                act.wait_ge(x_done, l)
            norm_squares()
            if l == 0:
                split_to(AHEAD - 1)
            for s in (2, 5):
                act.wait_ge(mod_reduced, 6 * l + s + 1)
                for h in range(2):
                    ins = copy(gtb[:, s // 3, 512 * h:512 * h + 512], psum[(2 if s == 2 else 4) + h][:, :])
                ins.then_inc(gt_ready, 1)
            norm_high(2 * l)
            for c in range(4):
                store_chunk(c, w + 2 * c + 1, 512 if c < 3 else W_IN - 1536)
            w += N_IN1
            act.wait_ge(proj_out, 4 * l + 4)
            square_job([(square[:, 0:n], nat[:, t, c0:c0 + n], stat[:, 2, 2 * i + t:2 * i + t + 1])
                        for i, (c0, n) in enumerate(((1536, QL), (1792, KVL), (1920, ROPE))) for t in range(TT)])
            rsqrt_guess(6)
            qk_heads(l, qdT, kdT, V_QD + l, V_KD + l)
            act.wait_ge(lat_float, l + 1)
            copy(lathi, latent).then_inc(lat_high, 1)
            split_to(w + AHEAD - 1)
            act.wait_ge(used, w + 1)
            for t in range(TT):
                b0 = 6 - 2 * t
                step(copy(nat[:, t, 0:512], psum[b0][:, :]))
                ins = copy(nat[:, t, 512:768], psum[b0 + 1][:, 0:256])
                if t == 0:
                    step(ins)
            ins.then_inc(qup_out, 1)
            act.wait_ge(qup_out, l + 1)
            split_to(w + 1 + AHEAD)
            for t in range(TT):
                square_job([(square[:, 0:QUP], nat[:, t, 0:QUP], None)])
            act.wait_ge(kvup_out, l + 1)
            for t in range(TT):
                square_job([(square[:, 0:512].rearrange("p (h d) -> p h d", d=DH),
                             kvup[:, t, :].rearrange("p (h d) -> p h d", d=P)[:, :, 0:DH], None)])
            rsqrt_guess(48)
            for b in range(4):
                act.wait_ge(mla_turned, 6 * l + b + 1)
                dst, g = ((qnT, V_QN + l), (knT, V_KN + l))[b // 2]
                copy(dst[:, 2 * (b % 2):2 * (b % 2) + 2, :], psum[4 + b][:, :].rearrange("p (a s) -> p a s", s=S),
                     scale=vec[:, g:g + 1]).then_inc(mla_out_a, 1)
            for h in range(H):
                softmax_head(16 * l + h, 1.0, False)
            for h in range(H):
                softmax_head(16 * l + H + h, float(DH + ROPE) ** -0.5, True)
            turn_o(l)
            w += 2
            for j in range(N_OUT):
                split_to(w + j + AHEAD)
            w += N_OUT
            act.wait_ge(x_mixed, 2 * l + 2)
            norm_squares()
            norm_high(2 * l + 1)

            def relu_block(b, slot, it=None):
                act.wait_ge(used, loop(w + 2 * b, it, RAW) if b else w + 1)
                if b >= 3:
                    act.wait_ge(f_two[l], loop(b - 2, it, 3))
                nc.scalar.activation(relu[:, 0, slot, :], psum[slot][:, :], ACT.Relu).then_inc(f_one[l], 1)

            def high_block(b, slot, it=None):
                act.wait_ge(f_two[l], loop(b + 1, it, 3))
                if b >= 3:
                    act.wait_ge(used, loop(w + 2 * (b - 3) + 3, it, RAW))
                copy(acthi[:, slot, :], relu[:, 1, slot, :]).then_inc(f_hi[l], 1)

            split_to(w + 2)
            relu_block(0, 0)
            high_block(0, 0)
            for j in range(3):
                split_to(w + 3 + 2 * j)
                relu_block(j + 1, (j + 1) % 3)
                split_to(w + 4 + 2 * j)
                high_block(j + 1, (j + 1) % 3)
            with act.Fori(0, 4) as it:
                for j in range(3, 6):
                    split(w + 3 + 2 * j, it)
                    relu_block(j + 1, (j + 1) % 3, it)
                    split(w + 4 + 2 * j, it)
                    high_block(j + 1, (j + 1) % 3, it)
            ahead[0] = w + N_MLP + 1
            split_to(w + N_MLP - 1 + AHEAD)

        for l in range(2):
            w = (W_B2, W_L3)[l]
            n = 4 + 2 * l
            act.wait_ge(x_done, 2 + l)
            norm_squares()
            norm_high(n)
            for c in range(4):
                store_chunk(c, w + 2 * c + 1, 512)
            w += N_NAT2
            for j in range(N_TURN2):
                split_to(w + j + AHEAD - 1)
                act.wait_ge(used, w + j + 1)
                b = psum[j % 4]
                if j < 4:
                    ins = copy((sqT, skT)[j // 2][:, 2 * (j % 2):2 * (j % 2) + 2, :],
                               b[:, :].rearrange("p (a s) -> p a s", s=S), scale=DH ** -0.5 if j < 2 else 1.0)
                else:
                    for i in range(2):
                        f = 2 * (j - 4) + i
                        ins = nc.scalar.activation(gates[:, S * f:S * f + S], b[:, S * i:S * i + S], ACT.Sigmoid,
                                                   bias=vec[:, V_BG + 16 * l + f:V_BG + 16 * l + f + 1])
                ins.then_inc(t2_out, 1)
                split_to(w + j + AHEAD)
            act.wait_ge(f_abs, l + 1)
            step(nc.scalar.activation(forget[:, 1, :], forget[:, 1, :], ACT.Exp, scale=-1.0))
            nc.scalar.activation(forget[:, 1, :], forget[:, 1, :], ACT.Ln, bias=1.0).then_inc(f_tail, 1)
            act.wait_ge(proj_out, 8 + 4 * l + 4)
            qk_heads(2 + l, fqT, fkT, V_QF + l, V_KF + l)
            g0 = 32 + 16 * l
            act.wait_ge(squares_used, sqs[0])

            def tail(h):
                g = g0 + h
                pv = probs[:, g % 2, 0:384]
                act.wait_ge(scores, g + 1)
                step(nc.scalar.activation(pv, psum[g % 2][:, 0:384], ACT.Abs))
                step(nc.scalar.activation(pv, pv, ACT.Exp, scale=-1.0))
                nc.scalar.activation(pv, pv, ACT.Ln, bias=1.0).then_inc(sb_tail, 1)

            tail(0)
            for h in range(H):
                if h + 1 < H:
                    tail(h + 1)
                g = g0 + h
                act.wait_ge(sb_log, H * l + h + 1)
                act.wait_ge(values, g - 1)
                nc.scalar.activation(pturn[:, g % 2, 0:384], probs[:, g % 2, 0:384], ACT.Exp).then_inc(probs_ready, 1)
            for h in range(H):
                softmax_head(g0 + H + h, 1.0, False, causal=True)
            turn_o(2 + l)
            w += N_TURN2
            for j in range(N_WO):
                split_to(w + j + AHEAD)
            act.wait_ge(used, w + N_WO)
            for q in range(4):
                act.wait_ge(gated, 4 * l + q + 1)
                copy(hhi[:, 2 * q:2 * q + 2, :], gates[:, 512 * q:512 * q + 512].rearrange("p (a s) -> p a s", s=S)) \
                    .then_inc(z_high, 1)
            w += N_WO
            for j in range(N_OUT):
                split_to(w + j + AHEAD)
            w += N_OUT
            act.wait_ge(x_mixed, 2 * (2 + l) + 2)
            norm_squares()
            norm_high(n + 1)

            def silu_block(f, w, b, n, it=None, per=0, wper=0):
                act.wait_ge(used, loop(w, it, wper))
                if b >= 2:
                    act.wait_ge(f_two[f], loop(b - 1, it, per))
                nc.scalar.activation(silu[:, 0, b % 2, 0:n], psum[b % 2][:, 0:n], ACT.Silu).then_inc(f_one[f], 1)

            def high_block2(f, w, b, n, it=None, per=0, wper=0):
                act.wait_ge(f_two[f], loop(b + 1, it, per))
                act.wait_ge(used, loop(w, it, wper))
                copy(acthi[:, b % 2, 0:n], silu[:, 1, b % 2, 0:n]).then_inc(f_hi[f], 1)

            if l == 0:
                split_to(w + 2)
                silu_block(2, w + 1, 0, 512)
                split_to(w + 3)
                high_block2(2, w, 0, 512)
                for j in range(2):
                    m = w + 2 + 3 * j
                    split_to(m + 2)
                    silu_block(2, m + 1, j + 1, 512)
                    split_to(m + 4)
                    high_block2(2, m, j + 1, 512)
                with act.Fori(0, 4) as it:
                    for j in range(2, 4):
                        m = w + 2 + 3 * j
                        split(m + 2, it)
                        silu_block(2, m + 1, j + 1, 512, it, 2, RAW)
                        split(m + 3, it)
                        split(m + 4, it)
                        high_block2(2, m, j + 1, 512, it, 2, RAW)
                ahead[0] = w + N_DENSE + 1
                split_to(w + N_DENSE - 1 + AHEAD)
            else:
                act.wait_ge(r_max, 1)
                for t in range(TT):
                    ins = nc.scalar.activation(route[:, 16 + 8 * t:24 + 8 * t], route[:, 8 * t:8 * t + 8], ACT.Exp,
                                               bias=route[:, 32 + t:33 + t])
                ins.then_inc(r_exp, 1)
                act.wait_ge(r_spread, 1)
                for q in range(4):
                    ins = copy(combine[:, 2 * q:2 * q + 2, :], psum[q][:, :].rearrange("p (e s) -> p e s", s=S))
                ins.then_inc(r_out, 1)

                def expert(it, last):
                    def split_ahead(m):
                        if not last or m < w + EXPERT:
                            split(m, it, EXPERT)

                    split_ahead(w + 2)
                    silu_block(3, w + 1, 0, 512, it, 6, EXPERT)
                    split_ahead(w + 3)
                    high_block2(3, w, 0, 512, it, 6, EXPERT)
                    for b in range(1, 6):
                        m = w + 3 * b - 1
                        n = 512 if b < 5 else 256
                        split_ahead(m + 2)
                        silu_block(3, m + 1, b, n, it, 6, EXPERT)
                        split_ahead(m + 3)
                        split_ahead(m + 4)
                        high_block2(3, m, b, n, it, 6, EXPERT)
                    split_ahead(w + EXPERT + 1)

                with act.Fori(0, NE - 1) as it:
                    expert(it, False)
                expert(NE - 1, True)

    @block.vector
    def _(dve):
        steps, low, jobs, sqs, setups = [0], [0], [0], [0], [0]
        V = nc.vector

        def step(ins):
            steps[0] += 1
            ins.then_inc(vstep, 1)
            dve.wait_ge(vstep, steps[0])

        def rest(w, it=None, per=RAW):
            dve.wait_ge(high_done, loop(w + 1, it, per))
            V.tensor_tensor(wlo[w % SPLIT][:, :], raw[raw_of(w) % RAW][:, :], whi[w % SPLIT][:, :].bitcast(F32),
                            ALU.subtract).then_inc(raw_used, 1)

        def rest_to(w):
            while low[0] <= min(w, W_END - 1):
                rest(low[0])
                low[0] += 1

        def take_squares():
            sqs[0] += 1
            dve.wait_ge(squares, sqs[0])

        def means(parts):
            for c, n, size in parts:
                ins = V.tensor_scalar(stat[:, 0, c:c + n], stat[:, 2, c:c + n], 1.0 / size, EPS, ALU.mult, ALU.add)
            return ins

        def refine(n):
            jobs[0] += 1
            v, y, u = stat[:, 0, 0:n], stat[:, 1, 0:n], stat[:, 3, 0:n]
            dve.wait_ge(rs_ready, jobs[0])
            step(V.tensor_tensor(u, y, y, ALU.mult))
            step(V.tensor_tensor(u, u, v, ALU.mult))
            step(V.tensor_scalar(u, u, -0.5, 1.5, ALU.mult, ALU.add))
            step(V.tensor_tensor(y, y, u, ALU.mult))

        def norm(n, scale, shift_):
            take_squares()
            ins = means([(0, TT, D)])
            step(ins)
            V.sem_inc(ms_ready, 1)
            V.sem_inc(squares_used, 1)
            refine(TT)
            for t in range(TT):
                ins = V.tensor_scalar(nat[:, t, 0:D], x[:, t, :], stat[:, 1, t:t + 1], None, ALU.mult)
            ins.then_inc(xn_ready, 1)
            hf = hf1 if n < 4 else hf2

            def low_part(b):
                dve.wait_ge(h_high, 4 * n + b + 1)
                V.tensor_tensor(hlo[:, 2 * b:2 * b + 2, :],
                                hf[:, 512 * b:512 * b + 512].rearrange("p (a s) -> p a s", s=S),
                                hhi[:, 2 * b:2 * b + 2, :].bitcast(F32), ALU.subtract).then_inc(h_low, 1)

            for b in range(4):
                dve.wait_ge(h_turned, 4 * n + b + 1)
                for i in range(2):
                    k = 2 * b + i
                    ins = V.tensor_scalar(hf[:, S * k:S * k + S], psum[b][:, S * i:S * i + S], scale(k),
                                          shift_(k) if shift_ else None, ALU.mult, *([ALU.add] if shift_ else []))
                ins.then_inc(h_float, 1)
                if b:
                    low_part(b - 1)
            low_part(3)

        def heads_norm(l):
            for t in range(TT):
                take_squares()
                V.tensor_reduce(stat[:, 2, 16 * t:16 * t + 16], square.rearrange("p (h d) -> p h d", d=DH),
                                AX.X, ALU.add).then_inc(squares_used, 1)
            dve.wait_ge(squares_used, sqs[0])
            means([(0, 32, DH)]).then_inc(ms_ready, 1)
            refine(32)
            for t in range(TT):
                v = nat[:, t, 0:D].rearrange("p (h d) -> p h d", d=DH)
                ins = V.tensor_tensor(v, v, stat[:, 1, 16 * t:16 * t + 16].unsqueeze(2).to_broadcast([P, 16, DH]), ALU.mult)
            ins.then_inc(qk_norm, 1)

        def turn_store(g, n):
            dve.wait_ge(turned, softmax_of(g) + 1)
            if g >= 2:
                dve.wait_ge(values, g - 1)
            V.tensor_copy(pturn[:, g % 2, 0:n], psum[2 + g % 2][:, 0:n]).then_inc(pt_ready, 1)

        def slot_free(g):
            if g >= 2:
                dve.wait_ge(probs_ready, g - 1)
                if softmax_of(g) >= 2:
                    dve.wait_ge(turned, softmax_of(g) - 1)

        def added_max(g, addends):
            dve.wait_ge(scores, g + 1)
            slot_free(g)
            for t, (n, add) in enumerate(addends):
                c = slice(S * t, S * t + n)
                ins = V.tensor_tensor_reduce(probs[:, g % 2, c], psum[g % 2][:, c], add, 1.0, LOWEST,
                                             ALU.add, ALU.max, rowmax[:, g % 2, t:t + 1])
            step(ins)
            V.tensor_scalar(negmax[:, g % 2, :], rowmax[:, g % 2, :], -1.0, None, ALU.mult).then_inc(shift, 1)

        def dilated_max(g, l, h):
            dve.wait_ge(bias_ready, 8 * l + h + 1)
            added_max(g, [(S, bias[:, (8 * l + h) % 2, S * t:S * t + S]) for t in range(TT)])

        def plain_max(g, scale):
            dve.wait_ge(scores, g + 1)
            slot_free(g)
            step(V.tensor_reduce(rowmax[:, g % 2, :], psum[g % 2][:, :].rearrange("p (t s) -> p t s", s=S), AX.X, ALU.max))
            V.tensor_scalar(negmax[:, g % 2, :], rowmax[:, g % 2, :], -scale, None, ALU.mult).then_inc(shift, 1)

        def store_group(layer, second, divide=True):
            j = group_of(layer, second)
            dve.wait_ge(probs_ready, 8 * j + 8)
            if divide:
                sums = expsum[:, j % 2, :]
                step(V.reciprocal(sums, sums))
            dve.wait_ge(values, 8 * j + 8)
            for t in range(TT):
                dst = nat[:, t, 512 * second:512 * second + 512]
                if divide:
                    ins = V.tensor_tensor(dst.rearrange("p (h d) -> p h d", d=DH),
                                          psum[4 + t][:, :].rearrange("p (h d) -> p h d", d=DH),
                                          sums[:, 8 * t:8 * t + 8].unsqueeze(2).to_broadcast([P, H, DH]), ALU.mult)
                else:
                    ins = V.tensor_copy(dst, psum[4 + t][:, :])
            ins.then_inc(attn_out, 1)

        def turn_o(l):
            for b in range(4):
                dve.wait_ge(o_high, 4 * l + b + 1)
                V.tensor_tensor(hlo[:, 2 * b:2 * b + 2, :], psum[b][:, :].rearrange("p (a s) -> p a s", s=S),
                                hhi[:, 2 * b:2 * b + 2, :].bitcast(F32), ALU.subtract).then_inc(o_low, 1)

        def add_to_x(bank, t, half, gate):
            xs = x[:, t, 512 * half:512 * half + 512]
            if gate is None:
                return V.tensor_tensor(xs, xs, psum[bank][:, :], ALU.add)
            tmp = square[:, 512 * t:512 * t + 512]
            step(V.tensor_tensor(tmp, psum[bank][:, :], gtb[:, gate, 512 * half:512 * half + 512], ALU.mult))
            return V.tensor_tensor(xs, xs, tmp, ALU.add)

        dve.wait_ge(setup_t, 1)
        V.tensor_copy(vec[:, :], psum[0][:, 0:N_VEC]).then_inc(setup_v, 1)
        V.tensor_copy(pos_row, pos_int).then_inc(setup_v, 1)
        dve.wait_ge(setup_t, 2)
        V.tensor_copy(poscol[:, :], psum[1][:, 0:TT]).then_inc(setup_v, 1)
        V.tensor_copy(grope[:, :, :, :].rearrange("p a b c -> p (a b c)"), psum[1][:, P:2 * P]).then_inc(setup_v, 1)
        step(V.tensor_scalar(vec[:, V_QD:V_QD + 2], vec[:, V_QD:V_QD + 2], DH ** -0.5, None, ALU.mult))
        step(V.tensor_scalar(vec[:, V_QF:V_QF + 2], vec[:, V_QF:V_QF + 2], DH ** -0.5, None, ALU.mult))
        dve.wait_ge(setup_v, 4)
        two_pi = 2 * np.pi
        c1 = 6.28125
        c2 = float(np.float32(two_pi - c1))
        c3 = float(two_pi - c1 - c2)
        half = ROPE // 2
        for t in range(TT):
            d = dist[:, S * t:S * t + S]
            step(V.tensor_scalar(d, psum[2][:, 0:S], poscol[:, t:t + 1], None, ALU.subtract))
            step(V.scalar_tensor_tensor(d, d, -1.0, d, ALU.mult, ALU.max))
            ang, k = square[:, 0:half], square[:, 512:512 + half]
            step(V.tensor_scalar(ang, con[:, C_INV:C_INV + half], poscol[:, t:t + 1], None, ALU.mult))
            for i, turns in enumerate((0.25, 0.0)):
                r = trig[:, i, t, :]
                step(V.tensor_scalar(k, ang, 1 / two_pi, turns, ALU.mult, ALU.add))
                step(V.tensor_scalar(k, k, MAGIC, None, ALU.add))
                step(V.tensor_scalar(k, k, MAGIC, None, ALU.subtract))
                step(V.scalar_tensor_tensor(r, k, -c1, ang, ALU.mult, ALU.add))
                step(V.scalar_tensor_tensor(r, k, -c2, r, ALU.mult, ALU.add))
                step(V.scalar_tensor_tensor(r, k, -c3, r, ALU.mult, ALU.add))
                if turns:
                    step(V.tensor_scalar(r, r, np.pi / 2, None, ALU.add))
                step(V.tensor_scalar(r, r, 3.1415925, -3.1415925, ALU.min, ALU.max))
        V.sem_inc(setup_v, 1)

        for l in range(2):
            w = l * L1
            rmod = 0 if l == 0 else raw_of(L1) + AHEAD
            cols = (0, 1, None, 2, 3, None)
            banks = (0, 1, None, 6, 7, None)

            def store_mod(s):
                if cols[s] is None:
                    return
                dve.wait_ge(mod_reduced, 6 * l + s + 1)
                src = psum[banks[s]][:, 0:KD]
                if s in (1, 4):
                    g0 = (V_G1, V_G2)[s // 4] + KD * l
                    step(V.scalar_tensor_tensor(modc[:, cols[s], :], src, 1.0, vec[:, g0:g0 + KD], ALU.add, ALU.mult))
                else:
                    step(V.tensor_copy(modc[:, cols[s], :], src))

            if l == 0:
                dve.wait_ge(setup_a, 1)
            for s in range(6):
                g = 6 * l + s
                dve.wait_ge(bias_row, 16 * (g + 1))
                for q in range(4):
                    r = rmod + 4 * s + q
                    dve.wait_ge(arrived[r % RAW], 16 * (r // RAW + 1))
                    for i in range(2):
                        k = 2 * q + i
                        step(V.scalar_tensor_tensor(modsum[:, g % 2, :], raw[r % RAW][:, D * i:D * i + D],
                                                    vec[:, V_C + k:V_C + k + 1], modsum[:, g % 2, :], ALU.mult, ALU.add))
                    V.sem_inc(raw_used, 1)
                V.sem_inc(mod_summed, 1)
                if s:
                    store_mod(s - 1)
            norm(2 * l, lambda k: modc[:, 1, k:k + 1], lambda k: modc[:, 0, k:k + 1])
            for j in range(N_IN1):
                rest_to(w + j + AHEAD)
            w += N_IN1
            take_squares()
            step(means([(0, 2, QL), (2, 2, KVL), (4, 2, ROPE)]))
            V.sem_inc(ms_ready, 1)
            V.sem_inc(squares_used, 1)
            refine(6)
            for t in range(TT):
                V.tensor_scalar(nat[:, t, 1536:1792], nat[:, t, 1536:1792], stat[:, 1, t:t + 1], None, ALU.mult)
                V.tensor_scalar(nat[:, t, 1792:1920], nat[:, t, 1792:1920], stat[:, 1, 2 + t:3 + t], None, ALU.mult)
                step(V.tensor_scalar(nat[:, t, 1920:1952], nat[:, t, 1920:1952], stat[:, 1, 4 + t:5 + t], None, ALU.mult))
            V.sem_inc(lat_norm, 1)
            heads_norm(l)
            dve.wait_ge(lat_turned, l + 1)
            for i in range(3):
                src = psum[4][:, S * i:S * i + S] if i < 2 else psum[5][:, 0:S]
                g = V_CQ + 2 * l + i if i < 2 else V_CKV + l
                ins = V.tensor_scalar(latent[:, S * i:S * i + S], src, vec[:, g:g + 1], None, ALU.mult)
            ins.then_inc(lat_float, 1)
            dve.wait_ge(lat_high, l + 1)
            V.tensor_tensor(latlo, latent, lathi.bitcast(F32), ALU.subtract).then_inc(lat_low, 1)
            rest_to(w + AHEAD - 1)
            rest_to(w + AHEAD)
            dve.wait_ge(used, w + 2)
            for t in range(TT):
                for i in range(2):
                    ins = V.tensor_copy(kvup[:, t, 512 * i:512 * i + 512], psum[2 * t + i][:, :])
            ins.then_inc(kvup_out, 1)
            rest_to(w + 1 + AHEAD)
            for t in range(TT):
                take_squares()
                v = square[:, 0:QUP].rearrange("p (h d) -> p h d", d=DH + ROPE)
                V.tensor_reduce(stat[:, 2, 8 * t:8 * t + 8], v[:, :, 0:DH], AX.X, ALU.add)
                V.tensor_reduce(stat[:, 2, 16 + 8 * t:24 + 8 * t], v[:, :, DH:DH + ROPE], AX.X, ALU.add) \
                    .then_inc(squares_used, 1)
            for t in range(TT):
                take_squares()
                V.tensor_reduce(stat[:, 2, 32 + 8 * t:40 + 8 * t], square[:, 0:512].rearrange("p (h d) -> p h d", d=DH),
                                AX.X, ALU.add).then_inc(squares_used, 1)
            dve.wait_ge(squares_used, sqs[0])
            means([(0, 16, DH), (16, 16, ROPE), (32, 16, DH)]).then_inc(ms_ready, 1)
            refine(48)
            for t in range(TT):
                v = nat[:, t, 0:QUP].rearrange("p (h d) -> p h d", d=DH + ROPE)
                k = kvup[:, t, :].rearrange("p (h d) -> p h d", d=P)[:, :, 0:DH]

                def rs(c, n):
                    return stat[:, 1, c + 8 * t:c + 8 * t + 8].unsqueeze(2).to_broadcast([P, H, n])

                V.tensor_tensor(qn_nat[:, t, :].rearrange("p (h d) -> p h d", d=DH), v[:, :, 0:DH], rs(0, DH), ALU.mult)
                V.tensor_tensor(v[:, :, DH:DH + ROPE], v[:, :, DH:DH + ROPE], rs(16, ROPE), ALU.mult)
                step(V.tensor_tensor(pturn[:, t, :].rearrange("p (h d) -> p h d", d=DH), k, rs(32, DH), ALU.mult))
                g = grope[:, 0, l, :].unsqueeze(1).to_broadcast([P, H, ROPE])
                V.tensor_tensor(v[:, :, DH:DH + ROPE], v[:, :, DH:DH + ROPE], g, ALU.mult)
                kr = nat[:, t, 1920:1952]
                step(V.tensor_tensor(kr, kr, grope[:, 1, l, :], ALU.mult))
            if l == 0:
                dve.wait_ge(setup_a, 2)
            for t in range(TT):
                v = nat[:, t, 0:QUP].rearrange("p (h d) -> p h d", d=DH + ROPE)
                kr = nat[:, t, 1920:1952]
                for heads, x1, x2, dst in (
                    (H, v[:, :, DH:DH + half], v[:, :, DH + half:DH + ROPE],
                     nat[:, t, 1536:1792].rearrange("p (h d) -> p h d", d=ROPE)),
                    (4, kr[:, 0:half].unsqueeze(1).to_broadcast([P, 4, half]),
                     kr[:, half:ROPE].unsqueeze(1).to_broadcast([P, 4, half]),
                     nat[:, t, 1792:1920].rearrange("p (h d) -> p h d", d=ROPE)),
                ):
                    cos, sin = (trig[:, i, t, :].unsqueeze(1).to_broadcast([P, heads, half]) for i in range(2))
                    ra, rb, rc, rd = (rtmp[:, i // 2, 128 * (i % 2):128 * (i % 2) + heads * half]
                                      .rearrange("p (h d) -> p h d", d=half) for i in range(4))
                    V.tensor_tensor(ra, x1, cos, ALU.mult)
                    V.tensor_tensor(rb, x2, sin, ALU.mult)
                    V.tensor_tensor(rc, x2, cos, ALU.mult)
                    step(V.tensor_tensor(rd, x1, sin, ALU.mult))
                    V.tensor_tensor(dst[:, :, 0:half], ra, rb, ALU.subtract)
                    step(V.tensor_tensor(dst[:, :, half:ROPE], rc, rd, ALU.add))
            V.sem_inc(mla_norm, 1)
            dve.wait_ge(mla_turned, 6 * l + 5)
            V.tensor_copy(qrT, psum[0][:, :].rearrange("p (a s) -> p a s", s=S)).then_inc(mla_out_v, 1)
            dve.wait_ge(mla_turned, 6 * l + 6)
            V.tensor_copy(krT, psum[1][:, 0:S]).then_inc(mla_out_v, 1)

            g0 = 16 * l
            dilated_max(g0, l, 0)
            for h in range(H):
                if h + 1 < H:
                    dilated_max(g0 + h + 1, l, h + 1)
                turn_store(g0 + h, 2 * S)
            store_group(l, 0)
            scale = float(DH + ROPE) ** -0.5
            plain_max(g0 + H, scale)
            for h in range(H, 2 * H):
                if h + 1 < 2 * H:
                    plain_max(g0 + h + 1, scale)
                turn_store(g0 + h, 2 * S)
            store_group(l, 1)
            turn_o(l)
            w += 2
            for j in range(N_OUT):
                rest_to(w + j + AHEAD)
                if j % 2:
                    dve.wait_ge(used, w + j + 1)
                    for t in range(TT):
                        ins = add_to_x(4 + 2 * (j // 2) + t, t, j // 2, 0)
                        if t == 0:
                            step(ins)
                    ins.then_inc(x_mixed, 1)
            w += N_OUT
            dve.wait_ge(x_mixed, 2 * l + 2)
            norm(2 * l + 1, lambda k: modc[:, 3, k:k + 1], lambda k: modc[:, 2, k:k + 1])

            def squares_of(b, slot, it=None):
                dve.wait_ge(f_one[l], loop(b + 1, it, 3))
                if b >= 3:
                    dve.wait_ge(f_hi[l], loop(b - 2, it, 3))
                V.tensor_tensor(relu[:, 1, slot, :], relu[:, 0, slot, :], relu[:, 0, slot, :], ALU.mult) \
                    .then_inc(f_two[l], 1)

            def low_block(b, slot, it=None):
                dve.wait_ge(f_hi[l], loop(b + 1, it, 3))
                V.tensor_tensor(actlo[:, slot, :], relu[:, 1, slot, :], acthi[:, slot, :].bitcast(F32), ALU.subtract) \
                    .then_inc(f_lo[l], 1)

            rest_to(w + 2)
            squares_of(0, 0)
            low_block(0, 0)
            for j in range(3):
                rest_to(w + 3 + 2 * j)
                squares_of(j + 1, (j + 1) % 3)
                rest_to(w + 4 + 2 * j)
                low_block(j + 1, (j + 1) % 3)
            with dve.Fori(0, 4) as it:
                for j in range(3, 6):
                    rest(w + 3 + 2 * j, it)
                    squares_of(j + 1, (j + 1) % 3, it)
                    rest(w + 4 + 2 * j, it)
                    low_block(j + 1, (j + 1) % 3, it)
            low[0] = w + N_MLP + 1
            rest_to(w + N_MLP - 1 + AHEAD)
            dve.wait_ge(used, w + N_MLP)
            for i in range(4):
                ins = add_to_x(4 + i, i // 2, i % 2, 1)
                if i < 3:
                    step(ins)
            ins.then_inc(x_done, 1)
            dve.wait_ge(x_done, l + 1)

        for l in range(2):
            w = (W_B2, W_L3)[l]
            n = 4 + 2 * l
            norm(n, lambda k: vec[:, V_G3 + KD * l + k:V_G3 + KD * l + k + 1], None)
            for j in range(N_NAT2):
                rest_to(w + j + AHEAD)
            w += N_NAT2
            dve.wait_ge(f_logit, l + 1)
            z = psum[3][:, 0:TT * H]
            step(V.tensor_scalar(forget[:, 0, :], z, -1.0, None, ALU.mult))
            V.tensor_tensor(forget[:, 1, :], z, forget[:, 0, :], ALU.max).then_inc(f_abs, 1)
            for j in range(N_TURN2):
                rest_to(w + j + AHEAD)
            w += N_TURN2
            dve.wait_ge(f_tail, l + 1)
            V.scalar_tensor_tensor(forget[:, 2, :], forget[:, 0, :], 0.0, forget[:, 1, :], ALU.max, ALU.add) \
                .then_inc(f_cost, 1)
            heads_norm(2 + l)
            dve.wait_ge(small_in, 80)
            g0 = 32 + 16 * l

            def softplus(h):
                g = g0 + h
                pv = probs[:, g % 2, 0:384]
                dve.wait_ge(sb_tail, H * l + h + 1)
                step(V.scalar_tensor_tensor(pv, psum[g % 2][:, 0:384], 0.0, pv, ALU.max, ALU.add))
                V.tensor_tensor(pv, pv, con2[:, C_SBM:C_SBM + 384], ALU.mult).then_inc(sb_soft, 1)

            softplus(0)
            for h in range(H):
                if h + 1 < H:
                    softplus(h + 1)
                g = g0 + h
                dve.wait_ge(sb_sum, H * l + h + 1)
                V.scalar_tensor_tensor(probs[:, g % 2, 0:384], psum[g % 2][:, 0:384], 0.0, con2[:, C_SBN:C_SBN + 384],
                                       ALU.min, ALU.add).then_inc(sb_log, 1)
            store_group(2 + l, 0, divide=False)
            g0 += H
            adds = [(P, con2[:, C_CAUS + P:C_CAUS + S]), (S, con2[:, C_CAUS:C_CAUS + S])]
            added_max(g0, adds)
            for h in range(H):
                if h + 1 < H:
                    added_max(g0 + h + 1, adds)
                turn_store(g0 + h, 384)
            store_group(2 + l, 1)
            turn_o(2 + l)
            for j in range(N_WO):
                rest_to(w + j + AHEAD)
            for q in range(8):
                dve.wait_ge(used, w + q // 2 + 1)
                v = gates[:, 512 * q:512 * q + 512]
                V.tensor_tensor(v, v, psum[q][:, :], ALU.mult).then_inc(vstep, 1)
                steps[0] += 1
            dve.wait_ge(vstep, steps[0])
            for q in range(4):
                v = gates[:, 512 * q:512 * q + 512]
                V.tensor_tensor(v, v, gates[:, 2048 + 512 * q:2560 + 512 * q], ALU.add).then_inc(gated, 1)
            for q in range(4):
                dve.wait_ge(z_high, 4 * l + q + 1)
                V.tensor_tensor(hlo[:, 2 * q:2 * q + 2, :],
                                gates[:, 512 * q:512 * q + 512].rearrange("p (a s) -> p a s", s=S),
                                hhi[:, 2 * q:2 * q + 2, :].bitcast(F32), ALU.subtract).then_inc(z_low, 1)
            w += N_WO
            for j in range(N_OUT):
                rest_to(w + j + AHEAD)
                if j % 2:
                    dve.wait_ge(used, w + j + 1)
                    for t in range(TT):
                        ins = add_to_x(4 + 2 * (j // 2) + t, t, j // 2, None)
                    ins.then_inc(x_mixed, 1)
            w += N_OUT
            dve.wait_ge(x_mixed, 2 * (2 + l) + 2)
            norm(n + 1, lambda k: vec[:, V_G4 + KD * l + k:V_G4 + KD * l + k + 1], None)

            def product(f, w, b, n, it=None, per=0, wper=0, e=None):
                dve.wait_ge(f_one[f], loop(b + 1, it, per))
                dve.wait_ge(used, loop(w, it, wper))
                if b >= 2:
                    dve.wait_ge(f_hi[f], loop(b - 1, it, per))
                dst = silu[:, 1, b % 2, 0:n]
                ins = V.tensor_tensor(dst, silu[:, 0, b % 2, 0:n], psum[2 + b % 2][:, 0:n], ALU.mult)
                if e is not None:
                    ins.then_inc(e_comb, 1)
                    dve.wait_ge(e_comb, loop(b + 1, it, per))
                    v = dst.rearrange("p (f s) -> p f s", s=S)
                    ins = V.tensor_tensor(v, v, combine[:, bass.ds(e, 1), :].to_broadcast([P, n // S, S]), ALU.mult)
                ins.then_inc(f_two[f], 1)

            def low_block2(f, b, n, it=None, per=0):
                dve.wait_ge(f_hi[f], loop(b + 1, it, per))
                V.tensor_tensor(actlo[:, b % 2, 0:n], silu[:, 1, b % 2, 0:n], acthi[:, b % 2, 0:n].bitcast(F32),
                                ALU.subtract).then_inc(f_lo[f], 1)

            if l == 0:
                rest_to(w + 2)
                rest_to(w + 3)
                product(2, w + 2, 0, 512)
                low_block2(2, 0, 512)
                for j in range(2):
                    m = w + 2 + 3 * j
                    rest_to(m + 3)
                    product(2, m + 2, j + 1, 512)
                    rest_to(m + 4)
                    low_block2(2, j + 1, 512)
                with dve.Fori(0, 4) as it:
                    for j in range(2, 4):
                        m = w + 2 + 3 * j
                        rest(m + 2, it)
                        rest(m + 3, it)
                        product(2, m + 2, j + 1, 512, it, 2, RAW)
                        rest(m + 4, it)
                        low_block2(2, j + 1, 512, it, 2)
                low[0] = w + N_DENSE + 1
                rest_to(w + N_DENSE - 1 + AHEAD)
                dve.wait_ge(used, w + N_DENSE)
                for i in range(4):
                    ins = add_to_x(4 + i, i // 2, i % 2, None)
                ins.then_inc(x_done, 1)
                dve.wait_ge(x_done, 3)
            else:
                dve.wait_ge(r_logit, 1)
                lg = route[:, 0:16]
                step(V.tensor_copy(lg, psum[4][:, 0:16]))
                mx = route[:, 32:34]
                step(V.tensor_reduce(mx, lg.rearrange("p (t e) -> p t e", e=NE), AX.X, ALU.max))
                V.tensor_scalar(mx, mx, -1.0, None, ALU.mult).then_inc(r_max, 1)
                for t in range(TT):
                    v = lg[:, 8 * t:8 * t + 8]
                    other = v.unsqueeze(1).to_broadcast([P, NE, NE])
                    own = v.unsqueeze(2).to_broadcast([P, NE, NE])
                    big, same = (route[:, c:c + 64].rearrange("p (e j) -> p e j", j=NE) for c in (64, 128))
                    V.tensor_tensor(big, other, own, ALU.is_gt)
                    step(V.tensor_tensor(same, other, own, ALU.is_equal))
                    step(V.tensor_tensor(same, same, con2[:, C_TIE:C_TIE + 64].rearrange("p (e j) -> p e j", j=NE), ALU.mult))
                    step(V.tensor_tensor(big, big, same, ALU.add))
                    step(V.tensor_reduce(route[:, 40 + 8 * t:48 + 8 * t], big, AX.X, ALU.add))
                chosen = route[:, 40:56]
                step(V.tensor_scalar(chosen, chosen, 2.0, None, ALU.is_lt))
                dve.wait_ge(r_exp, 1)
                ex = route[:, 16:32]
                step(V.tensor_tensor(ex, ex, chosen, ALU.mult))
                step(V.tensor_reduce(route[:, 34:36], ex.rearrange("p (t e) -> p t e", e=NE), AX.X, ALU.add))
                step(V.reciprocal(route[:, 34:36], route[:, 34:36]))
                for t in range(TT):
                    ins = V.tensor_scalar(ex[:, 8 * t:8 * t + 8], ex[:, 8 * t:8 * t + 8], route[:, 34 + t:35 + t], None, ALU.mult)
                ins.then_inc(r_comb, 1)
                dve.wait_ge(r_out, 1)

                def expert(it, last):
                    def rest_ahead(m):
                        if not last or m < w + EXPERT:
                            rest(m, it, EXPERT)

                    rest_ahead(w + 2)
                    rest_ahead(w + 3)
                    product(3, w + 2, 0, 512, it, 6, EXPERT, it)
                    low_block2(3, 0, 512, it, 6)
                    for b in range(1, 6):
                        m = w + 3 * b - 1
                        n = 512 if b < 5 else 256
                        rest_ahead(m + 2)
                        rest_ahead(m + 3)
                        product(3, m + 2, b, n, it, 6, EXPERT, it)
                        rest_ahead(m + 4)
                        low_block2(3, b, n, it, 6)
                    rest_ahead(w + EXPERT + 1)
                    dve.wait_ge(used, loop(w + EXPERT, it, EXPERT))
                    for i in range(4):
                        ins = add_to_x(4 + i, i // 2, i % 2, None)
                    ins.then_inc(x_done, 1)
                    dve.wait_ge(x_done, loop(4, it, 1))

                with dve.Fori(0, NE - 1) as it:
                    expert(it, False)
                expert(NE - 1, True)

    @block.tensor
    def _(pe):
        T = nc.tensor

        def piece(w, it=None, per=RAW):
            pe.wait_ge(raw_used, loop(raw_of(w) + 1, it, per))
            return whi[w % SPLIT], wlo[w % SPLIT]

        def passes(out, pairs, start, stop):
            for i, (lhsT, rhs) in enumerate(pairs):
                ins = T.matmul(out, lhsT, rhs, start=start and i == 0, stop=stop and i == len(pairs) - 1)
            return ins

        def natural(w, k0, n, out, first, last, hi=hhi, lo=hlo, kt=4, kbase=0):
            wh, wl = piece(w)
            for t in range(TT):
                for k in range(kt):
                    c = slice(k * n, k * n + n)
                    hs, ls = hi[:, k0 + k, P * t:P * t + P], lo[:, k0 + k, P * t:P * t + P]
                    ins = passes(out[t][:, 0:n], [(hs, wh[:, c]), (hs, wl[:, c]), (ls, wh[:, c])],
                                 first and k == 0, last and k == kt - 1)
            ins.then_inc(used, 1)

        def turned_product(w, n, kt, tiles, k0=0, it=None, per=RAW):
            wh, wl = piece(w, it, per)
            for f, (bank, c0) in enumerate(tiles):
                for k in range(kt):
                    c = slice(k * n + P * f, k * n + P * f + P)
                    ins = passes(bank[:, c0:c0 + S], [(wh[:, c], hhi[:, k0 + k, :]), (wh[:, c], hlo[:, k0 + k, :]),
                                                      (wl[:, c], hhi[:, k0 + k, :])], k == 0, k == kt - 1)
            ins.then_inc(used, 1)

        def down_product(w, slot, kt, first, last, it=None, per=RAW):
            wh, wl = piece(w, it, per)
            for t in range(TT):
                for k in range(kt):
                    c = slice(S * k + P * t, S * k + P * t + P)
                    hs, ls = acthi[:, slot, c], actlo[:, slot, c]
                    for half in range(2):
                        d = slice(D * k + 512 * half, D * k + 512 * half + 512)
                        ins = passes(psum[4 + 2 * t + half][:, :], [(hs, wh[:, d]), (hs, wl[:, d]), (ls, wh[:, d])],
                                     first and k == 0, last and k == kt - 1)
            ins.then_inc(used, 1)

        def turn(out, src):
            return T.transpose(out, src, ident)

        def turn_h(n):
            pe.wait_ge(xn_ready, n + 1)
            for b in range(4):
                for i in range(2):
                    for t in range(TT):
                        k = 2 * b + i
                        ins = turn(psum[b][:, S * i + P * t:S * i + P * t + P], nat[:, t, P * k:P * k + P])
                ins.then_inc(h_turned, 1)
            pe.wait_ge(h_low, 4 * n + 4)

        def turn_qk(l):
            pe.wait_ge(qk_norm, l + 1)
            for b in range(4):
                for i in range(2):
                    for t in range(TT):
                        c = 512 * (b // 2) + P * (2 * (b % 2) + i)
                        ins = turn(psum[b][:, S * i + P * t:S * i + P * t + P], nat[:, t, c:c + P])
                ins.then_inc(qk_turned, 1)

        def bank_free(g):
            if g >= 2:
                pe.wait_ge(probs_ready, g - 1)

        def rows(t, h):
            return t[DH * (h % 2):DH * (h % 2) + DH, h // 2, :]

        def score_dilated(g, h):
            bank_free(g)
            q, k = rows(qdT, h), rows(kdT, h)
            for t in range(TT):
                ins = T.matmul(psum[g % 2][:, S * t:S * t + S], q[:, P * t:P * t + P], k, start=True, stop=True)
            ins.then_inc(scores, 1)

        def score_mla(g, h):
            bank_free(g)
            q, k = rows(qnT, h), rows(knT, h)
            r = slice(ROPE * (h % 4), ROPE * (h % 4) + ROPE)
            for t in range(TT):
                o = psum[g % 2][:, S * t:S * t + S]
                T.matmul(o, q[:, P * t:P * t + P], k, start=True, stop=False)
                ins = T.matmul(o, qrT[r, h // 4, P * t:P * t + P], krT[r, :], start=False, stop=True)
            ins.then_inc(scores, 1)

        def score_forget(g, h):
            bank_free(g)
            q, k = rows(fqT, h), rows(fkT, h)
            cost = [forget[:, 2, 8 * t + h:8 * t + h + 1].to_broadcast([P, P]) for t in range(TT)]
            tri = con2[:, C_TRI:C_TRI + S]
            b = psum[g % 2]
            T.matmul(b[:, 0:P], q[:, 0:P], k[:, 0:P], start=True, stop=False)
            T.matmul(b[:, 0:P], cost[0], tri[:, 0:P], start=False, stop=True)
            T.matmul(b[:, S:2 * S], q[:, P:S], k, start=True, stop=False)
            T.matmul(b[:, S:2 * S], cost[0], tri, start=False, stop=True)
            ins = T.matmul(b[:, S + P:2 * S], cost[1], tri[:, 0:P], start=False, stop=True, skip_group_check=True)
            ins.then_inc(scores, 1)

        def score_stick(g, h):
            bank_free(g)
            q, k = rows(sqT, h), rows(skT, h)
            T.matmul(psum[g % 2][:, 0:S], k[:, 0:P], q, start=True, stop=True)
            T.matmul(psum[g % 2][:, S:384], k[:, P:S], q[:, P:S], start=False, stop=True,
                     skip_group_check=True).then_inc(scores, 1)

        def sum_stick(g, i):
            pe.wait_ge(sb_soft, i + 1)
            b, pv, ntri = psum[g % 2], probs[:, g % 2, :], con2[:, C_NTRI:C_NTRI + P]
            T.matmul(b[:, 0:S], ntri, pv[:, 0:S], start=False, stop=True, skip_group_check=True)
            T.matmul(b[:, P:S], minus[:, :], pv[:, S:384], start=False, stop=True, skip_group_check=True)
            T.matmul(b[:, S:384], ntri, pv[:, S:384], start=False, stop=True, skip_group_check=True).then_inc(sb_sum, 1)

        FULL = ((0, 0, 0), (1, 0, P), (0, 1, S), (1, 1, S + P))
        CAUSAL = ((0, 0, 0), (1, 0, P), (1, 1, S))

        def turn_probs(g, blocks):
            pe.wait_ge(probs_ready, g + 1)
            if softmax_of(g) >= 2:
                pe.wait_ge(pt_ready, softmax_of(g) - 1)
            for qt, kt, c in blocks:
                ins = turn(psum[2 + g % 2][:, c:c + P], probs[:, g % 2, S * qt + P * kt:S * qt + P * kt + P])
            ins.then_inc(turned, 1)

        def weigh(g, blocks, v, plain=False):
            if plain:
                pe.wait_ge(probs_ready, g + 1)
            else:
                pe.wait_ge(pt_ready, softmax_of(g) + 1)
            if g % H == 0 and g:
                pe.wait_ge(attn_out, g // H)
            h = g % H
            for qt in range(TT):
                own = [b for b in blocks if b[0] == qt]
                for i, (_, kt, c) in enumerate(own):
                    ins = T.matmul(psum[4 + qt][:, DH * h:DH * h + DH], pturn[:, g % 2, c:c + P], v(kt, h),
                                   start=i == 0, stop=i == len(own) - 1)
            ins.then_inc(values, 1)

        def heads(g0, score, blocks, v):
            score(g0, 0)
            for h in range(H):
                if h + 1 < H:
                    score(g0 + h + 1, h + 1)
                turn_probs(g0 + h, blocks)
                if h:
                    weigh(g0 + h - 1, blocks, v)
            weigh(g0 + H - 1, blocks, v)

        def turn_o(l):
            pe.wait_ge(attn_out, 2 * l + 2)
            for b in range(4):
                for i in range(2):
                    for t in range(TT):
                        k = 2 * b + i
                        ins = turn(psum[b][:, S * i + P * t:S * i + P * t + P], nat[:, t, P * k:P * k + P])
                ins.then_inc(o_turned, 1)
            pe.wait_ge(o_low, 4 * l + 4)

        def out_product(w):
            for j in range(N_OUT):
                natural(w + j, 4 * (j % 2), 512, [psum[4 + 2 * (j // 2) + t] for t in range(TT)], j % 2 == 0, j % 2 == 1)

        pe.wait_ge(loaded, 16 * N_LOADS)
        pe.wait_ge(ones_set, 2)
        T.transpose(psum[0][:, 0:P], stage, ident).then_inc(setup_t, 1)
        pe.wait_ge(setup_v, 2)
        for t in range(TT):
            T.matmul(psum[1][:, t:t + 1], pos_row[:, P * t:P * t + P], ones[0:1, 0:1], start=True, stop=True)
        T.matmul(psum[1][:, P:2 * P], ones[0:1, :], gain_row, start=True, stop=True)
        T.matmul(psum[2][:, 0:S], ones[0:1, :], pos_row, start=True, stop=True).then_inc(setup_t, 1)
        pe.wait_ge(setup_v, SETUP_V)

        for l in range(2):
            w = l * L1
            cols, banks = (0, 1, None, 2, 3, None), (0, 1, None, 6, 7, None)
            for s in range(6):
                g = 6 * l + s
                pe.wait_ge(mod_summed, g + 1)
                sums = modsum[:, g % 2, :]
                if cols[s] is None:
                    for half in range(2):
                        ins = T.matmul(psum[(2 if s == 2 else 4) + half][:, :], ones[:, :], sums[:, 512 * half:512 * half + 512],
                                       start=True, stop=True)
                else:
                    for k in range(KD):
                        ins = T.matmul(psum[banks[s]][:, k:k + 1], sums[:, P * k:P * k + P], ones[:, 0:1],
                                       start=True, stop=True)
                ins.then_inc(mod_reduced, 1)
            pe.wait_ge(gt_ready, 2 * l + 2)
            turn_h(2 * l)
            for c in range(4):
                if c >= 2:
                    pe.wait_ge(proj_out, 4 * l + c - 1)
                n = 512 if c < 3 else W_IN - 1536
                for half in range(2):
                    natural(w + 2 * c + half, 4 * half, n, [psum[4 + 2 * (c % 2) + t] for t in range(TT)],
                            half == 0, half == 1)
            w += N_IN1
            pe.wait_ge(lat_norm, l + 1)
            for t in range(TT):
                for i in range(2):
                    turn(psum[4][:, S * i + P * t:S * i + P * t + P], nat[:, t, 1536 + P * i:1664 + P * i])
                ins = turn(psum[5][:, P * t:P * t + P], nat[:, t, 1792:1920])
            ins.then_inc(lat_turned, 1)
            turn_qk(l)
            pe.wait_ge(lat_low, l + 1)
            lh, ll = (v.rearrange("p (k s) -> p k s", s=S) for v in (lathi, latlo))
            wh, wl = piece(w)
            for t in range(TT):
                for c0, n, bank in ((0, 512, 6 - 2 * t), (512, 256, 7 - 2 * t)):
                    for k in range(2):
                        c = slice(QUP * k + c0, QUP * k + c0 + n)
                        hs, ls = lh[:, k, P * t:P * t + P], ll[:, k, P * t:P * t + P]
                        ins = passes(psum[bank][:, 0:n], [(hs, wh[:, c]), (hs, wl[:, c]), (ls, wh[:, c])], k == 0, k == 1)
            ins.then_inc(used, 1)
            pe.wait_ge(qk_out, 4 * l + 4)
            wh, wl = piece(w + 1)
            for t in range(TT):
                for i in range(2):
                    c = slice(512 * i, 512 * i + 512)
                    hs, ls = lh[:, 2, P * t:P * t + P], ll[:, 2, P * t:P * t + P]
                    ins = passes(psum[2 * t + i][:, :], [(hs, wh[:, c]), (hs, wl[:, c]), (ls, wh[:, c])], True, True)
            ins.then_inc(used, 1)
            w += 2
            pe.wait_ge(mla_norm, l + 1)
            for b in range(4):
                for i in range(2):
                    pair = 2 * (b % 2) + i
                    for t in range(TT):
                        v = (qn_nat, pturn)[b // 2]
                        ins = turn(psum[4 + b][:, S * i + P * t:S * i + P * t + P], v[:, t, P * pair:P * pair + P])
                ins.then_inc(mla_turned, 1)
            for i in range(2):
                for t in range(TT):
                    ins = turn(psum[0][:, S * i + P * t:S * i + P * t + P], nat[:, t, 1536 + P * i:1664 + P * i])
            ins.then_inc(mla_turned, 1)
            for t in range(TT):
                ins = turn(psum[1][:, P * t:P * t + P], nat[:, t, 1792:1920])
            ins.then_inc(mla_turned, 1)
            pe.wait_ge(mla_out_v, 2 * l + 2)
            pe.wait_ge(mla_out_a, 4 * l + 4)
            heads(16 * l, score_dilated, FULL, lambda kt, h: nat[:, kt, 1024 + DH * h:1024 + DH * h + DH])
            heads(16 * l + H, score_mla, FULL, lambda kt, h: kvup[:, kt, P * h + DH:P * h + P])
            turn_o(l)
            out_product(w)
            w += N_OUT
            turn_h(2 * l + 1)

            def up_block(b, slot, it=None):
                m = w + 2 * b - 1 if b else w
                if b >= 3:
                    pe.wait_ge(f_one[l], loop(b - 2, it, 3))
                turned_product(m, S, KD, [(psum[slot], 0), (psum[slot], S)], it=it)

            def down_block(b, slot, first, last, it=None):
                pe.wait_ge(f_lo[l], loop(b + 1, it, 3))
                down_product(w + 2 + 2 * b if b < F1 // 256 - 1 else w + N_MLP - 1, slot, 2, first, last, it)

            up_block(0, 0)
            for j in range(3):
                up_block(j + 1, (j + 1) % 3)
                down_block(j, j % 3, j == 0, False)
            with pe.Fori(0, 4) as it:
                for j in range(3, 6):
                    up_block(j + 1, (j + 1) % 3, it)
                    down_block(j, j % 3, False, False, it)
            down_block(F1 // 256 - 1, 0, False, True)

        for l in range(2):
            w = (W_B2, W_L3)[l]
            n = 4 + 2 * l
            turn_h(n)
            for c in range(4):
                if c >= 2:
                    pe.wait_ge(proj_out, 8 + 4 * l + c - 1)
                for half in range(2):
                    natural(w + 2 * c + half, 4 * half, 512, [psum[4 + 2 * (c % 2) + t] for t in range(TT)],
                            half == 0, half == 1)
            w += N_NAT2

            def small_product(slot, bank, bias_):
                for t in range(TT):
                    o = bank[:, 8 * t:8 * t + 8]
                    if bias_ is not None:
                        T.matmul(o, ones[0:1, :], bias_, start=True, stop=False)
                    for k in range(KD):
                        for i, part in enumerate((hhi, hlo)):
                            ins = T.matmul(o, part[:, k, P * t:P * t + P].bitcast(F32),
                                           wsmall[:, slot, 8 * k:8 * k + 8],
                                           start=bias_ is None and k == 0 and i == 0, stop=k == KD - 1 and i == 1)
                return ins

            pe.wait_ge(small_in, 80)
            small_product(l, psum[3], small[0:1, 8 * l:8 * l + 8]).then_inc(f_logit, 1)
            for j in range(N_TURN2):
                if j == 3:
                    pe.wait_ge(f_abs, l + 1)
                if j >= 4:
                    pe.wait_ge(t2_out, N_TURN2 * l + j - 3)
                turned_product(w + j, S, KD, [(psum[j % 4], 0), (psum[j % 4], S)])
            pe.wait_ge(t2_out, N_TURN2 * (l + 1))
            turn_qk(2 + l)
            pe.wait_ge(qk_out, 4 * (2 + l) + 4)
            g0 = 32 + 16 * l

            def v_stick(kt, h):
                return nat[:, kt, 1536 + DH * h:1536 + DH * h + DH]

            score_stick(g0, 0)
            for h in range(H):
                if h + 1 < H:
                    score_stick(g0 + h + 1, h + 1)
                sum_stick(g0 + h, H * l + h)
                if h:
                    weigh(g0 + h - 1, CAUSAL, v_stick, plain=True)
            weigh(g0 + H - 1, CAUSAL, v_stick, plain=True)
            pe.wait_ge(f_cost, l + 1)
            heads(g0 + H, score_forget, CAUSAL, lambda kt, h: nat[:, kt, 1024 + DH * h:1024 + DH * h + DH])
            turn_o(2 + l)
            w += N_TURN2
            for j in range(N_WO):
                turned_product(w + j, 512, 4, [(psum[2 * j + i // 2], S * (i % 2)) for i in range(4)], k0=4 * (j // 2))
            w += N_WO
            pe.wait_ge(z_low, 4 * l + 4)
            out_product(w)
            w += N_OUT
            turn_h(n + 1)

            def gate_block(f, w, b, n, it=None, per=0, wper=0):
                if b >= 2:
                    pe.wait_ge(f_one[f], loop(b - 1, it, per))
                turned_product(w, n // 2 if n == 512 else P, KD, [(psum[b % 2], S * i) for i in range(n // S)], it=it, per=wper)

            def up_block2(f, w, b, n, it=None, per=0, wper=0):
                if b >= 2:
                    pe.wait_ge(f_two[f], loop(b - 1, it, per))
                turned_product(w, n // 2 if n == 512 else P, KD, [(psum[2 + b % 2], S * i) for i in range(n // S)], it=it, per=wper)

            def down_block2(f, w, b, kt, first, last, it=None, per=0, wper=0):
                pe.wait_ge(f_lo[f], loop(b + 1, it, per))
                down_product(w, b % 2, kt, first, last, it, wper)

            if l == 0:
                gate_block(2, w, 0, 512)
                up_block2(2, w + 1, 0, 512)
                for j in range(2):
                    m = w + 2 + 3 * j
                    gate_block(2, m, j + 1, 512)
                    up_block2(2, m + 1, j + 1, 512)
                    down_block2(2, m + 2, j, 2, j == 0, False)
                with pe.Fori(0, 4) as it:
                    for j in range(2, 4):
                        m = w + 2 + 3 * j
                        gate_block(2, m, j + 1, 512, it, 2, RAW)
                        up_block2(2, m + 1, j + 1, 512, it, 2, RAW)
                        down_block2(2, m + 2, j, 2, False, False, it, 2, RAW)
                down_block2(2, w + N_DENSE - 1, F2 // 256 - 1, 2, False, True)
            else:
                small_product(2, psum[4], None).then_inc(r_logit, 1)
                pe.wait_ge(r_comb, 1)
                for e in range(NE):
                    for t in range(TT):
                        c = 16 + 8 * t + e
                        ins = T.matmul(psum[e // 2][:, S * (e % 2) + P * t:S * (e % 2) + P * t + P],
                                       route[:, c:c + 1].to_broadcast([P, P]), ident, start=True, stop=True)
                ins.then_inc(r_spread, 1)
                pe.wait_ge(r_out, 1)
                with pe.Fori(0, NE) as it:
                    gate_block(3, w, 0, 512, it, 6, EXPERT)
                    up_block2(3, w + 1, 0, 512, it, 6, EXPERT)
                    pe.wait_ge(x_done, loop(3, it, 1))
                    for b in range(1, 6):
                        m = w + 3 * b - 1
                        n = 512 if b < 5 else 256
                        gate_block(3, m, b, n, it, 6, EXPERT)
                        up_block2(3, m + 1, b, n, it, 6, EXPERT)
                        down_block2(3, m + 2, b - 1, 2, b == 1, False, it, 6, EXPERT)
                    down_block2(3, w + EXPERT - 1, 5, 1, False, True, it, 6, EXPERT)


_INS = ["x", "c", "positions", "w_mod", "b_mod", "g_norm_mix", "w_in", "g_q_dil", "g_k_dil", "g_cq", "w_q_up",
        "g_ckv", "w_kv_up", "g_q_nope", "g_q_rope", "g_k_nope", "g_k_rope", "w_out", "g_norm_mlp", "w_mlp_in",
        "w_mlp_out", "g_mix_2", "w_in_2", "b_f_2", "b_gate_2", "g_q_2", "g_k_2", "w_o_sb_2", "w_o_fox_2",
        "w_out_2", "g_ffn_2", "w_gu_dense_2", "w_dn_dense_2", "w_router_2", "w_gu_exp_2", "w_dn_exp_2"]


def kernel(**inputs):
    import numpy as _np
    import concourse.bacc as _bacc
    from concourse import mybir as _mybir
    from concourse.bass_utils import run_bass_kernel_spmd as _run

    nc = _bacc.Bacc("TRN2", target_bir_lowering=False, num_devices=1)
    arrays, args = {}, {}
    for name in _INS:
        v = _np.ascontiguousarray(inputs[name])
        arrays[f"in_{name}_dram"] = v
        args[name] = nc.dram_tensor(f"in_{name}_dram", v.shape, _mybir.dt.from_np(v.dtype), kind="ExternalInput").ap()
    consts = []
    for i, v in enumerate(constants()):
        arrays[f"in_constants{i}_dram"] = v
        consts.append(nc.dram_tensor(f"in_constants{i}_dram", v.shape, F32, kind="ExternalInput").ap())
    out = nc.dram_tensor("out_0_dram", (1, S, D), F32, kind="ExternalOutput").ap()
    two_blocks_kernel(nc, args, consts, out)
    r = _run(nc, [arrays], core_ids=[0])
    return r.results[0]["out_0_dram"]
```

```python
from contextlib import ExitStack

import concourse.bass as bass
import numpy as np
from concourse import mybir

F32 = mybir.dt.float32
F32R = mybir.dt.float32r
I32 = mybir.dt.int32
ACT = mybir.ActivationFunctionType
ALU = mybir.AluOpType
AX = mybir.AxisListType

P = 128
S = 256
D = 1024
TT = S // P
KD = D // P
H = 8
DH = 64
ROPE = 32
QL, KVL = 256, 128
QUP = H * (DH + ROPE)
KVUP = H * 2 * DH
W_IN = 1952
F1 = 4096
F2 = 2816
NE, FE = 8, 1408
EPS = 1e-6
PIECE = 2048
RAW, SPLIT = 6, 3
AHEAD = 2
BIG = 1.0e30
LOWEST = -3.0e38
LN_EXP_SET = 6
MAGIC = 1.5 * 2.0**23

N_IN1, N_QUP, N_KVUP, N_OUT, N_MLP = 8, 1, 1, 4, 2 * (F1 // 256)
L1 = N_IN1 + N_QUP + N_KVUP + N_OUT + N_MLP
W_HEADS = N_IN1 + N_QUP + N_KVUP + AHEAD - 1
N_NAT2, N_TURN2, N_WO, N_DENSE = 8, 12, 4, 3 * (F2 // 256)
N_QK2 = 4
EXPERT = 18
W_B2 = 2 * L1
L2_MIX = N_NAT2 + N_TURN2 + N_WO + N_OUT
W_DENSE = W_B2 + L2_MIX
W_L3 = W_DENSE + N_DENSE
W_MOE = W_L3 + L2_MIX
W_END = W_MOE + NE * EXPERT


def stream():
    after = {(0, 0): -1, (0, 1): -1, (1, 0): W_HEADS, (1, 1): W_HEADS}
    for l in range(2):
        for s in range(2):
            after[l, 4 + s] = W_HEADS + l * L1
            after[l, 2 + s] = l * L1 + AHEAD + 4 * s
    sections = [(0, 0), (0, 1), (0, 2), (0, 3), (1, 0), (1, 1), (0, 4), (0, 5), (1, 2), (1, 3), (1, 4), (1, 5)]
    place, mod, r = {}, {}, 0
    for w in range(-1, W_END):
        if w >= 0:
            place[w] = r
            r += 1
        for l, s in sections:
            for q in range(4):
                if after[l, s] + (q if s in (2, 3) else 0) == w:
                    mod[l, s, q] = r
                    r += 1
    return place, mod, sections


PLACE, MOD_PLACE, SECTIONS = stream()


def raw_of(w):
    return PLACE[w]


C_ID = 0
C_LNM = C_ID + P
C_INV = C_LNM + TT * S
N_FIRST = C_INV + 16
C_CAUS = 0
C_SBM = C_CAUS + S
C_SBN = C_SBM + 384
C_NTRI = C_SBN + 384
C_TRI = C_NTRI + P
C_TIE = C_TRI + S
C_SLOT = C_TIE + 64
N_SECOND = C_SLOT + P

V_C, V_G1, V_G2, V_G3, V_G4 = 0, 8, 24, 40, 56
V_CQ, V_CKV, V_BG = 72, 76, 78
V_QD, V_KD, V_QN, V_KN, V_QF, V_KF = 110, 112, 114, 116, 118, 120
N_ROWS = 128
V_BM = N_ROWS
N_VEC = N_ROWS + 96
N_LOADS = 24
SETUP_V, SETUP_TRIG = 5, 6


def constants():
    first = np.zeros((P, N_FIRST), np.float32)
    c = np.zeros((P, N_SECOND), np.float32)
    p = np.arange(P)
    first[:, C_ID:C_ID + P] = np.eye(P)
    q, k = np.arange(S)[:, None], np.arange(S)[None, :]
    count = np.zeros((S, S))
    for window, dil in ((128, 1), (512, 4), (2048, 16)):
        count += ((k - q) % dil == 0) & (np.abs(k - q) <= window // 2)
    ln = np.where(count > 0, np.log(np.maximum(count, 1)), -BIG)
    first[:, C_LNM:C_LNM + TT * S] = ln.reshape(TT, P, S).transpose(1, 0, 2).reshape(P, TT * S)
    c[:, C_CAUS + P:C_CAUS + S] = np.where(p[None, :] <= p[:, None], 0, -BIG)
    before = (p[:, None] < p[None, :]).astype(np.float32)
    blocks = np.concatenate([before, np.ones((P, P)), before], 1)
    c[:, C_SBM:C_SBM + 384] = blocks
    c[:, C_SBN:C_SBN + 384] = (1 - blocks) * -BIG
    c[:, C_NTRI:C_NTRI + P] = -(p[:, None] >= p[None, :]).astype(np.float32)
    c[:, C_TRI:C_TRI + P] = p[:, None] <= p[None, :]
    c[:, C_TRI + P:C_TRI + S] = 1
    half = ROPE // 2
    first[:, C_INV:C_INV + half] = np.float32(10000.0) ** (-np.arange(half, dtype=np.float32) / half)
    e = np.arange(NE)
    c[:, C_TIE:C_TIE + 64] = (e[None, :] < e[:, None]).reshape(1, 64)
    c[:, C_SLOT:C_SLOT + P] = p[None, :]
    return first, c


def two_blocks_kernel(nc, a, consts, out):
    with ExitStack() as ctx:
        program(nc, ctx, a, consts, out)


def program(nc, ctx, a, consts, out):
    def sb(name, shape, dt=F32, into=ctx):
        return into.enter_context(nc.sbuf_tensor(name, shape, dt))

    def sem(name):
        return ctx.enter_context(nc.semaphore(name))

    raw = [sb(f"raw{i}", [P, PIECE]) for i in range(RAW)]
    whi_all = sb("w_high", [P, SPLIT, PIECE], F32R)
    wlo_all = sb("w_low", [P, SPLIT, PIECE], F32R)
    whi = [whi_all[:, i, :] for i in range(SPLIT)]
    wlo = [wlo_all[:, i, :] for i in range(SPLIT)]
    x = sb("x", [P, TT, D])
    hhi = sb("h_high", [P, KD, S], F32R)
    hlo = sb("h_low", [P, KD, S], F32R)
    acthi = sb("act_high", [P, 3, 512], F32R)
    actlo = sb("act_low", [P, 3, 512], F32R)
    nat = sb("natural", [P, TT, 2048])
    probs = sb("probs", [P, 2, 2 * S])
    pturn = sb("probs_turned", [P, 2, 2 * S])
    con = sb("constants", [P, N_FIRST])
    vec = sb("vector_columns", [P, N_VEC])
    ones = sb("ones", [P, P])
    minus = sb("minus_ones", [P, P])
    modc = sb("mod_columns", [P, 6, KD])
    ccol = sb("c_columns", [P, KD])
    stat = sb("statistics", [P, 4, 48])
    expsum = sb("exp_sums", [P, 2, TT * H])
    rowmax = sb("row_max", [P, 2, TT])
    negmax = sb("negative_max", [P, 2, TT])
    trig = sb("trig", [P, 2, TT, ROPE // 2])
    grope = sb("rope_gains", [P, 2, 2, ROPE])
    poscol = sb("position_columns", [P, TT])
    psum = [ctx.enter_context(nc.psum_tensor(f"bank{i}", [P, 512], F32)) for i in range(8)]

    first = ExitStack()
    ta = sb("turned1", [P, 4864 + 2048], into=first)
    bias = sb("dilated_bias", [P, TT * S], into=first)
    mod_sums = sb("mod_sums", [P, 2, 512], into=first)
    rtmp = sb("rope_products", [P, 2, TT * H * ROPE // 2], into=first)
    gtb = sb("gate_rows", [P, 2, D], into=first)
    dist = sb("distance", [P, TT * S], into=first)
    first.close()
    second = ExitStack()
    tb = sb("turned2", [P, 8192], into=second)
    second.close()
    hn_hi = sb("h_rows_high", [P, TT, D], F32R)
    hn_lo = sb("h_rows_low", [P, TT, D], F32R)
    yhi = sb("y_high", [P, D], F32R)
    ylo = sb("y_low", [P, D], F32R)
    pick = sb("picks", [P, TT, NE, P], F32R)
    pick_now = sb("picks_turned_now", [P, 2, S], F32R)
    con2 = sb("constants2", [P, N_SECOND])
    forget = sb("forget", [P, 3, TT * H])
    wsmall = sb("small_weights", [P, 3, KD * H])
    wsmall_hi = sb("small_weights_high", [P, 3, KD * H], F32R)
    wsmall_lo = sb("small_weights_low", [P, 3, KD * H], F32R)
    small = sb("forget_bias", [H, 2])
    srows = sb("small_logits", [H, S])
    most = sb("most_tokens", [1, 1], I32)
    wcur = sb("slot_weights_now", [P, 2])
    silu_table = sb("silu_table", [1, 1])

    def heads_turned(t, c0):
        return t[:, c0:c0 + 1024].rearrange("p (a s) -> p a s", s=S)

    qdT, kdT, qnT, knT = (heads_turned(ta, 1024 * i) for i in range(4))
    qrT = ta[:, 4096:4608].rearrange("p (a s) -> p a s", s=S)
    krT = ta[:, 4608:4864]
    qup = ta[:, 2048:2048 + TT * QUP].rearrange("p (t n) -> p t n", t=TT)
    kvup = ta[:, 4864:6912].rearrange("p (t n) -> p t n", t=TT)
    kv_heads = ta[:, 4864:6912].rearrange("p (h d) -> p h d", d=P)
    hf1 = ta[:, 4864:6912]
    latent = ta[:, 2048:2816]
    relu = ta[:, 0:3072].rearrange("p (i b n) -> p i b n", i=2, b=3)
    sqT, skT, fqT, fkT = (heads_turned(tb, 1024 * i) for i in range(4))
    gates = tb[:, 4096:8192]
    hf2 = tb[:, 4864:6912]
    silu = tb[:, 0:2048].rearrange("p (i b n) -> p i b n", i=2, b=2)
    combine = tb[:, 2048:4096].rearrange("p (e s) -> p e s", s=S)
    pick_pair = pick[:, :, :, :].rearrange("p t (g e) n -> p t g (e n)", e=2)
    gain_rows = pturn[:, :, :].rearrange("p b s -> p (b s)")
    nat_flat = nat[:, :, :].rearrange("p t n -> p (t n)")
    sgate, sprod = (nat_flat[:, c:c + 512].rearrange("p (b n) -> p b n", b=2) for c in (D, D + 512))
    pickT = nat_flat[:, 2 * D:4 * D].rearrange("p (e s) -> p e s", s=S)
    ident = con[:, C_ID:C_ID + P]
    lathi = acthi[:, :, :].rearrange("p a n -> p (a n)")[:, 0:768]
    latlo = actlo[:, :, :].rearrange("p a n -> p (a n)")[:, 0:768]
    square = probs[:, :, :].rearrange("p b s -> p (b s)")
    route = square[:, 0:512]
    qn_nat = probs
    stage = bias[:, 0:P]
    mod_rows = bias[0:96, P:2 * P]
    pos_int = bias[0:1, S:2 * S].bitcast(I32)
    pos_row = rtmp[0:1, 0, 0:S]
    gain_row = rtmp[0:1, 1, 0:4 * ROPE]

    arrived = [sem(f"piece_arrived{i}") for i in range(RAW)]
    high_done = sem("weights_high_done")
    raw_used = sem("raw_piece_used")
    used = sem("piece_multiplied")
    loaded, ones_set, small_in = sem("vectors_loaded"), sem("ones_set"), sem("small_weights_in")
    c_in, x_in, stage_clear = sem("c_in"), sem("x_in"), sem("stage_cleared")
    setup_t, setup_v, setup_a = sem("setup_tensor"), sem("setup_vector"), sem("setup_scalar")
    mod_summed, mod_reduced = sem("mod_half_summed"), sem("mod_half_reduced")
    mod_stored, gt_spread, gt_ready = sem("mod_section_stored"), sem("gates_spread"), sem("gate_rows_ready")
    squares, squares_used = sem("squares_ready"), sem("squares_used")
    ms_ready, rs_ready = sem("mean_squares_ready"), sem("rsqrt_guess_ready")
    xn_ready, h_turned, h_float = sem("xn_ready"), sem("h_turned"), sem("h_float")
    h_high, h_low = sem("h_high_ready"), sem("h_low_ready")
    proj_out = sem("projection_stored")
    qk_norm, qk_turned, qk_out = sem("qk_normed"), sem("qk_turned"), sem("qk_turned_stored")
    lat_norm, lat_turned, lat_float = sem("latent_normed"), sem("latent_turned"), sem("latent_float")
    lat_high, lat_low = sem("latent_high"), sem("latent_low")
    qup_out, kvup_out = sem("q_up_stored"), sem("kv_up_stored")
    mla_norm, mla_turned = sem("mla_normed"), sem("mla_turned")
    mla_out_a, mla_out_v = sem("mla_nope_stored"), sem("mla_rope_stored")
    scores, shift, probs_ready = sem("scores_ready"), sem("row_shift_ready"), sem("probs_ready")
    turned, pt_ready, values = sem("probs_turned"), sem("probs_turned_stored"), sem("values_done")
    attn_out = sem("attention_stored")
    sb_tail, sb_soft, sb_sum, sb_log = sem("sb_tail"), sem("sb_softplus"), sem("sb_summed"), sem("sb_log_weights")
    o_turned, o_high, o_low = sem("o_turned"), sem("o_high"), sem("o_low")
    x_mixed, x_first, x_done = sem("x_mixed"), sem("x_first_tokens_done"), sem("x_done")
    f_logit, f_abs, f_tail, f_cost = sem("forget_logits"), sem("forget_abs"), sem("forget_tail"), sem("forget_cost")
    t2_out = sem("turned_projection_stored")
    ws_high, ws_low = sem("small_weights_high_ready"), sem("small_weights_low_ready")
    s_logit, s_rows = sem("small_logits_ready"), sem("small_logits_stored")
    gate_out, gate_open = sem("gate_logits_stored"), sem("gates_open")
    gated, z_high, z_low = sem("gated"), sem("gated_high"), sem("gated_low")
    r_logit, r_max, r_exp, r_comb = sem("router_logits"), sem("router_max"), sem("router_exp"), sem("router_weights")
    r_spread, r_out = sem("router_spread"), sem("router_spread_stored")
    r_place, r_most, gain_in = sem("router_places"), sem("most_tokens_known"), sem("gain_rows_in")
    p_ready, p_turned, p_stored = sem("picks_ready"), sem("picks_turned"), sem("picks_turned_stored")
    hn_ready, hn_high, hn_low = sem("h_rows"), sem("h_rows_high"), sem("h_rows_low")
    now_ready, gathered = sem("picks_of_expert"), sem("tokens_gathered")
    g_high, g_low, s_turned = sem("gathered_high"), sem("gathered_low"), sem("slot_activations_turned")
    y_high, y_low, scattered, x_added = sem("y_high"), sem("y_low"), sem("y_scattered"), sem("x_added")
    f_one = [sem(f"ff{i}_function") for i in range(4)]
    f_two = [sem(f"ff{i}_product") for i in range(4)]
    f_hi = [sem(f"ff{i}_high") for i in range(4)]
    f_lo = [sem(f"ff{i}_low") for i in range(4)]
    e_comb = sem("expert_silu_up")
    vstep, astep, pstep = sem("vector_step"), sem("scalar_step"), sem("pool_step")
    stored = sem("out_stored")

    block = ctx.enter_context(nc.Block())

    def loop(value, it, per):
        return value if it is None else value + it * per

    def group_of(layer, second):
        return 2 * layer + second

    def mod_count(l, s, q=0):
        return 4 * SECTIONS.index((l, s)) + q

    def mod_bank(s):
        return psum[(0 if s in (2, 3) else 6) + s % 2]

    def softmax_of(g):
        return g if g < 32 else 32 + (g - 32) // 16 * H + g % 16 - H

    @block.sync
    def _(sp):
        def load(r, src, it=None, per=RAW):
            if r >= RAW:
                sp.wait_ge(raw_used, loop(r - RAW + 1, it, per))
            k, n = src.shape[1], src.shape[2]
            dst = raw[r % RAW][:, 0:k * n].rearrange("p (k n) -> p k n", k=k)
            sp.dma_start(dst, src).then_inc(arrived[r % RAW], 16)

        def rows_of_k(w):
            return w.rearrange("(k p) n -> p k n", p=P)

        def load_mod(l, s, quarters=range(4)):
            w = rows_of_k(a["w_mod"][l])
            for q in quarters:
                c0 = s * D + 512 * (q // 2)
                load(MOD_PLACE[l, s, q], w[:, 4 * (q % 2):4 * (q % 2) + 4, c0:c0 + 512])

        def load_natural(w, w0, chunks, behind=lambda w: None):
            for i, (c0, n) in enumerate(chunks):
                for half in range(2):
                    load(raw_of(w0), rows_of_k(w)[:, 4 * half:4 * half + 4, c0:c0 + n])
                    behind(w0)
                    w0 += 1

        def take(w, b, k):
            return w.rearrange("(b k p) n -> p b k n", k=k, p=P)[:, bass.ds(b, 1)].rearrange("p b k n -> p (b k) n")

        load_mod(0, 0)
        load_mod(0, 1)
        for l in range(2):
            w = l * L1

            def quarter(v):
                v -= l * L1 + AHEAD
                if 0 <= v < 8:
                    load_mod(l, 2 + v // 4, [v % 4])

            load_natural(a["w_in"][l], w, [(0, 512), (512, 512), (1024, 512), (1536, W_IN - 1536)], quarter)
            w += N_IN1
            load(raw_of(w), rows_of_k(a["w_q_up"][l]))
            quarter(w)
            load(raw_of(w + 1), rows_of_k(a["w_kv_up"][l]))
            quarter(w + 1)
            load_natural(a["w_out"][l], w + 2, [(0, 512)])
            if l == 0:
                load_mod(1, 0)
                load_mod(1, 1)
            load_mod(l, 4)
            load_mod(l, 5)
            load_natural(a["w_out"][l], w + 4, [(512, 512)])
            w += 2 + N_OUT
            wu, wd = rows_of_k(a["w_mlp_in"][l]), a["w_mlp_out"][l]

            def pair(j, it):
                b = j if it is None else it * 3 + j
                load(raw_of(w + 1 + 2 * j), wu[:, :, bass.ds((b + 1) * 256, 256)], it)
                load(raw_of(w + 2 + 2 * j), take(wd, b, 2), it)

            load(raw_of(w), wu[:, :, 0:256])
            for j in range(3):
                pair(j, None)
            with sp.Fori(1, 5) as it:
                for j in range(3):
                    pair(j, it)
            load(raw_of(w + N_MLP - 1), take(wd, F1 // 256 - 1, 2))
        for l in range(2):
            w = (W_B2, W_L3)[l]
            wi = a["w_in_2"][l]
            load_natural(wi, w, [(1536, 512), (2048, 512), (2560, 512), (1024, 512)])
            w += N_NAT2
            for j in range(N_TURN2):
                c0 = 256 * j if j < 4 else 3080 + 256 * (j - 4)
                load(raw_of(w + j), rows_of_k(wi)[:, :, c0:c0 + 256])
            w += N_TURN2
            for i, name in enumerate(("w_o_sb_2", "w_o_fox_2")):
                for j in range(2):
                    load(raw_of(w + 2 * i + j), rows_of_k(a[name][l])[:, :, 512 * j:512 * j + 512])
            load_natural(a["w_out_2"][l], w + N_WO, [(0, 512), (512, 512)])
            if l == 0:
                w = W_DENSE
                wu, wd = rows_of_k(a["w_gu_dense_2"][0]), a["w_dn_dense_2"][0]

                def triple(j, it):
                    b = j if it is None else it * 2 + j
                    load(raw_of(w + 2 + 3 * j), wu[:, :, bass.ds((b + 1) * 256, 256)], it)
                    load(raw_of(w + 3 + 3 * j), wu[:, :, bass.ds((b + 1) * 256 + F2, 256)], it)
                    load(raw_of(w + 4 + 3 * j), take(wd, b, 2), it)

                load(raw_of(w), wu[:, :, 0:256])
                load(raw_of(w + 1), wu[:, :, F2:F2 + 256])
                for j in range(2):
                    triple(j, None)
                with sp.Fori(1, 5) as it:
                    for j in range(2):
                        triple(j, it)
                load(raw_of(w + N_DENSE - 1), take(wd, F2 // 256 - 1, 2))
            else:
                wu = a["w_gu_exp_2"][0].rearrange("e (k p) n -> p e k n", p=P)
                wd = a["w_dn_exp_2"][0].rearrange("e (k p) n -> p e k n", p=P)
                with sp.Fori(0, NE) as it:
                    r = raw_of(W_MOE)

                    def gate_up(b, c0):
                        n = 256 if b < 5 else 128
                        v = wu[:, bass.ds(it, 1), :, c0 + 256 * b:c0 + 256 * b + n]
                        return v.rearrange("p e k n -> p (e k) n")

                    def down(b):
                        v = wd[:, bass.ds(it, 1), 2 * b:min(2 * b + 2, 11), :]
                        return v.rearrange("p e k n -> p (e k) n")

                    load(r, gate_up(0, 0), it, EXPERT)
                    load(r + 1, gate_up(0, FE), it, EXPERT)
                    for b in range(5):
                        load(r + 2 + 3 * b, gate_up(b + 1, 0), it, EXPERT)
                        load(r + 3 + 3 * b, gate_up(b + 1, FE), it, EXPERT)
                        load(r + 4 + 3 * b, down(b), it, EXPERT)
                    load(r + 17, down(5), it, EXPERT)
        sp.wait_ge(x_done, 3 + NE)
        sp.dma_start(out.rearrange("b (t p) d -> p (b t) d", p=P), x[:, :, :]).then_inc(stored, 16)
        sp.wait_ge(stored, 16)

    @block.gpsimd
    def _(pool):
        nc.gpsimd.memset(stage, 0.0).then_inc(stage_clear, 1)
        nc.gpsimd.memset(minus[:, :], -1.0).then_inc(ones_set, 1)
        nc.gpsimd.memset(ones[:, :], 1.0).then_inc(ones_set, 1)
        pool.wait_ge(x_done, 2)
        pool.dma_start(con2[:, :], consts[1]).then_inc(small_in, 16)
        pool.dma_start(small[:, :], a["b_f_2"].rearrange("l h -> h l"), allow_slow_non_contiguous=True).then_inc(small_in, 16)
        for i, w in enumerate((a["w_in_2"][0][:, 3072:3080], a["w_in_2"][1][:, 3072:3080], a["w_router_2"][0])):
            pool.dma_start(wsmall[:, i, :].rearrange("p (k n) -> p k n", k=KD),
                           w.rearrange("(k p) n -> p k n", p=P), allow_slow_non_contiguous=True).then_inc(small_in, 16)
        pool.wait_ge(x_mixed, 16)
        pool.dma_start(gain_rows, a["g_ffn_2"][1:2, :].to_broadcast([P, D])).then_inc(gain_in, 16)
        pool.wait_ge(r_most, 1)
        tokens = pool.value_load(most[0:1, 0:1], min_val=0, max_val=S)
        with pool.If(tokens < P + 1):
            def picks(e, i, it=None):
                nc.gpsimd.tensor_copy(pick_now[:, i, :], pickT[:, e, :] if it is None else pickT[:, bass.ds(e, 1), :]
                                      .rearrange("p e s -> p (e s)")).then_inc(now_ready, 1)
                nc.gpsimd.tensor_copy(wcur[:, i:i + 1], route[:, 224:232][:, e:e + 1] if it is None
                                      else route[:, 224:232][:, bass.ds(e, 1)]).then_inc(now_ready, 1)

            pool.wait_ge(p_stored, 5)
            picks(0, 1)
            picks(0, 0)
            with pool.Fori(0, NE // 2 - 1) as it:
                for i in (1, 2):
                    pool.wait_ge(scattered, loop(i, it, 2))
                    picks(it * 2 + i, i % 2, it)
            pool.wait_ge(scattered, NE - 1)
            picks(NE - 1, 1)

    @block.scalar
    def _(act):
        steps, ahead, jobs, sqs = [0], [0], [0], [0]

        def step(ins):
            steps[0] += 1
            ins.then_inc(astep, 1)
            act.wait_ge(astep, steps[0])

        def copy(dst, src, scale=1.0):
            return nc.scalar.activation(dst, src, ACT.Copy, scale=scale)

        def split(w, it=None, per=RAW):
            r = raw_of(w)
            act.wait_ge(arrived[r % RAW], loop(16 * (r // RAW + 1), it, 16 * per // RAW))
            if w >= SPLIT:
                act.wait_ge(used, loop(w - SPLIT + 1, it, per))
            copy(whi[w % SPLIT][:, :], raw[r % RAW][:, :]).then_inc(high_done, 1)

        def split_to(w):
            while ahead[0] <= min(w, W_END - 1):
                split(ahead[0])
                ahead[0] += 1

        def load_ln_exp():
            nc.scalar.add_instruction(mybir.InstLoadActFuncSet(
                name=nc.get_next_instruction_name(), act_func_set_id=LN_EXP_SET, ins=[], outs=[]))

        def load_silu():
            nc.scalar.activation(silu_table[:, :], ones[0:1, 0:1], ACT.Silu)

        def rsqrt_guess(n):
            jobs[0] += 1
            act.wait_ge(ms_ready, jobs[0])
            step(nc.scalar.activation(stat[:, 1, 0:n], stat[:, 0, 0:n], ACT.Ln))
            nc.scalar.activation(stat[:, 1, 0:n], stat[:, 1, 0:n], ACT.Exp, scale=-0.5).then_inc(rs_ready, 1)

        def square_job(parts):
            if sqs[0]:
                act.wait_ge(squares_used, sqs[0])
            for dst, src, total in parts[:-1]:
                step(nc.scalar.activation(dst, src, ACT.Square, accum_out=total))
            dst, src, total = parts[-1]
            ins = nc.scalar.activation(dst, src, ACT.Square, accum_out=total) if total is not None \
                else nc.scalar.activation(dst, src, ACT.Square)
            ins.then_inc(squares, 1)
            sqs[0] += 1

        def norm_squares(*ready):
            if sqs[0]:
                act.wait_ge(squares_used, sqs[0])
            for t in range(TT):
                act.wait_ge(*ready[t])
                ins = nc.scalar.activation(square, x[:, t, :], ACT.Square, accum_out=stat[:, 2, t:t + 1])
                if t == 0:
                    step(ins)
            ins.then_inc(squares, 1)
            sqs[0] += 1
            rsqrt_guess(TT)

        def norm_high(n):
            hf = hf1 if n < 4 else hf2
            for b in range(4):
                act.wait_ge(h_float, 4 * n + b + 1)
                copy(hhi[:, 2 * b:2 * b + 2, :], hf[:, 512 * b:512 * b + 512].rearrange("p (a s) -> p a s", s=S)) \
                    .then_inc(h_high, 1)

        def store_chunk(c, w, n):
            split_to(w + AHEAD)
            act.wait_ge(used, w + 1)
            for t in range(TT):
                ins = copy(nat[:, t, 512 * c:512 * c + n], psum[4 + 2 * (c % 2) + t][:, 0:n])
            ins.then_inc(proj_out, 1)

        def store_qk(l, qT, kT, vq, vk):
            for b in range(4):
                act.wait_ge(qk_turned, 4 * l + b + 1)
                dst, g = ((qT, vq), (kT, vk))[b // 2]
                copy(dst[:, 2 * (b % 2):2 * (b % 2) + 2, :], psum[b][:, :].rearrange("p (a s) -> p a s", s=S),
                     scale=vec[:, g:g + 1]).then_inc(qk_out, 1)

        def softmax_head(g, scale, from_psum, causal=False):
            si = softmax_of(g)
            act.wait_ge(shift, si + 1)
            if g >= 2:
                act.wait_ge(turned, max(si - 1, 1))
            for t in range(TT):
                n = P if causal and t == 0 else S
                src = psum[g % 2] if from_psum else probs[:, g % 2, :]
                i = 8 * t + g % H
                ins = nc.scalar.activation(probs[:, g % 2, S * t:S * t + n], src[:, S * t:S * t + n], ACT.Exp,
                                           bias=negmax[:, g % 2, t:t + 1], scale=scale,
                                           accum_out=expsum[:, (g // H) % 2, i:i + 1])
            ins.then_inc(probs_ready, 1)

        def turn_o(l):
            for b in range(4):
                act.wait_ge(o_turned, 4 * l + b + 1)
                copy(hhi[:, 2 * b:2 * b + 2, :], psum[b][:, :].rearrange("p (a s) -> p a s", s=S)).then_inc(o_high, 1)

        n = [0]

        def fetch(dst, src):
            act.dma_start(dst, src).then_inc(loaded, 16)
            n[0] += 1

        act.dma_start(ccol[:, :], a["c"].rearrange("o (k p) -> p (o k)", p=P), allow_slow_non_contiguous=True) \
            .then_inc(c_in, 16)
        act.dma_start(x[:, :, :], a["x"].rearrange("b (t p) d -> p (b t) d", p=P)).then_inc(x_in, 16)
        act.wait_ge(c_in, 16)
        nc.scalar.activation(ccol[:, :], ccol[:, :], ACT.Silu).then_inc(setup_a, 1)
        act.wait_ge(stage_clear, 1)
        fetch(con[:, :], consts[0])
        for r, name in ((V_G1, "g_norm_mix"), (V_G2, "g_norm_mlp"), (V_G3, "g_mix_2"), (V_G4, "g_ffn_2"),
                        (V_CQ, "g_cq"), (V_CKV, "g_ckv"), (V_BG, "b_gate_2")):
            src = a[name].rearrange("l (k p) -> (l k) p", p=P)
            fetch(stage[r:r + src.shape[0], :], src)
        fetch(mod_rows, a["b_mod"].rearrange("l (k p) -> (l k) p", p=P))
        for r, name in ((V_QD, "g_q_dil"), (V_KD, "g_k_dil"), (V_QN, "g_q_nope"), (V_KN, "g_k_nope"),
                        (V_QF, "g_q_2"), (V_KF, "g_k_2")):
            for twice in range(2):
                fetch(stage[r:r + 2, DH * twice:DH * twice + DH], a[name])
        fetch(pos_int, a["positions"])
        for i, name in enumerate(("g_q_rope", "g_k_rope")):
            fetch(gain_row[:, 64 * i:64 * i + 64], a[name].rearrange("(o l) r -> o (l r)", o=1))
        assert n[0] == N_LOADS

        for l in range(2):
            w = l * L1
            load_ln_exp()
            norm_squares(*[(x_first, l), (x_done, l)] if l else [(x_in, 16)] * TT)
            if l == 0:
                split_to(AHEAD - 1)
            norm_high(2 * l)
            for c in range(4):
                store_chunk(c, w + 2 * c + 1, 512 if c < 3 else W_IN - 1536)
                if l == 0 and c == 1:
                    act.wait_ge(setup_v, SETUP_TRIG)
                    nc.scalar.activation(trig[:, :, :, :], trig[:, :, :, :], ACT.Sin).then_inc(setup_a, 1)
                    load_ln_exp()
            w += N_IN1
            act.wait_ge(proj_out, 4 * l + 4)
            square_job([(square[:, 0:n], nat[:, t, c0:c0 + n], stat[:, 2, 2 * i + t:2 * i + t + 1])
                        for i, (c0, n) in enumerate(((1536, QL), (1792, KVL), (1920, ROPE))) for t in range(TT)])
            rsqrt_guess(6)
            act.wait_ge(lat_float, l + 1)
            copy(lathi, latent).then_inc(lat_high, 1)
            for t in range(TT):
                square_job([(square, nat[:, t, 0:D], None)])
            rsqrt_guess(32)
            split_to(w + AHEAD - 1)
            act.wait_ge(used, w + 1)
            for t in range(TT):
                b0 = 6 - 2 * t
                step(copy(qup[:, t, 0:512], psum[b0][:, :]))
                ins = copy(qup[:, t, 512:768], psum[b0 + 1][:, 0:256])
                if t == 0:
                    step(ins)
            ins.then_inc(qup_out, 1)
            act.wait_ge(qup_out, l + 1)
            for t in range(TT):
                square_job([(square[:, 0:QUP], qup[:, t, :], None)])
            act.wait_ge(kvup_out, l + 1)
            square_job([(square.rearrange("p (h d) -> p h d", d=DH), kv_heads[:, :, 0:DH], None)])
            rsqrt_guess(48)
            split_to(w + 1 + AHEAD)
            store_qk(l, qdT, kdT, V_QD + l, V_KD + l)
            for b in range(4):
                act.wait_ge(mla_turned, 6 * l + b + 1)
                dst, g = ((qnT, V_QN + l), (knT, V_KN + l))[b // 2]
                copy(dst[:, 2 * (b % 2):2 * (b % 2) + 2, :], psum[4 + b][:, :].rearrange("p (a s) -> p a s", s=S),
                     scale=vec[:, g:g + 1]).then_inc(mla_out_a, 1)
            for h in range(H):
                softmax_head(16 * l + h, 1.0, False)
            for h in range(H):
                softmax_head(16 * l + H + h, float(DH + ROPE) ** -0.5, True)
            for i in range(2):
                act.wait_ge(gt_spread, 2 * l + i + 1)
                for half in range(2):
                    ins = copy(gtb[:, i, 512 * half:512 * half + 512], psum[6 - 2 * i + half][:, :])
                ins.then_inc(gt_ready, 1)
            turn_o(l)
            w += 2
            for j in range(N_OUT):
                split_to(w + j + AHEAD)
            w += N_OUT
            norm_squares((x_mixed, 4 * l + 3), (x_mixed, 4 * l + 4))
            norm_high(2 * l + 1)

            def relu_block(b, slot, it=None):
                act.wait_ge(used, loop(w + 2 * b, it, RAW) if b else w + 1)
                if b >= 3:
                    act.wait_ge(f_two[l], loop(b - 2, it, 3))
                nc.scalar.activation(relu[:, 0, slot, :], psum[slot][:, :], ACT.Relu).then_inc(f_one[l], 1)

            def high_block(b, slot, it=None):
                act.wait_ge(f_two[l], loop(b + 1, it, 3))
                if b >= 3:
                    act.wait_ge(used, loop(w + 2 * (b - 3) + 3, it, RAW))
                copy(acthi[:, slot, :], relu[:, 1, slot, :]).then_inc(f_hi[l], 1)

            split_to(w + 2)
            relu_block(0, 0)
            high_block(0, 0)
            for j in range(3):
                split_to(w + 3 + 2 * j)
                relu_block(j + 1, (j + 1) % 3)
                split_to(w + 4 + 2 * j)
                high_block(j + 1, (j + 1) % 3)
            with act.Fori(0, 4) as it:
                for j in range(3, 6):
                    split(w + 3 + 2 * j, it)
                    relu_block(j + 1, (j + 1) % 3, it)
                    split(w + 4 + 2 * j, it)
                    high_block(j + 1, (j + 1) % 3, it)
            ahead[0] = w + N_MLP + 1
            split_to(w + N_MLP - 1 + AHEAD)

        for l in range(2):
            w = (W_B2, W_L3)[l]
            n = 4 + 2 * l
            load_ln_exp()
            norm_squares((x_first, 2 + l), (x_done, 2 + l))
            norm_high(n)
            for c in range(4):
                store_chunk(c, w + 2 * c + 1, 512)
                if c == 0 and l == 0:
                    act.wait_ge(small_in, 80)
                    copy(wsmall_hi[:, :, :], wsmall[:, :, :]).then_inc(ws_high, 1)
            w += N_NAT2
            for j in range(N_QK2):
                split_to(w + j + AHEAD - 1)
                act.wait_ge(used, w + j + 1)
                copy((sqT, skT)[j // 2][:, 2 * (j % 2):2 * (j % 2) + 2, :], psum[j][:, :].rearrange("p (a s) -> p a s", s=S),
                     scale=DH ** -0.5 if j < 2 else 1.0).then_inc(t2_out, 1)
                split_to(w + j + AHEAD)
                if j < 2:
                    square_job([(square, nat[:, j, 0:D], None)])
                if j == 2:
                    rsqrt_guess(32)
            act.wait_ge(f_abs, l + 1)
            step(nc.scalar.activation(forget[:, 1, :], forget[:, 1, :], ACT.Exp, scale=-1.0))
            nc.scalar.activation(forget[:, 1, :], forget[:, 1, :], ACT.Ln, bias=1.0).then_inc(f_tail, 1)
            store_qk(2 + l, fqT, fkT, V_QF + l, V_KF + l)
            g0 = 32 + 16 * l
            act.wait_ge(squares_used, sqs[0])

            def tail(h):
                g = g0 + h
                pv = probs[:, g % 2, 0:384]
                act.wait_ge(scores, g + 1)
                step(nc.scalar.activation(pv, psum[g % 2][:, 0:384], ACT.Abs))
                step(nc.scalar.activation(pv, pv, ACT.Exp, scale=-1.0))
                nc.scalar.activation(pv, pv, ACT.Ln, bias=1.0).then_inc(sb_tail, 1)

            tail(0)
            for h in range(H):
                if h + 1 < H:
                    tail(h + 1)
                g = g0 + h
                act.wait_ge(sb_log, H * l + h + 1)
                act.wait_ge(values, g - 1)
                nc.scalar.activation(pturn[:, g % 2, 0:384], probs[:, g % 2, 0:384], ACT.Exp).then_inc(probs_ready, 1)
                if h % 2 == 0:
                    split_to(w + N_QK2 + h // 2 + AHEAD)
            for h in range(H):
                softmax_head(g0 + H + h, 1.0, False, causal=True)
                if h % 2 == 0:
                    split_to(w + N_QK2 + (H + h) // 2 + AHEAD)
            turn_o(2 + l)
            w += N_TURN2
            split_to(w + AHEAD)
            for q in range(8):
                act.wait_ge(gate_out, 8 * l + q + 1)
                v = gates[:, 512 * q:512 * q + 512]
                nc.scalar.activation(v, v, ACT.Sigmoid).then_inc(gate_open, 1)
            load_ln_exp()
            for j in range(N_WO):
                split_to(w + j + AHEAD)
            act.wait_ge(used, w + N_WO)
            for q in range(4):
                act.wait_ge(gated, 4 * l + q + 1)
                copy(hhi[:, 2 * q:2 * q + 2, :], gates[:, 512 * q:512 * q + 512].rearrange("p (a s) -> p a s", s=S)) \
                    .then_inc(z_high, 1)
            w += N_WO
            for j in range(N_OUT):
                split_to(min(w + j + AHEAD, W_MOE))
            w += N_OUT
            norm_squares((x_mixed, 4 * (2 + l) + 3), (x_mixed, 4 * (2 + l) + 4))
            norm_high(n + 1)

            def silu_block(f, w, b, n, it=None, per=0, wper=0):
                act.wait_ge(used, loop(w, it, wper))
                if b >= 2:
                    act.wait_ge(f_two[f], loop(b - 1, it, per))
                nc.scalar.activation(silu[:, 0, b % 2, 0:n], psum[b % 2][:, 0:n], ACT.Silu).then_inc(f_one[f], 1)

            def high_block2(f, w, b, n, it=None, per=0, wper=0):
                act.wait_ge(f_two[f], loop(b + 1, it, per))
                act.wait_ge(used, loop(w, it, wper))
                copy(acthi[:, b % 2, 0:n], silu[:, 1, b % 2, 0:n]).then_inc(f_hi[f], 1)

            if l == 0:
                split_to(w + 2)
                silu_block(2, w + 1, 0, 512)
                split_to(w + 3)
                high_block2(2, w, 0, 512)
                for j in range(2):
                    m = w + 2 + 3 * j
                    split_to(m + 2)
                    silu_block(2, m + 1, j + 1, 512)
                    split_to(m + 4)
                    high_block2(2, m, j + 1, 512)
                with act.Fori(0, 4) as it:
                    for j in range(2, 4):
                        m = w + 2 + 3 * j
                        split(m + 2, it)
                        silu_block(2, m + 1, j + 1, 512, it, 2, RAW)
                        split(m + 3, it)
                        split(m + 4, it)
                        high_block2(2, m, j + 1, 512, it, 2, RAW)
                ahead[0] = w + N_DENSE + 1
                split_to(w + N_DENSE - 1 + AHEAD)
            else:
                act.wait_ge(hn_ready, 1)
                for t in range(TT):
                    copy(hn_hi[:, t, :], nat[:, t, 0:D]).then_inc(hn_high, 1)
                act.wait_ge(r_max, 1)
                for t in range(TT):
                    ins = nc.scalar.activation(route[:, 16 + 8 * t:24 + 8 * t], route[:, 8 * t:8 * t + 8], ACT.Exp,
                                               bias=route[:, 32 + t:33 + t])
                ins.then_inc(r_exp, 1)
                def expert(it, last):
                    def split_ahead(m):
                        if not last or m < w + EXPERT:
                            split(m, it, EXPERT)

                    split_ahead(w + 2)
                    silu_block(3, w + 1, 0, 512, it, 6, EXPERT)
                    split_ahead(w + 3)
                    high_block2(3, w, 0, 512, it, 6, EXPERT)
                    for b in range(1, 6):
                        m = w + 3 * b - 1
                        n = 512 if b < 5 else 256
                        split_ahead(m + 2)
                        silu_block(3, m + 1, b, n, it, 6, EXPERT)
                        split_ahead(m + 3)
                        split_ahead(m + 4)
                        high_block2(3, m, b, n, it, 6, EXPERT)
                    split_ahead(w + EXPERT + 1)

                def few_tokens(it, i, last):
                    v0 = w + EXPERT * i

                    def at(value, per):
                        return loop(value + i * per, it, 2 * per)

                    def split_ahead(m):
                        if not last or m < w + 2 * EXPERT:
                            split(m, it, 2 * EXPERT)

                    if i == 0:
                        for b in range(4):
                            act.wait_ge(gathered, loop(b + 1, it, 4))
                            copy(hhi[:, 2 * b:2 * b + 2, :], psum[6 + b % 2][:, :].rearrange("p (a s) -> p a s", s=S)) \
                                .then_inc(g_high, 1)
                            if b == 1:
                                split_ahead(v0 + 1)

                    def silu_slots(b, n):
                        act.wait_ge(used, loop(v0 + 3 * b + 1 if b else v0 + 2, it, 2 * EXPERT))
                        if b >= 2:
                            act.wait_ge(f_two[3], at(b - 1, 6))
                        nc.scalar.activation(sgate[:, b % 2, 0:n], psum[b % 2][:, 0:n], ACT.Silu).then_inc(f_one[3], 1)

                    def high_slots(b, n):
                        act.wait_ge(s_turned, at(b + 1, 6))
                        if b >= 2:
                            act.wait_ge(used, loop(v0 + 3 * b - 1, it, 2 * EXPERT))
                        copy(acthi[:, b % 2, 0:n], psum[2 + b % 2][:, 0:n]).then_inc(f_hi[3], 1)

                    split_ahead(v0 + 2)
                    silu_slots(0, 256)
                    split_ahead(v0 + 3)
                    for b in range(1, 6):
                        m = v0 + 3 * b - 1
                        n = 256 if b < 5 else 128
                        split_ahead(m + 2)
                        if b < 5:
                            high_slots(b - 1, 256)
                            split_ahead(m + 3)
                            silu_slots(b, n)
                            split_ahead(m + 4)
                        else:
                            high_slots(4, 256)
                            silu_slots(5, n)
                            split_ahead(m + 3)
                            high_slots(5, n)
                            split_ahead(m + 4)
                    if i == 0:
                        split_ahead(v0 + EXPERT + 1)
                    act.wait_ge(used, loop(v0 + EXPERT, it, 2 * EXPERT))
                    act.wait_ge(now_ready, at(4, 2))
                    for half in range(2):
                        copy(yhi[:, 512 * half:512 * half + 512], psum[4 + half][:, :], scale=wcur[:, i:i + 1]) \
                            .then_inc(y_high, 1)

                act.wait_ge(r_most, 1)
                tokens = act.value_load(most[0:1, 0:1], min_val=0, max_val=S)
                with act.If(tokens < P + 1):
                    act.wait_ge(hn_low, 2)
                    for q in range(4):
                        act.wait_ge(p_turned, q + 1)
                        copy(pickT[:, 2 * q:2 * q + 2, :], psum[q][:, :].rearrange("p (e s) -> p e s", s=S)) \
                            .then_inc(p_stored, 1)
                    load_silu()
                    with act.Fori(0, NE // 2 - 1) as it:
                        for i in range(2):
                            few_tokens(it, i, False)
                    for i in range(2):
                        few_tokens(NE // 2 - 1, i, True)
                with act.Else():
                    act.wait_ge(r_spread, 1)
                    for q in range(4):
                        ins = copy(combine[:, 2 * q:2 * q + 2, :], psum[q][:, :].rearrange("p (e s) -> p e s", s=S))
                    ins.then_inc(r_out, 1)
                    split(w + 1)
                    with act.Fori(0, NE - 1) as it:
                        expert(it, False)
                    expert(NE - 1, True)

    @block.vector
    def _(dve):
        steps, low, jobs, sqs, adds = [0], [0], [0], [0], [0]
        V = nc.vector

        def step(ins):
            steps[0] += 1
            ins.then_inc(vstep, 1)
            dve.wait_ge(vstep, steps[0])

        def rest(w, it=None, per=RAW):
            dve.wait_ge(high_done, loop(w + 1, it, per))
            V.tensor_tensor(wlo[w % SPLIT][:, :], raw[raw_of(w) % RAW][:, :], whi[w % SPLIT][:, :].bitcast(F32),
                            ALU.subtract).then_inc(raw_used, 1)

        def rest_to(w):
            while low[0] <= min(w, W_END - 1):
                rest(low[0])
                low[0] += 1

        def take_squares():
            sqs[0] += 1
            dve.wait_ge(squares, sqs[0])

        def means(parts):
            for c, n, size in parts:
                ins = V.tensor_scalar(stat[:, 0, c:c + n], stat[:, 2, c:c + n], 1.0 / size, EPS, ALU.mult, ALU.add)
            return ins

        def refine(n):
            jobs[0] += 1
            v, y, u = stat[:, 0, 0:n], stat[:, 1, 0:n], stat[:, 3, 0:n]
            dve.wait_ge(rs_ready, jobs[0])
            step(V.tensor_tensor(u, y, y, ALU.mult))
            step(V.tensor_tensor(u, u, v, ALU.mult))
            step(V.tensor_scalar(u, u, -0.5, 1.5, ALU.mult, ALU.add))
            step(V.tensor_tensor(y, y, u, ALU.mult))

        def norm_rows():
            take_squares()
            ins = means([(0, TT, D)])
            step(ins)
            V.sem_inc(ms_ready, 1)
            V.sem_inc(squares_used, 1)
            refine(TT)
            for t in range(TT):
                ins = V.tensor_scalar(nat[:, t, 0:D], x[:, t, :], stat[:, 1, t:t + 1], None, ALU.mult)
            ins.then_inc(xn_ready, 1)

        def norm(n, scale, shift_):
            if n:
                norm_rows()
            hf = hf1 if n < 4 else hf2

            def low_part(b):
                dve.wait_ge(h_high, 4 * n + b + 1)
                V.tensor_tensor(hlo[:, 2 * b:2 * b + 2, :],
                                hf[:, 512 * b:512 * b + 512].rearrange("p (a s) -> p a s", s=S),
                                hhi[:, 2 * b:2 * b + 2, :].bitcast(F32), ALU.subtract).then_inc(h_low, 1)

            for b in range(4):
                dve.wait_ge(h_turned, 4 * n + b + 1)
                for i in range(2):
                    k = 2 * b + i
                    ins = V.tensor_scalar(hf[:, S * k:S * k + S], psum[b][:, S * i:S * i + S], scale(k),
                                          shift_(k) if shift_ else None, ALU.mult, *([ALU.add] if shift_ else []))
                ins.then_inc(h_float, 1)
                if b:
                    low_part(b - 1)
            low_part(3)

        def head_sums(t):
            take_squares()
            V.tensor_reduce(stat[:, 2, 16 * t:16 * t + 16], square.rearrange("p (h d) -> p h d", d=DH),
                            AX.X, ALU.add).then_inc(squares_used, 1)
            if t == TT - 1:
                dve.wait_ge(squares_used, sqs[0])
                means([(0, 32, DH)]).then_inc(ms_ready, 1)

        def heads_norm():
            refine(32)
            for t in range(TT):
                v = nat[:, t, 0:D].rearrange("p (h d) -> p h d", d=DH)
                ins = V.tensor_tensor(v, v, stat[:, 1, 16 * t:16 * t + 16].unsqueeze(2).to_broadcast([P, 16, DH]), ALU.mult)
            ins.then_inc(qk_norm, 1)

        def turn_store(g, n):
            dve.wait_ge(turned, softmax_of(g) + 1)
            if g >= 2:
                dve.wait_ge(values, g - 1)
            V.tensor_copy(pturn[:, g % 2, 0:n], psum[2 + g % 2][:, 0:n]).then_inc(pt_ready, 1)

        def slot_free(g):
            if g >= 2:
                dve.wait_ge(probs_ready, g - 1)
                if softmax_of(g) >= 2:
                    dve.wait_ge(turned, softmax_of(g) - 1)

        def added_max(g, addends):
            dve.wait_ge(scores, g + 1)
            slot_free(g)
            for t, (n, add) in enumerate(addends):
                c = slice(S * t, S * t + n)
                ins = V.tensor_tensor_reduce(probs[:, g % 2, c], psum[g % 2][:, c], add, 1.0, LOWEST,
                                             ALU.add, ALU.max, rowmax[:, g % 2, t:t + 1])
            step(ins)
            V.tensor_scalar(negmax[:, g % 2, :], rowmax[:, g % 2, :], -1.0, None, ALU.mult).then_inc(shift, 1)

        def dilated_max(g, h):
            step(V.scalar_tensor_tensor(bias[:, :], dist[:, :], -(2.0 ** -(h + 1)), con[:, C_LNM:C_LNM + TT * S],
                                        ALU.mult, ALU.add))
            added_max(g, [(S, bias[:, S * t:S * t + S]) for t in range(TT)])

        def sum_mod(l, s, q, store=True):
            n, r = mod_count(l, s, q) // 2, MOD_PLACE[l, s, q]
            dve.wait_ge(arrived[r % RAW], 16 * (r // RAW + 1))
            if n >= 2 and q % 2 == 0:
                dve.wait_ge(mod_reduced, n - 1)
            acc, v = mod_sums[:, n % 2, :], raw[r % RAW]
            for i in range(4):
                k = 4 * (q % 2) + i
                vk = v[:, 512 * i:512 * i + 512]
                if k:
                    ins = V.scalar_tensor_tensor(acc, vk, ccol[:, k:k + 1], acc, ALU.mult, ALU.add)
                else:
                    ins = V.tensor_scalar(acc, vk, ccol[:, 0:1], None, ALU.mult)
                step(ins)
            V.sem_inc(raw_used, 1)
            if q % 2:
                V.sem_inc(mod_summed, 1)
            if q == 3 and s % 2 and store:
                store_mod(l, s - 1)

        def store_mod(l, s):
            dve.wait_ge(mod_reduced, mod_count(l, s) // 2 + 2)
            col = (0, 1, 4, 2, 3, 5)[s]
            b0 = V_BM + 8 * (6 * l + s)
            step(V.tensor_tensor(modc[:, col, :], mod_bank(s)[:, 0:KD], vec[:, b0:b0 + KD], ALU.add))
            if s in (1, 4):
                g0 = (V_G1, V_G2)[s // 4] + KD * l
                step(V.scalar_tensor_tensor(modc[:, col, :], modc[:, col, :], 1.0, vec[:, g0:g0 + KD], ALU.add, ALU.mult))
            V.sem_inc(mod_stored, 1)

        def plain_max(g, scale):
            dve.wait_ge(scores, g + 1)
            slot_free(g)
            step(V.tensor_reduce(rowmax[:, g % 2, :], psum[g % 2][:, :].rearrange("p (t s) -> p t s", s=S), AX.X, ALU.max))
            V.tensor_scalar(negmax[:, g % 2, :], rowmax[:, g % 2, :], -scale, None, ALU.mult).then_inc(shift, 1)

        def store_group(layer, second, divide=True):
            j = group_of(layer, second)
            dve.wait_ge(probs_ready, 8 * j + 8)
            if divide:
                sums = expsum[:, j % 2, :]
                step(V.reciprocal(sums, sums))
            dve.wait_ge(values, 8 * j + 8)
            for t in range(TT):
                dst = nat[:, t, 512 * second:512 * second + 512]
                if divide:
                    ins = V.tensor_tensor(dst.rearrange("p (h d) -> p h d", d=DH),
                                          psum[4 + t][:, :].rearrange("p (h d) -> p h d", d=DH),
                                          sums[:, 8 * t:8 * t + 8].unsqueeze(2).to_broadcast([P, H, DH]), ALU.mult)
                else:
                    ins = V.tensor_copy(dst, psum[4 + t][:, :])
            ins.then_inc(attn_out, 1)

        def turn_o(l):
            for b in range(4):
                dve.wait_ge(o_high, 4 * l + b + 1)
                V.tensor_tensor(hlo[:, 2 * b:2 * b + 2, :], psum[b][:, :].rearrange("p (a s) -> p a s", s=S),
                                hhi[:, 2 * b:2 * b + 2, :].bitcast(F32), ALU.subtract).then_inc(o_low, 1)

        def add_to_x(bank, t, half, gate):
            xs = x[:, t, 512 * half:512 * half + 512]
            if gate is None:
                return V.tensor_tensor(xs, xs, psum[bank][:, :], ALU.add)
            adds[0] += 1
            tmp = pturn[:, adds[0] % 2, :]
            step(V.tensor_tensor(tmp, psum[bank][:, :], gtb[:, gate, 512 * half:512 * half + 512], ALU.mult))
            return V.tensor_tensor(xs, xs, tmp, ALU.add)

        dve.wait_ge(setup_a, 1)
        for q in range(4):
            sum_mod(0, 0, q, False)
        for q in range(3):
            sum_mod(0, 1, q)
        norm_rows()
        dve.wait_ge(setup_t, 1)
        V.tensor_copy(vec[:, :], psum[0][:, 0:N_VEC]).then_inc(setup_v, 1)
        V.tensor_copy(pos_row, pos_int).then_inc(setup_v, 1)
        sum_mod(0, 1, 3, False)
        dve.wait_ge(setup_v, 1)
        store_mod(0, 0)
        dve.wait_ge(setup_t, 2)
        V.tensor_copy(poscol[:, :], psum[1][:, 0:TT]).then_inc(setup_v, 1)
        V.tensor_copy(grope[:, :, :, :].rearrange("p a b c -> p (a b c)"), psum[1][:, P:2 * P]).then_inc(setup_v, 1)
        step(V.tensor_scalar(vec[:, V_QD:V_QD + 2], vec[:, V_QD:V_QD + 2], DH ** -0.5, None, ALU.mult))
        step(V.tensor_scalar(vec[:, V_QF:V_QF + 2], vec[:, V_QF:V_QF + 2], DH ** -0.5, None, ALU.mult))
        dve.wait_ge(setup_v, 4)
        two_pi = 2 * np.pi
        c1 = 6.28125
        c2 = float(np.float32(two_pi - c1))
        c3 = float(two_pi - c1 - c2)
        half = ROPE // 2
        ang, k, r = pturn[:, 0, 0:ROPE], pturn[:, 1, 0:2 * ROPE], trig[:, :, :, :].rearrange("p i t n -> p (i t n)")
        for t in range(TT):
            V.tensor_scalar(dist[:, S * t:S * t + S], psum[2][:, 0:S], poscol[:, t:t + 1], None, ALU.subtract)
            ins = V.tensor_scalar(ang[:, half * t:half * t + half], con[:, C_INV:C_INV + half], poscol[:, t:t + 1], None, ALU.mult)
        step(ins)
        V.sem_inc(setup_v, 1)

        def angles():
            V.scalar_tensor_tensor(dist[:, :], dist[:, :], -1.0, dist[:, :], ALU.mult, ALU.max)
            V.tensor_scalar(k[:, 0:ROPE], ang, 1 / two_pi, 0.25, ALU.mult, ALU.add)
            step(V.tensor_scalar(k[:, ROPE:2 * ROPE], ang, 1 / two_pi, None, ALU.mult))
            step(V.tensor_scalar(k, k, MAGIC, None, ALU.add))
            step(V.tensor_scalar(k, k, MAGIC, None, ALU.subtract))
            for i in range(2):
                ins = V.scalar_tensor_tensor(r[:, ROPE * i:ROPE * i + ROPE], k[:, ROPE * i:ROPE * i + ROPE], -c1, ang, ALU.mult, ALU.add)
            step(ins)
            step(V.scalar_tensor_tensor(r, k, -c2, r, ALU.mult, ALU.add))
            step(V.scalar_tensor_tensor(r, k, -c3, r, ALU.mult, ALU.add))
            step(V.tensor_scalar(r[:, 0:ROPE], r[:, 0:ROPE], np.pi / 2, None, ALU.add))
            step(V.tensor_scalar(r, r, 3.1415925, -3.1415925, ALU.min, ALU.max))
            V.sem_inc(setup_v, 1)

        for l in range(2):
            w = l * L1
            if l == 0:
                store_mod(0, 1)
            norm(2 * l, lambda k: modc[:, 1, k:k + 1], lambda k: modc[:, 0, k:k + 1])
            for j in range(N_IN1):
                rest_to(w + j + AHEAD)
                if l == 0 and j == 0:
                    angles()
                sum_mod(l, 2 + j // 4, j % 4)
            store_mod(l, 3)
            w += N_IN1
            take_squares()
            step(means([(0, 2, QL), (2, 2, KVL), (4, 2, ROPE)]))
            V.sem_inc(ms_ready, 1)
            V.sem_inc(squares_used, 1)
            refine(6)
            for t in range(TT):
                V.tensor_scalar(nat[:, t, 1536:1792], nat[:, t, 1536:1792], stat[:, 1, t:t + 1], None, ALU.mult)
                V.tensor_scalar(nat[:, t, 1792:1920], nat[:, t, 1792:1920], stat[:, 1, 2 + t:3 + t], None, ALU.mult)
                step(V.tensor_scalar(nat[:, t, 1920:1952], nat[:, t, 1920:1952], stat[:, 1, 4 + t:5 + t], None, ALU.mult))
            V.sem_inc(lat_norm, 1)
            dve.wait_ge(lat_turned, l + 1)
            for i in range(3):
                src = psum[4][:, S * i:S * i + S] if i < 2 else psum[5][:, 0:S]
                g = V_CQ + 2 * l + i if i < 2 else V_CKV + l
                ins = V.tensor_scalar(latent[:, S * i:S * i + S], src, vec[:, g:g + 1], None, ALU.mult)
            ins.then_inc(lat_float, 1)
            dve.wait_ge(lat_high, l + 1)
            V.tensor_tensor(latlo, latent, lathi.bitcast(F32), ALU.subtract).then_inc(lat_low, 1)
            rest_to(w + AHEAD - 1)
            for t in range(TT):
                head_sums(t)
            heads_norm()
            dve.wait_ge(used, w + 2)
            for t in range(TT):
                for i in range(2):
                    ins = V.tensor_copy(kvup[:, t, 512 * i:512 * i + 512], psum[2 * t + i][:, :])
            ins.then_inc(kvup_out, 1)
            for t in range(TT):
                take_squares()
                v = square[:, 0:QUP].rearrange("p (h d) -> p h d", d=DH + ROPE)
                V.tensor_reduce(stat[:, 2, 8 * t:8 * t + 8], v[:, :, 0:DH], AX.X, ALU.add)
                V.tensor_reduce(stat[:, 2, 16 + 8 * t:24 + 8 * t], v[:, :, DH:DH + ROPE], AX.X, ALU.add) \
                    .then_inc(squares_used, 1)
            take_squares()
            V.tensor_reduce(stat[:, 2, 32:48], square.rearrange("p (h d) -> p h d", d=DH), AX.X, ALU.add) \
                .then_inc(squares_used, 1)
            dve.wait_ge(squares_used, sqs[0])
            means([(0, 16, DH), (16, 16, ROPE), (32, 16, DH)]).then_inc(ms_ready, 1)
            refine(48)
            for t in range(TT):
                v = qup[:, t, :].rearrange("p (h d) -> p h d", d=DH + ROPE)
                k = kvup[:, t, :].rearrange("p (h d) -> p h d", d=P)[:, :, 0:DH]

                def rs(c, n):
                    return stat[:, 1, c + 8 * t:c + 8 * t + 8].unsqueeze(2).to_broadcast([P, H, n])

                V.tensor_tensor(qn_nat[:, t, :].rearrange("p (h d) -> p h d", d=DH), v[:, :, 0:DH], rs(0, DH), ALU.mult)
                V.tensor_tensor(v[:, :, DH:DH + ROPE], v[:, :, DH:DH + ROPE], rs(16, ROPE), ALU.mult)
                step(V.tensor_tensor(pturn[:, t, :].rearrange("p (h d) -> p h d", d=DH), k, rs(32, DH), ALU.mult))
                g = grope[:, 0, l, :].unsqueeze(1).to_broadcast([P, H, ROPE])
                V.tensor_tensor(v[:, :, DH:DH + ROPE], v[:, :, DH:DH + ROPE], g, ALU.mult)
                kr = nat[:, t, 1920:1952]
                step(V.tensor_tensor(kr, kr, grope[:, 1, l, :], ALU.mult))
            if l == 0:
                dve.wait_ge(setup_a, 2)
            for t in range(TT):
                v = qup[:, t, :].rearrange("p (h d) -> p h d", d=DH + ROPE)
                kr = nat[:, t, 1920:1952]
                for heads, x1, x2, dst in (
                    (H, v[:, :, DH:DH + half], v[:, :, DH + half:DH + ROPE],
                     nat[:, t, 1536:1792].rearrange("p (h d) -> p h d", d=ROPE)),
                    (4, kr[:, 0:half].unsqueeze(1).to_broadcast([P, 4, half]),
                     kr[:, half:ROPE].unsqueeze(1).to_broadcast([P, 4, half]),
                     nat[:, t, 1792:1920].rearrange("p (h d) -> p h d", d=ROPE)),
                ):
                    cos, sin = (trig[:, i, t, :].unsqueeze(1).to_broadcast([P, heads, half]) for i in range(2))
                    ra, rb, rc, rd = (rtmp[:, i // 2, 128 * (i % 2):128 * (i % 2) + heads * half]
                                      .rearrange("p (h d) -> p h d", d=half) for i in range(4))
                    V.tensor_tensor(ra, x1, cos, ALU.mult)
                    V.tensor_tensor(rb, x2, sin, ALU.mult)
                    V.tensor_tensor(rc, x2, cos, ALU.mult)
                    step(V.tensor_tensor(rd, x1, sin, ALU.mult))
                    V.tensor_tensor(dst[:, :, 0:half], ra, rb, ALU.subtract)
                    step(V.tensor_tensor(dst[:, :, half:ROPE], rc, rd, ALU.add))
            V.sem_inc(mla_norm, 1)
            rest_to(w + 1 + AHEAD)
            dve.wait_ge(mla_turned, 6 * l + 5)
            V.tensor_copy(qrT, psum[0][:, :].rearrange("p (a s) -> p a s", s=S)).then_inc(mla_out_v, 1)
            dve.wait_ge(mla_turned, 6 * l + 6)
            V.tensor_copy(krT, psum[1][:, 0:S]).then_inc(mla_out_v, 1)

            g0 = 16 * l
            dilated_max(g0, 0)
            for h in range(H):
                if h + 1 < H:
                    dilated_max(g0 + h + 1, h + 1)
                turn_store(g0 + h, 2 * S)
                if l == 0:
                    sum_mod(1, h // 4, h % 4)
            if l == 0:
                store_mod(1, 1)
            store_group(l, 0)
            scale = float(DH + ROPE) ** -0.5
            plain_max(g0 + H, scale)
            for h in range(H, 2 * H):
                if h + 1 < 2 * H:
                    plain_max(g0 + h + 1, scale)
                turn_store(g0 + h, 2 * S)
                sum_mod(l, 4 + (h - H) // 4, h % 4)
            store_mod(l, 5)
            store_group(l, 1)
            turn_o(l)
            w += 2
            for j in range(N_OUT):
                rest_to(w + j + AHEAD)
                if j % 2:
                    dve.wait_ge(used, w + j + 1)
                    dve.wait_ge(gt_ready, 2 * l + 2)
                    for t in range(TT):
                        add_to_x(4 + 2 * (j // 2) + t, t, j // 2, 0).then_inc(x_mixed, 1)
            w += N_OUT
            dve.wait_ge(x_mixed, 4 * l + 4)
            norm(2 * l + 1, lambda k: modc[:, 3, k:k + 1], lambda k: modc[:, 2, k:k + 1])

            def squares_of(b, slot, it=None):
                dve.wait_ge(f_one[l], loop(b + 1, it, 3))
                if b >= 3:
                    dve.wait_ge(f_hi[l], loop(b - 2, it, 3))
                V.tensor_tensor(relu[:, 1, slot, :], relu[:, 0, slot, :], relu[:, 0, slot, :], ALU.mult) \
                    .then_inc(f_two[l], 1)

            def low_block(b, slot, it=None):
                dve.wait_ge(f_hi[l], loop(b + 1, it, 3))
                V.tensor_tensor(actlo[:, slot, :], relu[:, 1, slot, :], acthi[:, slot, :].bitcast(F32), ALU.subtract) \
                    .then_inc(f_lo[l], 1)

            rest_to(w + 2)
            squares_of(0, 0)
            low_block(0, 0)
            for j in range(3):
                rest_to(w + 3 + 2 * j)
                squares_of(j + 1, (j + 1) % 3)
                rest_to(w + 4 + 2 * j)
                low_block(j + 1, (j + 1) % 3)
            with dve.Fori(0, 4) as it:
                for j in range(3, 6):
                    rest(w + 3 + 2 * j, it)
                    squares_of(j + 1, (j + 1) % 3, it)
                    rest(w + 4 + 2 * j, it)
                    low_block(j + 1, (j + 1) % 3, it)
            low[0] = w + N_MLP + 1
            rest_to(w + N_MLP - 1 + AHEAD)
            dve.wait_ge(used, w + N_MLP)
            for i in range(4):
                ins = add_to_x(4 + i, i // 2, i % 2, 1)
                if i % 2:
                    ins.then_inc((x_first, x_done)[i // 2], 1)
            dve.wait_ge(x_done, l + 1)

        for l in range(2):
            w = (W_B2, W_L3)[l]
            n = 4 + 2 * l
            norm(n, lambda k: vec[:, V_G3 + KD * l + k:V_G3 + KD * l + k + 1], None)
            for j in range(N_NAT2):
                rest_to(w + j + AHEAD)
                if j == 3 and l == 0:
                    dve.wait_ge(ws_high, 1)
                    V.tensor_tensor(wsmall_lo[:, :, :], wsmall[:, :, :], wsmall_hi[:, :, :].bitcast(F32), ALU.subtract) \
                        .then_inc(ws_low, 1)
            w += N_NAT2
            dve.wait_ge(s_logit, l + 1)
            V.tensor_scalar(srows[:, :], psum[3][0:H, 0:S], small[:, l:l + 1], None, ALU.add).then_inc(s_rows, 1)
            for j in range(N_QK2):
                rest_to(w + j + AHEAD)
                if j < TT:
                    head_sums(j)
                if j == 1:
                    dve.wait_ge(f_logit, l + 1)
                    z = psum[3][:, S:S + TT * H]
                    step(V.tensor_scalar(forget[:, 0, :], z, -1.0, None, ALU.mult))
                    V.tensor_tensor(forget[:, 1, :], z, forget[:, 0, :], ALU.max).then_inc(f_abs, 1)
                if j == 2:
                    heads_norm()

            def store_gate(j):
                dve.wait_ge(used, w + N_QK2 + j + 1)
                for i in range(2):
                    f = 2 * j + i
                    c = V_BG + 16 * l + f
                    ins = V.tensor_scalar(gates[:, S * f:S * f + S], psum[6 + j % 2][:, S * i:S * i + S],
                                          vec[:, c:c + 1], None, ALU.add)
                ins.then_inc(gate_out, 1)

            def gate_step(h):
                if h % 2 == 0:
                    rest_to(w + N_QK2 + h // 2 + AHEAD)
                    if h:
                        store_gate(h // 2 - 1)

            dve.wait_ge(f_tail, l + 1)
            V.scalar_tensor_tensor(forget[:, 2, :], forget[:, 0, :], 0.0, forget[:, 1, :], ALU.max, ALU.add) \
                .then_inc(f_cost, 1)
            dve.wait_ge(small_in, 80)
            g0 = 32 + 16 * l

            def softplus(h):
                g = g0 + h
                pv = probs[:, g % 2, 0:384]
                dve.wait_ge(sb_tail, H * l + h + 1)
                step(V.scalar_tensor_tensor(pv, psum[g % 2][:, 0:384], 0.0, pv, ALU.max, ALU.add))
                V.tensor_tensor(pv, pv, con2[:, C_SBM:C_SBM + 384], ALU.mult).then_inc(sb_soft, 1)

            softplus(0)
            for h in range(H):
                if h + 1 < H:
                    softplus(h + 1)
                g = g0 + h
                dve.wait_ge(sb_sum, H * l + h + 1)
                V.scalar_tensor_tensor(probs[:, g % 2, 0:384], psum[g % 2][:, 0:384], 0.0, con2[:, C_SBN:C_SBN + 384],
                                       ALU.min, ALU.add).then_inc(sb_log, 1)
                gate_step(h)
            store_group(2 + l, 0, divide=False)
            g0 += H
            adds = [(P, con2[:, C_CAUS + P:C_CAUS + S]), (S, con2[:, C_CAUS:C_CAUS + S])]
            added_max(g0, adds)
            for h in range(H):
                if h + 1 < H:
                    added_max(g0 + h + 1, adds)
                turn_store(g0 + h, 384)
                gate_step(H + h)
            store_gate(7)
            store_group(2 + l, 1)
            turn_o(2 + l)
            w += N_TURN2
            for j in range(N_WO):
                rest_to(w + j + AHEAD)
            for q in range(8):
                dve.wait_ge(used, w + q // 2 + 1)
                dve.wait_ge(gate_open, 8 * l + q + 1)
                v = gates[:, 512 * q:512 * q + 512]
                V.tensor_tensor(v, v, psum[q][:, :], ALU.mult).then_inc(vstep, 1)
                steps[0] += 1
            dve.wait_ge(vstep, steps[0])
            for q in range(4):
                v = gates[:, 512 * q:512 * q + 512]
                V.tensor_tensor(v, v, gates[:, 2048 + 512 * q:2560 + 512 * q], ALU.add).then_inc(gated, 1)
            for q in range(4):
                dve.wait_ge(z_high, 4 * l + q + 1)
                V.tensor_tensor(hlo[:, 2 * q:2 * q + 2, :],
                                gates[:, 512 * q:512 * q + 512].rearrange("p (a s) -> p a s", s=S),
                                hhi[:, 2 * q:2 * q + 2, :].bitcast(F32), ALU.subtract).then_inc(z_low, 1)
            w += N_WO
            for j in range(N_OUT):
                rest_to(min(w + j + AHEAD, W_MOE))
                if j % 2:
                    dve.wait_ge(used, w + j + 1)
                    for t in range(TT):
                        add_to_x(4 + 2 * (j // 2) + t, t, j // 2, None).then_inc(x_mixed, 1)
            w += N_OUT
            dve.wait_ge(x_mixed, 4 * (2 + l) + 4)
            norm(n + 1, lambda k: vec[:, V_G4 + KD * l + k:V_G4 + KD * l + k + 1], None)

            def product(f, w, b, n, it=None, per=0, wper=0, e=None):
                dve.wait_ge(f_one[f], loop(b + 1, it, per))
                dve.wait_ge(used, loop(w, it, wper))
                if b >= 2:
                    dve.wait_ge(f_hi[f], loop(b - 1, it, per))
                dst = silu[:, 1, b % 2, 0:n]
                ins = V.tensor_tensor(dst, silu[:, 0, b % 2, 0:n], psum[2 + b % 2][:, 0:n], ALU.mult)
                if e is not None:
                    ins.then_inc(e_comb, 1)
                    dve.wait_ge(e_comb, loop(b + 1, it, per))
                    v = dst.rearrange("p (f s) -> p f s", s=S)
                    ins = V.tensor_tensor(v, v, combine[:, bass.ds(e, 1), :].to_broadcast([P, n // S, S]), ALU.mult)
                ins.then_inc(f_two[f], 1)

            def low_block2(f, b, n, it=None, per=0):
                dve.wait_ge(f_hi[f], loop(b + 1, it, per))
                V.tensor_tensor(actlo[:, b % 2, 0:n], silu[:, 1, b % 2, 0:n], acthi[:, b % 2, 0:n].bitcast(F32),
                                ALU.subtract).then_inc(f_lo[f], 1)

            if l == 0:
                rest_to(w + 2)
                rest_to(w + 3)
                product(2, w + 2, 0, 512)
                low_block2(2, 0, 512)
                for j in range(2):
                    m = w + 2 + 3 * j
                    rest_to(m + 3)
                    product(2, m + 2, j + 1, 512)
                    rest_to(m + 4)
                    low_block2(2, j + 1, 512)
                with dve.Fori(0, 4) as it:
                    for j in range(2, 4):
                        m = w + 2 + 3 * j
                        rest(m + 2, it)
                        rest(m + 3, it)
                        product(2, m + 2, j + 1, 512, it, 2, RAW)
                        rest(m + 4, it)
                        low_block2(2, j + 1, 512, it, 2)
                low[0] = w + N_DENSE + 1
                rest_to(w + N_DENSE - 1 + AHEAD)
                dve.wait_ge(used, w + N_DENSE)
                for i in range(4):
                    ins = add_to_x(4 + i, i // 2, i % 2, None)
                    if i % 2:
                        ins.then_inc((x_first, x_done)[i // 2], 1)
                dve.wait_ge(x_done, 3)
            else:
                dve.wait_ge(s_logit, 3)
                V.tensor_copy(srows[:, :], psum[4][0:H, 0:S]).then_inc(s_rows, 1)
                dve.wait_ge(gain_in, 16)
                for t in range(TT):
                    ins = V.tensor_tensor(nat[:, t, 0:D], nat[:, t, 0:D], gain_rows, ALU.mult)
                ins.then_inc(hn_ready, 1)
                dve.wait_ge(r_logit, 1)
                lg = route[:, 0:16]
                step(V.tensor_copy(lg, psum[4][:, S:S + 16]))
                mx = route[:, 32:34]
                step(V.tensor_reduce(mx, lg.rearrange("p (t e) -> p t e", e=NE), AX.X, ALU.max))
                V.tensor_scalar(mx, mx, -1.0, None, ALU.mult).then_inc(r_max, 1)
                for t in range(TT):
                    v = lg[:, 8 * t:8 * t + 8]
                    other = v.unsqueeze(1).to_broadcast([P, NE, NE])
                    own = v.unsqueeze(2).to_broadcast([P, NE, NE])
                    big, same = (route[:, c:c + 64].rearrange("p (e j) -> p e j", j=NE) for c in (64, 128))
                    V.tensor_tensor(big, other, own, ALU.is_gt)
                    step(V.tensor_tensor(same, other, own, ALU.is_equal))
                    step(V.tensor_tensor(same, same, con2[:, C_TIE:C_TIE + 64].rearrange("p (e j) -> p e j", j=NE), ALU.mult))
                    step(V.tensor_tensor(big, big, same, ALU.add))
                    step(V.tensor_reduce(route[:, 40 + 8 * t:48 + 8 * t], big, AX.X, ALU.add))
                chosen = route[:, 40:56]
                step(V.tensor_scalar(chosen, chosen, 2.0, None, ALU.is_lt))
                dve.wait_ge(r_exp, 1)
                ex = route[:, 16:32]
                step(V.tensor_tensor(ex, ex, chosen, ALU.mult))
                step(V.tensor_reduce(route[:, 34:36], ex.rearrange("p (t e) -> p t e", e=NE), AX.X, ALU.add))
                step(V.reciprocal(route[:, 34:36], route[:, 34:36]))
                for t in range(TT):
                    ins = V.tensor_scalar(ex[:, 8 * t:8 * t + 8], ex[:, 8 * t:8 * t + 8], route[:, 34 + t:35 + t], None, ALU.mult)
                ins.then_inc(r_comb, 1)
                dve.wait_ge(r_place, 1)
                slot = route[:, 200:216]
                step(V.tensor_tensor(slot, psum[5][:, 0:16], chosen, ALU.mult))
                V.tensor_scalar(slot, slot, -1.0, None, ALU.add)
                step(V.tensor_reduce(route[:, 216:217], psum[5][:, 16:24], AX.X, ALU.max))
                V.tensor_copy(most[0:1, 0:1], route[0:1, 216:217]).then_inc(r_most, 1)
                dve.wait_ge(r_most, 1)
                tokens = dve.value_load(most[0:1, 0:1], min_val=0, max_val=S)

                def expert(it, last):
                    def rest_ahead(m):
                        if not last or m < w + EXPERT:
                            rest(m, it, EXPERT)

                    rest_ahead(w + 2)
                    rest_ahead(w + 3)
                    product(3, w + 2, 0, 512, it, 6, EXPERT, it)
                    low_block2(3, 0, 512, it, 6)
                    for b in range(1, 6):
                        m = w + 3 * b - 1
                        n = 512 if b < 5 else 256
                        rest_ahead(m + 2)
                        rest_ahead(m + 3)
                        product(3, m + 2, b, n, it, 6, EXPERT, it)
                        rest_ahead(m + 4)
                        low_block2(3, b, n, it, 6)
                    rest_ahead(w + EXPERT + 1)
                    dve.wait_ge(used, loop(w + EXPERT, it, EXPERT))
                    for i in range(4):
                        ins = add_to_x(4 + i, i // 2, i % 2, None)
                    ins.then_inc(x_done, 1)
                    dve.wait_ge(x_done, loop(4, it, 1))

                def add_scattered(count, it):
                    dve.wait_ge(scattered, loop(count, it, 2))
                    for t in range(TT):
                        for half in range(2):
                            ins = add_to_x(6 - 2 * t + half, t, half, None)
                    return ins

                def few_tokens(it, i, last):
                    v0 = w + EXPERT * i

                    def at(value, per):
                        return loop(value + i * per, it, 2 * per)

                    def rest_ahead(m):
                        if not last or m < w + 2 * EXPERT:
                            rest(m, it, 2 * EXPERT)

                    if i == 0:
                        for b in range(4):
                            dve.wait_ge(g_high, loop(b + 1, it, 4))
                            V.tensor_tensor(hlo[:, 2 * b:2 * b + 2, :], psum[6 + b % 2][:, :].rearrange("p (a s) -> p a s", s=S),
                                            hhi[:, 2 * b:2 * b + 2, :].bitcast(F32), ALU.subtract).then_inc(g_low, 1)
                        rest_ahead(v0 + 1)

                    def product_slots(b, n):
                        dve.wait_ge(f_one[3], at(b + 1, 6))
                        dve.wait_ge(used, loop(v0 + 3 * b + 1 if b else v0 + 2, it, 2 * EXPERT))
                        if b >= 2:
                            dve.wait_ge(s_turned, at(b - 1, 6))
                        c = 256 if b < 5 else 128
                        V.tensor_tensor(sprod[:, b % 2, 0:n], sgate[:, b % 2, 0:n], psum[b % 2][:, c:c + n], ALU.mult) \
                            .then_inc(f_two[3], 1)

                    def low_slots(b, n):
                        dve.wait_ge(f_hi[3], at(b + 1, 6))
                        V.tensor_tensor(actlo[:, b % 2, 0:n], psum[2 + b % 2][:, 0:n], acthi[:, b % 2, 0:n].bitcast(F32),
                                        ALU.subtract).then_inc(f_lo[3], 1)

                    rest_ahead(v0 + 2)
                    rest_ahead(v0 + 3)
                    product_slots(0, 256)
                    add_scattered(i + 1, it).then_inc(x_added, 1)
                    for b in range(1, 6):
                        m = v0 + 3 * b - 1
                        n = 256 if b < 5 else 128
                        rest_ahead(m + 2)
                        low_slots(b - 1, 256)
                        if b < 5:
                            rest_ahead(m + 3)
                            product_slots(b, n)
                        else:
                            product_slots(b, n)
                            rest_ahead(m + 3)
                            low_slots(b, n)
                        rest_ahead(m + 4)
                    if i == 0:
                        rest_ahead(v0 + EXPERT + 1)
                    for half in range(2):
                        dve.wait_ge(y_high, at(half + 1, 2))
                        V.scalar_tensor_tensor(ylo[:, 512 * half:512 * half + 512], psum[4 + half][:, :], wcur[:, i:i + 1],
                                               yhi[:, 512 * half:512 * half + 512].bitcast(F32), ALU.mult, ALU.subtract) \
                            .then_inc(y_low, 1)

                with dve.If(tokens < P + 1):
                    for e in range(NE):
                        for t in range(TT):
                            ins = V.tensor_scalar(pick[:, t, e, :], con2[:, C_SLOT:C_SLOT + P],
                                                  slot[:, 8 * t + e:8 * t + e + 1], None, ALU.is_equal)
                        ins.then_inc(p_ready, 1)
                    zero = con2[:, C_SLOT:C_SLOT + P].unsqueeze(1).to_broadcast([P, KD, P])
                    V.tensor_scalar(yhi[:, :].rearrange("p (k n) -> p k n", n=P), zero, 0.0, None, ALU.mult).then_inc(y_low, 1)
                    V.tensor_scalar(ylo[:, :].rearrange("p (k n) -> p k n", n=P), zero, 0.0, None, ALU.mult).then_inc(y_low, 1)
                    for t in range(TT):
                        dve.wait_ge(hn_high, t + 1)
                        V.tensor_tensor(hn_lo[:, t, :], nat[:, t, 0:D], hn_hi[:, t, :].bitcast(F32), ALU.subtract) \
                            .then_inc(hn_low, 1)
                    dve.wait_ge(p_turned, 5)
                    V.tensor_copy(route[:, 224:232], psum[4][:, 0:NE]).then_inc(p_stored, 1)
                    with dve.Fori(0, NE // 2 - 1) as it:
                        for i in range(2):
                            few_tokens(it, i, False)
                    for i in range(2):
                        few_tokens(NE // 2 - 1, i, True)
                    add_scattered(NE + 1, None).then_inc(x_done, NE)
                with dve.Else():
                    dve.wait_ge(r_out, 1)
                    rest(w + 1)
                    with dve.Fori(0, NE - 1) as it:
                        expert(it, False)
                    expert(NE - 1, True)

    @block.tensor
    def _(pe):
        T = nc.tensor

        def piece(w, it=None, per=RAW):
            pe.wait_ge(raw_used, loop(raw_of(w) + 1, it, per))
            return whi[w % SPLIT], wlo[w % SPLIT]

        def passes(out, pairs, start, stop):
            for i, (lhsT, rhs) in enumerate(pairs):
                ins = T.matmul(out, lhsT, rhs, start=start and i == 0, stop=stop and i == len(pairs) - 1)
            return ins

        def natural(w, k0, n, out, first, last, hi=hhi, lo=hlo, kt=4, kbase=0):
            wh, wl = piece(w)
            for t in range(TT):
                for k in range(kt):
                    c = slice(k * n, k * n + n)
                    hs, ls = hi[:, k0 + k, P * t:P * t + P], lo[:, k0 + k, P * t:P * t + P]
                    ins = passes(out[t][:, 0:n], [(hs, wh[:, c]), (hs, wl[:, c]), (ls, wh[:, c])],
                                 first and k == 0, last and k == kt - 1)
            ins.then_inc(used, 1)

        def turned_product(w, n, kt, tiles, k0=0, it=None, per=RAW):
            wh, wl = piece(w, it, per)
            for f, (bank, c0) in enumerate(tiles):
                for k in range(kt):
                    c = slice(k * n + P * f, k * n + P * f + P)
                    ins = passes(bank[:, c0:c0 + S], [(wh[:, c], hhi[:, k0 + k, :]), (wh[:, c], hlo[:, k0 + k, :]),
                                                      (wl[:, c], hhi[:, k0 + k, :])], k == 0, k == kt - 1)
            ins.then_inc(used, 1)

        def down_product(w, slot, kt, first, last, it=None, per=RAW):
            wh, wl = piece(w, it, per)
            for t in range(TT):
                for k in range(kt):
                    c = slice(S * k + P * t, S * k + P * t + P)
                    hs, ls = acthi[:, slot, c], actlo[:, slot, c]
                    for half in range(2):
                        d = slice(D * k + 512 * half, D * k + 512 * half + 512)
                        ins = passes(psum[4 + 2 * t + half][:, :], [(hs, wh[:, d]), (hs, wl[:, d]), (ls, wh[:, d])],
                                     first and k == 0, last and k == kt - 1)
            ins.then_inc(used, 1)

        def turn(out, src):
            return T.transpose(out, src, ident)

        def turn_h(n):
            pe.wait_ge(xn_ready, n + 1)
            for b in range(4):
                for i in range(2):
                    for t in range(TT):
                        k = 2 * b + i
                        ins = turn(psum[b][:, S * i + P * t:S * i + P * t + P], nat[:, t, P * k:P * k + P])
                ins.then_inc(h_turned, 1)
            pe.wait_ge(h_low, 4 * n + 4)

        def turn_qk(l):
            pe.wait_ge(qk_norm, l + 1)
            for b in range(4):
                for i in range(2):
                    for t in range(TT):
                        c = 512 * (b // 2) + P * (2 * (b % 2) + i)
                        ins = turn(psum[b][:, S * i + P * t:S * i + P * t + P], nat[:, t, c:c + P])
                ins.then_inc(qk_turned, 1)

        def bank_free(g):
            if g >= 2:
                pe.wait_ge(probs_ready, g - 1)

        def rows(t, h):
            return t[DH * (h % 2):DH * (h % 2) + DH, h // 2, :]

        def score_dilated(g, h):
            bank_free(g)
            q, k = rows(qdT, h), rows(kdT, h)
            for t in range(TT):
                ins = T.matmul(psum[g % 2][:, S * t:S * t + S], q[:, P * t:P * t + P], k, start=True, stop=True)
            ins.then_inc(scores, 1)

        def score_mla(g, h):
            bank_free(g)
            q, k = rows(qnT, h), rows(knT, h)
            r = slice(ROPE * (h % 4), ROPE * (h % 4) + ROPE)
            for t in range(TT):
                o = psum[g % 2][:, S * t:S * t + S]
                T.matmul(o, q[:, P * t:P * t + P], k, start=True, stop=False)
                ins = T.matmul(o, qrT[r, h // 4, P * t:P * t + P], krT[r, :], start=False, stop=True)
            ins.then_inc(scores, 1)

        def score_forget(g, h):
            bank_free(g)
            q, k = rows(fqT, h), rows(fkT, h)
            cost = [forget[:, 2, 8 * t + h:8 * t + h + 1].to_broadcast([P, P]) for t in range(TT)]
            tri = con2[:, C_TRI:C_TRI + S]
            b = psum[g % 2]
            T.matmul(b[:, 0:P], q[:, 0:P], k[:, 0:P], start=True, stop=False)
            T.matmul(b[:, 0:P], cost[0], tri[:, 0:P], start=False, stop=True)
            T.matmul(b[:, S:2 * S], q[:, P:S], k, start=True, stop=False)
            T.matmul(b[:, S:2 * S], cost[0], tri, start=False, stop=True)
            ins = T.matmul(b[:, S + P:2 * S], cost[1], tri[:, 0:P], start=False, stop=True, skip_group_check=True)
            ins.then_inc(scores, 1)

        def score_stick(g, h):
            bank_free(g)
            q, k = rows(sqT, h), rows(skT, h)
            T.matmul(psum[g % 2][:, 0:S], k[:, 0:P], q, start=True, stop=True)
            T.matmul(psum[g % 2][:, S:384], k[:, P:S], q[:, P:S], start=False, stop=True,
                     skip_group_check=True).then_inc(scores, 1)

        def sum_stick(g, i):
            pe.wait_ge(sb_soft, i + 1)
            b, pv, ntri = psum[g % 2], probs[:, g % 2, :], con2[:, C_NTRI:C_NTRI + P]
            T.matmul(b[:, 0:S], ntri, pv[:, 0:S], start=False, stop=True, skip_group_check=True)
            T.matmul(b[:, P:S], minus[:, :], pv[:, S:384], start=False, stop=True, skip_group_check=True)
            T.matmul(b[:, S:384], ntri, pv[:, S:384], start=False, stop=True, skip_group_check=True).then_inc(sb_sum, 1)

        FULL = ((0, 0, 0), (1, 0, P), (0, 1, S), (1, 1, S + P))
        CAUSAL = ((0, 0, 0), (1, 0, P), (1, 1, S))

        def turn_probs(g, blocks):
            pe.wait_ge(probs_ready, g + 1)
            if softmax_of(g) >= 2:
                pe.wait_ge(pt_ready, softmax_of(g) - 1)
            for qt, kt, c in blocks:
                ins = turn(psum[2 + g % 2][:, c:c + P], probs[:, g % 2, S * qt + P * kt:S * qt + P * kt + P])
            ins.then_inc(turned, 1)

        def weigh(g, blocks, v, plain=False):
            if plain:
                pe.wait_ge(probs_ready, g + 1)
            else:
                pe.wait_ge(pt_ready, softmax_of(g) + 1)
            if g % H == 0 and g:
                pe.wait_ge(attn_out, g // H)
            h = g % H
            for qt in range(TT):
                own = [b for b in blocks if b[0] == qt]
                for i, (_, kt, c) in enumerate(own):
                    ins = T.matmul(psum[4 + qt][:, DH * h:DH * h + DH], pturn[:, g % 2, c:c + P], v(kt, h),
                                   start=i == 0, stop=i == len(own) - 1)
            ins.then_inc(values, 1)

        def reduce_mod(l, s, q):
            if q % 2 == 0:
                return
            n = mod_count(l, s, q) // 2
            if q == 1 and n >= 4:
                pe.wait_ge(mod_stored, n // 2 - 1)
            pe.wait_ge(mod_summed, n + 1)
            for f in range(4):
                c = 4 * (q // 2) + f
                ins = T.matmul(mod_bank(s)[:, c:c + 1], mod_sums[:, n % 2, P * f:P * f + P], ones[:, 0:1],
                               start=True, stop=True)
            ins.then_inc(mod_reduced, 1)

        def spread_gate(l, i):
            for k in range(KD):
                ins = T.matmul(psum[6 - 2 * i + k // 4][:, P * (k % 4):P * (k % 4) + P],
                               modc[:, 4 + i, k:k + 1].to_broadcast([P, P]), ident, start=True, stop=True)
            ins.then_inc(gt_spread, 1)

        def heads(g0, score, blocks, v, mod=None, between=None):
            score(g0, 0)
            for h in range(H):
                if h + 1 < H:
                    score(g0 + h + 1, h + 1)
                if between is not None:
                    between(H + h)
                turn_probs(g0 + h, blocks)
                if h:
                    weigh(g0 + h - 1, blocks, v)
                    if mod is not None:
                        reduce_mod(mod[0], mod[1] + (h - 1) // 4, (h - 1) % 4)
            weigh(g0 + H - 1, blocks, v)
            if mod is not None:
                reduce_mod(mod[0], mod[1] + 1, 3)

        def turn_o(l):
            pe.wait_ge(attn_out, 2 * l + 2)
            if l < 2:
                spread_gate(l, 1)
            for b in range(4):
                for i in range(2):
                    for t in range(TT):
                        k = 2 * b + i
                        ins = turn(psum[b][:, S * i + P * t:S * i + P * t + P], nat[:, t, P * k:P * k + P])
                ins.then_inc(o_turned, 1)
            pe.wait_ge(o_low, 4 * l + 4)

        def out_product(w):
            for j in range(N_OUT):
                natural(w + j, 4 * (j % 2), 512, [psum[4 + 2 * (j // 2) + t] for t in range(TT)], j % 2 == 0, j % 2 == 1)

        pe.wait_ge(ones_set, 2)
        for q in range(4):
            reduce_mod(0, 0, q)
        reduce_mod(0, 1, 1)
        pe.wait_ge(loaded, 16 * N_LOADS)
        T.transpose(psum[0][:, 0:P], stage, ident)
        T.transpose(psum[0][:, P:N_VEC], mod_rows, ident[0:96, 0:96]).then_inc(setup_t, 1)
        pe.wait_ge(setup_v, 2)
        for t in range(TT):
            T.matmul(psum[1][:, t:t + 1], pos_row[:, P * t:P * t + P], ones[0:1, 0:1], start=True, stop=True)
        T.matmul(psum[1][:, P:2 * P], ones[0:1, :], gain_row, start=True, stop=True)
        T.matmul(psum[2][:, 0:S], ones[0:1, :], pos_row, start=True, stop=True).then_inc(setup_t, 1)
        reduce_mod(0, 1, 3)
        pe.wait_ge(setup_v, SETUP_V)

        for l in range(2):
            w = l * L1
            turn_h(2 * l)
            for c in range(4):
                if c >= 2:
                    pe.wait_ge(proj_out, 4 * l + c - 1)
                n = 512 if c < 3 else W_IN - 1536
                for half in range(2):
                    natural(w + 2 * c + half, 4 * half, n, [psum[4 + 2 * (c % 2) + t] for t in range(TT)],
                            half == 0, half == 1)
                    j = 2 * c + half - 1
                    if j >= 0:
                        reduce_mod(l, 2 + j // 4, j % 4)
            reduce_mod(l, 3, 3)
            pe.wait_ge(mod_stored, mod_count(l, 3) // 4 + 1)
            w += N_IN1
            pe.wait_ge(lat_norm, l + 1)
            for t in range(TT):
                for i in range(2):
                    turn(psum[4][:, S * i + P * t:S * i + P * t + P], nat[:, t, 1536 + P * i:1664 + P * i])
                ins = turn(psum[5][:, P * t:P * t + P], nat[:, t, 1792:1920])
            ins.then_inc(lat_turned, 1)
            pe.wait_ge(lat_low, l + 1)
            lh, ll = (v.rearrange("p (k s) -> p k s", s=S) for v in (lathi, latlo))
            wh, wl = piece(w)
            for t in range(TT):
                for c0, n, bank in ((0, 512, 6 - 2 * t), (512, 256, 7 - 2 * t)):
                    for k in range(2):
                        c = slice(QUP * k + c0, QUP * k + c0 + n)
                        hs, ls = lh[:, k, P * t:P * t + P], ll[:, k, P * t:P * t + P]
                        ins = passes(psum[bank][:, 0:n], [(hs, wh[:, c]), (hs, wl[:, c]), (ls, wh[:, c])], k == 0, k == 1)
            ins.then_inc(used, 1)
            wh, wl = piece(w + 1)
            for t in range(TT):
                for i in range(2):
                    c = slice(512 * i, 512 * i + 512)
                    hs, ls = lh[:, 2, P * t:P * t + P], ll[:, 2, P * t:P * t + P]
                    ins = passes(psum[2 * t + i][:, :], [(hs, wh[:, c]), (hs, wl[:, c]), (ls, wh[:, c])], True, True)
            ins.then_inc(used, 1)
            w += 2
            pe.wait_ge(kvup_out, l + 1)
            turn_qk(l)
            pe.wait_ge(qk_out, 4 * l + 4)
            pe.wait_ge(mla_norm, l + 1)
            for b in range(4):
                for i in range(2):
                    pair = 2 * (b % 2) + i
                    for t in range(TT):
                        v = (qn_nat, pturn)[b // 2]
                        ins = turn(psum[4 + b][:, S * i + P * t:S * i + P * t + P], v[:, t, P * pair:P * pair + P])
                ins.then_inc(mla_turned, 1)
            for i in range(2):
                for t in range(TT):
                    ins = turn(psum[0][:, S * i + P * t:S * i + P * t + P], nat[:, t, 1536 + P * i:1664 + P * i])
            ins.then_inc(mla_turned, 1)
            for t in range(TT):
                ins = turn(psum[1][:, P * t:P * t + P], nat[:, t, 1792:1920])
            ins.then_inc(mla_turned, 1)
            pe.wait_ge(mla_out_v, 2 * l + 2)
            pe.wait_ge(mla_out_a, 4 * l + 4)
            heads(16 * l, score_dilated, FULL, lambda kt, h: nat[:, kt, 1024 + DH * h:1024 + DH * h + DH],
                  (1, 0) if l == 0 else None)
            heads(16 * l + H, score_mla, FULL, lambda kt, h: kvup[:, kt, P * h + DH:P * h + P], (l, 4))
            pe.wait_ge(mod_stored, mod_count(l, 5) // 4 + 1)
            spread_gate(l, 0)
            turn_o(l)
            pe.wait_ge(gt_ready, 2 * l + 2)
            out_product(w)
            w += N_OUT
            turn_h(2 * l + 1)

            def up_block(b, slot, it=None):
                m = w + 2 * b - 1 if b else w
                if b >= 3:
                    pe.wait_ge(f_one[l], loop(b - 2, it, 3))
                turned_product(m, S, KD, [(psum[slot], 0), (psum[slot], S)], it=it)

            def down_block(b, slot, first, last, it=None):
                pe.wait_ge(f_lo[l], loop(b + 1, it, 3))
                down_product(w + 2 + 2 * b if b < F1 // 256 - 1 else w + N_MLP - 1, slot, 2, first, last, it)

            up_block(0, 0)
            for j in range(3):
                up_block(j + 1, (j + 1) % 3)
                down_block(j, j % 3, j == 0, False)
            with pe.Fori(0, 4) as it:
                for j in range(3, 6):
                    up_block(j + 1, (j + 1) % 3, it)
                    down_block(j, j % 3, False, False, it)
            down_block(F1 // 256 - 1, 0, False, True)

        for l in range(2):
            w = (W_B2, W_L3)[l]
            n = 4 + 2 * l
            turn_h(n)
            for c in range(4):
                if c >= 2:
                    pe.wait_ge(proj_out, 8 + 4 * l + c - 1)
                for half in range(2):
                    natural(w + 2 * c + half, 4 * half, 512, [psum[4 + 2 * (c % 2) + t] for t in range(TT)],
                            half == 0, half == 1)
            w += N_NAT2

            def small_product(slot, bank):
                pe.wait_ge(ws_low, 1)
                for k in range(KD):
                    hs, ls = wsmall_hi[:, slot, 8 * k:8 * k + 8], wsmall_lo[:, slot, 8 * k:8 * k + 8]
                    ins = passes(bank[0:H, 0:S], [(hs, hhi[:, k, :]), (hs, hlo[:, k, :]), (ls, hhi[:, k, :])],
                                 k == 0, k == KD - 1)
                ins.then_inc(s_logit, 1)

            def turn_small(i, bank):
                pe.wait_ge(s_rows, i + 1)
                for t in range(TT):
                    ins = T.transpose(bank[:, S + H * t:S + H * t + H], srows[:, P * t:P * t + P], ident[0:H, 0:H])
                return ins

            small_product(l, psum[3])
            for j in range(N_QK2):
                if j == 3:
                    pe.wait_ge(f_abs, l + 1)
                turned_product(w + j, S, KD, [(psum[j], 0), (psum[j], S)])
                if j == 0:
                    turn_small(l, psum[3]).then_inc(f_logit, 1)
            pe.wait_ge(t2_out, N_QK2 * (l + 1))

            def gate_half(h):
                j, f = h // 2, h % 2
                if f == 0 and j >= 2:
                    pe.wait_ge(gate_out, 8 * l + j - 1)
                wh, wl = piece(w + N_QK2 + j)
                for k in range(KD):
                    c = slice(k * S + P * f, k * S + P * f + P)
                    ins = passes(psum[6 + j % 2][:, S * f:S * f + S], [(wh[:, c], hhi[:, k, :]), (wh[:, c], hlo[:, k, :]),
                                                                      (wl[:, c], hhi[:, k, :])], k == 0, k == KD - 1)
                if f:
                    ins.then_inc(used, 1)

            turn_qk(2 + l)
            pe.wait_ge(qk_out, 4 * (2 + l) + 4)
            g0 = 32 + 16 * l

            def v_stick(kt, h):
                return nat[:, kt, 1536 + DH * h:1536 + DH * h + DH]

            score_stick(g0, 0)
            for h in range(H):
                if h + 1 < H:
                    score_stick(g0 + h + 1, h + 1)
                gate_half(h)
                sum_stick(g0 + h, H * l + h)
                if h:
                    weigh(g0 + h - 1, CAUSAL, v_stick, plain=True)
            weigh(g0 + H - 1, CAUSAL, v_stick, plain=True)
            pe.wait_ge(f_cost, l + 1)
            heads(g0 + H, score_forget, CAUSAL, lambda kt, h: nat[:, kt, 1024 + DH * h:1024 + DH * h + DH],
                  between=gate_half)
            turn_o(2 + l)
            w += N_TURN2
            for j in range(N_WO):
                turned_product(w + j, 512, 4, [(psum[2 * j + i // 2], S * (i % 2)) for i in range(4)], k0=4 * (j // 2))
            w += N_WO
            pe.wait_ge(z_low, 4 * l + 4)
            out_product(w)
            w += N_OUT
            turn_h(n + 1)

            def gate_block(f, w, b, n, it=None, per=0, wper=0):
                if b >= 2:
                    pe.wait_ge(f_one[f], loop(b - 1, it, per))
                turned_product(w, n // 2 if n == 512 else P, KD, [(psum[b % 2], S * i) for i in range(n // S)], it=it, per=wper)

            def up_block2(f, w, b, n, it=None, per=0, wper=0):
                if b >= 2:
                    pe.wait_ge(f_two[f], loop(b - 1, it, per))
                turned_product(w, n // 2 if n == 512 else P, KD, [(psum[2 + b % 2], S * i) for i in range(n // S)], it=it, per=wper)

            def down_block2(f, w, b, kt, first, last, it=None, per=0, wper=0):
                pe.wait_ge(f_lo[f], loop(b + 1, it, per))
                down_product(w, b % 2, kt, first, last, it, wper)

            if l == 0:
                gate_block(2, w, 0, 512)
                up_block2(2, w + 1, 0, 512)
                for j in range(2):
                    m = w + 2 + 3 * j
                    gate_block(2, m, j + 1, 512)
                    up_block2(2, m + 1, j + 1, 512)
                    down_block2(2, m + 2, j, 2, j == 0, False)
                with pe.Fori(0, 4) as it:
                    for j in range(2, 4):
                        m = w + 2 + 3 * j
                        gate_block(2, m, j + 1, 512, it, 2, RAW)
                        up_block2(2, m + 1, j + 1, 512, it, 2, RAW)
                        down_block2(2, m + 2, j, 2, False, False, it, 2, RAW)
                down_block2(2, w + N_DENSE - 1, F2 // 256 - 1, 2, False, True)
            else:
                small_product(2, psum[4])
                turn_small(2, psum[4]).then_inc(r_logit, 1)
                pe.wait_ge(r_comb, 1)
                tri, chosen = con2[:, C_TRI:C_TRI + P], route[:, 40:56]
                T.matmul(psum[5][:, 0:8], tri, chosen[:, 0:8], start=True, stop=True)
                T.matmul(psum[5][:, 8:16], ones[:, :], chosen[:, 0:8], start=True, stop=False)
                T.matmul(psum[5][:, 8:16], tri, chosen[:, 8:16], start=False, stop=True)
                T.matmul(psum[5][:, 16:24], ones[:, :], chosen[:, 0:8], start=True, stop=False)
                T.matmul(psum[5][:, 16:24], ones[:, :], chosen[:, 8:16], start=False, stop=True).then_inc(r_place, 1)

                def scatter(i, count, it=None, per=0):
                    pe.wait_ge(y_low, loop(2 * count, it, 2 * per))
                    pe.wait_ge(now_ready, loop(2 * count, it, 2 * per))
                    for t in range(TT):
                        for half in range(2):
                            sel, c = pick_now[:, i, P * t:P * t + P], slice(512 * half, 512 * half + 512)
                            bank = psum[6 - 2 * t + half]
                            T.matmul(bank[:, :], sel, yhi[:, c], start=True, stop=False)
                            ins = T.matmul(bank[:, :], sel, ylo[:, c], start=False, stop=True)
                    ins.then_inc(scattered, 1)

                def few_tokens(it, i):
                    v0 = w + EXPERT * i
                    mine = slice(P * i, P * i + P)

                    def at(value, per):
                        return loop(value + i * per, it, 2 * per)

                    def slots_product(m, b, n, c):
                        wh, wl = piece(m, it, 2 * EXPERT)
                        for k in range(KD):
                            hs, ls, kn = hhi[:, k, mine], hlo[:, k, mine], slice(k * n, k * n + n)
                            ins = passes(psum[b % 2][:, c:c + n], [(hs, wh[:, kn]), (hs, wl[:, kn]), (ls, wh[:, kn])],
                                         k == 0, k == KD - 1)
                        ins.then_inc(used, 1)

                    def both_products(m, b):
                        piece(m + 1, it, 2 * EXPERT)
                        s0 = m % SPLIT
                        for k in range(KD):
                            hs, ls = hhi[:, k, mine], hlo[:, k, mine]
                            wh, wl = (v[:, s0:s0 + 2, P * k:P * k + P] for v in (whi_all, wlo_all))
                            ins = passes(psum[b % 2][:, 0:S].rearrange("p (a n) -> p a n", a=2),
                                         [(hs, wh), (hs, wl), (ls, wh)], k == 0, k == KD - 1)
                        ins.then_inc(used, 2)

                    def turn_slots(b, tiles=2):
                        pe.wait_ge(f_two[3], at(b + 1, 6))
                        for j in range(tiles):
                            ins = turn(psum[2 + b % 2][:, P * j:P * j + P], sprod[:, b % 2, P * j:P * j + P])
                        ins.then_inc(s_turned, 1)

                    def down_slots(m, b, kt):
                        pe.wait_ge(f_lo[3], at(b + 1, 6))
                        if b == 0:
                            pe.wait_ge(x_added, at(1, 1))
                        wh, wl = piece(m, it, 2 * EXPERT)
                        for k in range(kt):
                            hs, ls = acthi[:, b % 2, P * k:P * k + P], actlo[:, b % 2, P * k:P * k + P]
                            for half in range(2):
                                d = slice(D * k + 512 * half, D * k + 512 * half + 512)
                                ins = passes(psum[4 + half][:, :], [(hs, wh[:, d]), (hs, wl[:, d]), (ls, wh[:, d])],
                                             b == 0 and k == 0, b == 5 and k == kt - 1)
                        ins.then_inc(used, 1)

                    if i == 0:
                        for b in range(4):
                            if b >= 2:
                                pe.wait_ge(g_low, loop(b - 1, it, 4))
                            for j in range(2):
                                k = 2 * b + j
                                ins = passes(psum[6 + b % 2][:, S * j:S * j + S],
                                             [(part[:, t, P * k:P * k + P],
                                               pick_pair[:, t, bass.ds(it, 1), :].rearrange("p g n -> p (g n)"))
                                              for t in range(TT) for part in (hn_hi, hn_lo)], True, True)
                            ins.then_inc(gathered, 1)
                        pe.wait_ge(g_low, loop(4, it, 4))
                    slots_product(v0, 0, 256, 0)
                    slots_product(v0 + 1, 0, 256, 256)
                    scatter(1 - i, i + 1, it, 2)
                    for b in range(1, 5):
                        m = v0 + 3 * b - 1
                        slots_product(m, b, 256, 0)
                        turn_slots(b - 1)
                        slots_product(m + 1, b, 256, 256)
                        down_slots(m + 2, b - 1, 2)
                    turn_slots(4)
                    both_products(v0 + 14, 5)
                    down_slots(v0 + 16, 4, 2)
                    turn_slots(5, 1)
                    down_slots(v0 + 17, 5, 1)

                pe.wait_ge(r_most, 1)
                tokens = pe.value_load(most[0:1, 0:1], min_val=0, max_val=S)
                with pe.If(tokens < P + 1):
                    for e in range(NE):
                        pe.wait_ge(p_ready, e + 1)
                        for t in range(TT):
                            ins = turn(psum[e // 2][:, S * (e % 2) + P * t:S * (e % 2) + P * t + P],
                                       pick[:, t, e, :].bitcast(F32))
                        if e % 2:
                            ins.then_inc(p_turned, 1)
                    for e in range(NE):
                        for t in range(TT):
                            ins = T.matmul(psum[4][:, e:e + 1], pick[:, t, e, :].bitcast(F32),
                                           route[:, 16 + 8 * t + e:17 + 8 * t + e], start=t == 0, stop=t == 1)
                    ins.then_inc(p_turned, 1)
                    pe.wait_ge(hn_low, 2)
                    pe.wait_ge(p_stored, 5)
                    with pe.Fori(0, NE // 2) as it:
                        for i in range(2):
                            few_tokens(it, i)
                    scatter(1, NE + 1)
                with pe.Else():
                    for e in range(NE):
                        for t in range(TT):
                            c = 16 + 8 * t + e
                            ins = T.matmul(psum[e // 2][:, S * (e % 2) + P * t:S * (e % 2) + P * t + P],
                                           route[:, c:c + 1].to_broadcast([P, P]), ident, start=True, stop=True)
                    ins.then_inc(r_spread, 1)
                    pe.wait_ge(r_out, 1)
                    with pe.Fori(0, NE) as it:
                        gate_block(3, w, 0, 512, it, 6, EXPERT)
                        up_block2(3, w + 1, 0, 512, it, 6, EXPERT)
                        pe.wait_ge(x_done, loop(3, it, 1))
                        for b in range(1, 6):
                            m = w + 3 * b - 1
                            n = 512 if b < 5 else 256
                            gate_block(3, m, b, n, it, 6, EXPERT)
                            up_block2(3, m + 1, b, n, it, 6, EXPERT)
                            down_block2(3, m + 2, b - 1, 2, b == 1, False, it, 6, EXPERT)
                        down_block2(3, w + EXPERT - 1, 5, 1, False, True, it, 6, EXPERT)


_INS = ["x", "c", "positions", "w_mod", "b_mod", "g_norm_mix", "w_in", "g_q_dil", "g_k_dil", "g_cq", "w_q_up",
        "g_ckv", "w_kv_up", "g_q_nope", "g_q_rope", "g_k_nope", "g_k_rope", "w_out", "g_norm_mlp", "w_mlp_in",
        "w_mlp_out", "g_mix_2", "w_in_2", "b_f_2", "b_gate_2", "g_q_2", "g_k_2", "w_o_sb_2", "w_o_fox_2",
        "w_out_2", "g_ffn_2", "w_gu_dense_2", "w_dn_dense_2", "w_router_2", "w_gu_exp_2", "w_dn_exp_2"]


def kernel(**inputs):
    import numpy as _np
    import concourse.bacc as _bacc
    from concourse import mybir as _mybir
    from concourse.bass_utils import run_bass_kernel_spmd as _run

    nc = _bacc.Bacc("TRN2", target_bir_lowering=False, num_devices=1)
    arrays, args = {}, {}
    for name in _INS:
        v = _np.ascontiguousarray(inputs[name])
        arrays[f"in_{name}_dram"] = v
        args[name] = nc.dram_tensor(f"in_{name}_dram", v.shape, _mybir.dt.from_np(v.dtype), kind="ExternalInput").ap()
    consts = []
    for i, v in enumerate(constants()):
        arrays[f"in_constants{i}_dram"] = v
        consts.append(nc.dram_tensor(f"in_constants{i}_dram", v.shape, F32, kind="ExternalInput").ap())
    out = nc.dram_tensor("out_0_dram", (1, S, D), F32, kind="ExternalOutput").ap()
    two_blocks_kernel(nc, args, consts, out)
    r = _run(nc, [arrays], core_ids=[0])
    return r.results[0]["out_0_dram"]
```
